# Optimizing a Trainium2 kernel written in Bass

```python
import jax, jax.numpy as jnp
from jax import lax
import numpy as np
import math

D_MODEL = 1024
BATCH = 1
SEQ = 256
DEPTH = 1

HEAD_DIM = 64
N_Q_HEADS = 8
N_KV_HEADS = 2
WINDOW = 128
ATT_BLOCK = 128
N_BUCKETS = 32
MAX_DISTANCE = 128
REC_HEADS = 4
REC_KEY_DIM = 128
REC_VAL_DIM = 128
REC_CHUNK = 64
D_FF = 2816
PLE_DIM = 256
EPS = 1e-6

ATT_Q_W = N_Q_HEADS * HEAD_DIM
ATT_KV_W = N_KV_HEADS * HEAD_DIM
REC_K_W = REC_HEADS * REC_KEY_DIM
REC_V_W = REC_HEADS * REC_VAL_DIM
IN_W = ATT_Q_W + 2 * ATT_KV_W + 2 * REC_K_W + 2 * REC_V_W + 2 * D_MODEL


def _split_points():
    widths = [ATT_Q_W, ATT_KV_W, ATT_KV_W, REC_K_W, REC_K_W, REC_V_W, REC_V_W, D_MODEL]
    return [int(v) for v in np.cumsum(widths)]

def rms_norm(x, g):
    xf = x.astype(jnp.float32)
    y = xf * lax.rsqrt(jnp.mean(xf * xf, axis=-1, keepdims=True) + EPS)
    return (y * g.astype(jnp.float32)).astype(x.dtype)

def swiglu(x, w_in, w_out):
    gate, up = jnp.split(x @ w_in, 2, axis=-1)
    return (jax.nn.silu(gate) * up) @ w_out

def t5_band_buckets():
    qi = np.arange(ATT_BLOCK)[:, None] + ATT_BLOCK
    kj = np.arange(2 * ATT_BLOCK)[None, :]
    dist = qi - kj
    n = np.maximum(dist, 0)
    max_exact = N_BUCKETS // 2
    large = max_exact + (np.log(np.maximum(n, 1) / max_exact)
                         / np.log(MAX_DISTANCE / max_exact)
                         * (N_BUCKETS - max_exact)).astype(np.int32)
    large = np.minimum(large, N_BUCKETS - 1)
    bucket = np.where(n < max_exact, n, large).astype(np.int32)
    return bucket, dist.astype(np.int32)

def sliding_window_attention(q, k, v, rel_table, sinks):
    B, S = q.shape[0], q.shape[1]
    nb = S // ATT_BLOCK
    G = N_Q_HEADS // N_KV_HEADS
    qb = q.reshape(B, nb, ATT_BLOCK, N_KV_HEADS, G, HEAD_DIM)

    def band(t):
        t = t.reshape(B, nb, ATT_BLOCK, N_KV_HEADS, HEAD_DIM)
        prev = jnp.pad(t, ((0, 0), (1, 0), (0, 0), (0, 0), (0, 0)))[:, :-1]
        return jnp.concatenate([prev, t], axis=2)

    kb, vb = band(k), band(v)
    s = jnp.einsum('bnqhgd,bnkhd->bnhgqk', qb, kb).astype(jnp.float32) * (HEAD_DIM ** -0.5)
    bucket, dist = t5_band_buckets()
    bias = rel_table.astype(jnp.float32)[bucket]
    bias = bias.transpose(2, 0, 1).reshape(N_KV_HEADS, G, ATT_BLOCK, 2 * ATT_BLOCK)
    key_pos = (jnp.arange(nb)[:, None, None] * ATT_BLOCK - ATT_BLOCK
               + jnp.arange(2 * ATT_BLOCK)[None, None, :])
    dist_j = jnp.asarray(dist)[None]
    valid = (dist_j >= 0) & (dist_j < WINDOW) & (key_pos >= 0)
    s = jnp.where(valid[None, :, None, None], s + bias, -jnp.inf)
    sink = sinks.astype(jnp.float32).reshape(N_KV_HEADS, G, 1, 1)
    m = jnp.maximum(jnp.max(s, axis=-1, keepdims=True), sink)
    e = jnp.exp(s - m)
    probs = e / (jnp.sum(e, axis=-1, keepdims=True) + jnp.exp(sink - m))
    o = jnp.einsum('bnhgqk,bnkhd->bnqhgd', probs.astype(v.dtype), vb)
    return o.reshape(B, S, ATT_Q_W)

def hgrn2_recurrence(q, f_logit, i, lb):
    B, S = q.shape[0], q.shape[1]
    nc = S // REC_CHUNK
    lbf = lb.astype(jnp.float32).reshape(REC_HEADS, REC_KEY_DIM)
    f = lbf + (1.0 - lbf) * jax.nn.sigmoid(f_logit.astype(jnp.float32))
    log_f = jnp.log(f)
    k = 1.0 - f

    def to_chunks(t):
        return t.reshape(B, nc, REC_CHUNK, REC_HEADS, t.shape[-1]).transpose(1, 0, 3, 2, 4)

    qc = to_chunks(q.astype(jnp.float32))
    kc = to_chunks(k)
    vc = to_chunks(i.astype(jnp.float32))
    gc = to_chunks(log_f)
    causal = jnp.tril(jnp.ones((REC_CHUNK, REC_CHUNK), dtype=bool))[:, :, None]

    def step(state, inp):
        qt, kt, vt, gt = inp
        b = jnp.cumsum(gt, axis=2)
        diff = b[:, :, :, None, :] - b[:, :, None, :, :]
        decay = jnp.exp(jnp.where(causal, diff, -jnp.inf))
        attn = jnp.einsum('bhtd,bhsd,bhtsd->bhts', qt, kt, decay)
        o = (jnp.einsum('bhts,bhsv->bhtv', attn, vt)
             + jnp.einsum('bhtd,bhdv->bhtv', qt * jnp.exp(b), state))
        b_last = b[:, :, -1:, :]
        new_state = (jnp.exp(b_last[:, :, 0, :])[..., None] * state
                     + jnp.einsum('bhsd,bhsv->bhdv', kt * jnp.exp(b_last - b), vt))
        return new_state, o

    s0 = jnp.zeros((B, REC_HEADS, REC_KEY_DIM, REC_VAL_DIM), jnp.float32)
    _, o = lax.scan(step, s0, (qc, kc, vc, gc))
    return o.transpose(1, 0, 3, 2, 4).reshape(B, S, REC_HEADS, REC_VAL_DIM).astype(q.dtype)

def first_inputs(seed: int = 0) -> dict:
    key = jax.random.key(seed)
    ks = jax.random.split(key, 24)
    f32 = jnp.float32

    def nrm(k, shape, scale):
        return jax.random.normal(k, shape, f32) * scale

    def gain(k, shape):
        return 1.0 + 0.05 * jax.random.normal(k, shape, f32)

    return {
        "x": nrm(ks[0], (BATCH, SEQ, D_MODEL), 1.0),
        "p": nrm(ks[1], (DEPTH, BATCH, SEQ, PLE_DIM), 1.0),
        "rel_bias": nrm(ks[2], (N_BUCKETS, N_Q_HEADS), 0.5),
        "lb_param": nrm(ks[3], (DEPTH + 1, REC_K_W), 1.0),
        "norm_ffn1": gain(ks[4], (DEPTH, D_MODEL)),
        "w_ffn1_in": nrm(ks[5], (DEPTH, D_MODEL, 2 * D_FF), D_MODEL ** -0.5),
        "w_ffn1_out": nrm(ks[6], (DEPTH, D_FF, D_MODEL), D_FF ** -0.5),
        "norm_mix": gain(ks[7], (DEPTH, D_MODEL)),
        "w_in": nrm(ks[8], (DEPTH, D_MODEL, IN_W), D_MODEL ** -0.5),
        "attn_sinks": nrm(ks[9], (DEPTH, N_Q_HEADS), 1.0),
        "rec_norm": gain(ks[10], (DEPTH, REC_VAL_DIM)),
        "w_att_proj": nrm(ks[11], (DEPTH, ATT_Q_W, D_MODEL), ATT_Q_W ** -0.5),
        "w_rec_proj": nrm(ks[12], (DEPTH, REC_V_W, D_MODEL), REC_V_W ** -0.5),
        "w_out": nrm(ks[13], (DEPTH, D_MODEL, D_MODEL), D_MODEL ** -0.5),
        "norm_ffn2": gain(ks[14], (DEPTH, D_MODEL)),
        "w_ffn2_in": nrm(ks[15], (DEPTH, D_MODEL, 2 * D_FF), D_MODEL ** -0.5),
        "w_ffn2_out": nrm(ks[16], (DEPTH, D_FF, D_MODEL), D_FF ** -0.5),
        "norm_ple": gain(ks[17], (DEPTH, D_MODEL)),
        "w_ple_gate": nrm(ks[18], (DEPTH, D_MODEL, D_MODEL), D_MODEL ** -0.5),
        "w_ple_proj": nrm(ks[19], (DEPTH, PLE_DIM, D_MODEL), PLE_DIM ** -0.5),
        "norm_final": gain(ks[20], (D_MODEL,)),
    }

def first_block(x, p, rel_bias, lb_param, norm_ffn1, w_ffn1_in, w_ffn1_out, norm_mix, w_in,
              attn_sinks, rec_norm, w_att_proj, w_rec_proj, w_out, norm_ffn2, w_ffn2_in,
              w_ffn2_out, norm_ple, w_ple_gate, w_ple_proj, norm_final):
    B, S = x.shape[0], x.shape[1]
    lower_bounds = jnp.cumsum(jax.nn.softmax(lb_param.astype(jnp.float32), axis=0), axis=0)
    splits = _split_points()
    h = x
    for layer in range(DEPTH):
        h = h + 0.5 * swiglu(rms_norm(h, norm_ffn1[layer]), w_ffn1_in[layer], w_ffn1_out[layer])

        u = rms_norm(h, norm_mix[layer])
        proj = u @ w_in[layer]
        aq, ak, av, rq, rf, ri, rg, ga, gb = jnp.split(proj, splits, axis=-1)

        att = sliding_window_attention(
            aq.reshape(B, S, N_Q_HEADS, HEAD_DIM),
            ak.reshape(B, S, N_KV_HEADS, HEAD_DIM),
            av.reshape(B, S, N_KV_HEADS, HEAD_DIM),
            rel_bias, attn_sinks[layer])

        rec = hgrn2_recurrence(
            rq.reshape(B, S, REC_HEADS, REC_KEY_DIM),
            rf.reshape(B, S, REC_HEADS, REC_KEY_DIM),
            ri.reshape(B, S, REC_HEADS, REC_VAL_DIM),
            lower_bounds[layer])
        rec = rms_norm(rec, rec_norm[layer]).reshape(B, S, REC_V_W) * jax.nn.sigmoid(rg)

        y_a = att @ w_att_proj[layer]
        y_b = rec @ w_rec_proj[layer]
        merged = jax.nn.sigmoid(ga) * y_a + jax.nn.sigmoid(gb) * y_b
        h = h + merged @ w_out[layer]

        h = h + 0.5 * swiglu(rms_norm(h, norm_ffn2[layer]), w_ffn2_in[layer], w_ffn2_out[layer])

        gate = jax.nn.sigmoid(rms_norm(h, norm_ple[layer]) @ w_ple_gate[layer])
        h = h + gate * (p[layer] @ w_ple_proj[layer])
    return rms_norm(h, norm_final)


DEPTH_2 = 2

SB_HEADS = 8
SB_HEAD_DIM = 64
SB_WIDTH = SB_HEADS * SB_HEAD_DIM
RW_HEADS = 8
RW_HEAD_DIM = 64
RW_WIDTH = RW_HEADS * RW_HEAD_DIM
RW_DECAY_LORA = 64
RW_AAA_LORA = 64
RW_GATE_LORA = 160
RW_GN_EPS = 64e-5
RW_IN = 3 * RW_WIDTH + RW_DECAY_LORA + RW_AAA_LORA + RW_GATE_LORA
HYB_IN = 3 * SB_WIDTH + RW_IN
HYB_OUT = SB_WIDTH + RW_WIDTH
MLA_HEADS = 16
MLA_NOPE = 64
MLA_ROPE = 32
MLA_V = 64
MLA_Q_RANK = 384
MLA_KV_RANK = 256
MLA_DOWN = MLA_Q_RANK + MLA_KV_RANK + MLA_ROPE
ROPE_THETA = 10000.0
FFN_DIM = 2816
CONV_WIDTH = 3
Q_BLOCK = 128
NORM_EPS = 1e-6
N_EVEN = (DEPTH_2 + 1) // 2
N_ODD = DEPTH_2 // 2


F32 = jnp.float32

def rmsnorm(x, g):
    xf = x.astype(F32)
    y = xf * lax.rsqrt(jnp.mean(xf * xf, axis=-1, keepdims=True) + NORM_EPS)
    return (y * g.astype(F32)).astype(x.dtype)

def shift_right(x, n):
    return jnp.pad(x, ((0, 0), (n, 0), (0, 0)))[:, : x.shape[1]]

def sweep_query_blocks(fn, q):
    b, s, h, e = q.shape
    nb = s // Q_BLOCK
    qb = q.reshape(b, nb, Q_BLOCK, h, e).transpose(1, 0, 2, 3, 4)
    starts = jnp.arange(nb, dtype=jnp.int32) * Q_BLOCK
    out = lax.map(lambda args: fn(args[0], args[1]), (qb, starts))
    return out.transpose(1, 0, 2, 3, 4).reshape(b, s, h, out.shape[-1])

def stick_breaking_attention(q, k, v):
    s_len = k.shape[1]
    scale = 1.0 / math.sqrt(q.shape[-1])
    key_pos = jnp.arange(s_len, dtype=jnp.int32)
    kf = k.astype(F32)
    vf = v.astype(F32)

    def block(qb, t0):
        z = jnp.einsum('bqhe,bshe->bhqs', qb.astype(F32), kf) * scale
        qpos = t0 + jnp.arange(Q_BLOCK, dtype=jnp.int32)
        mask = key_pos[None, :] < qpos[:, None]
        log_one_minus = jnp.where(mask, -jax.nn.softplus(z), 0.0)
        rev = lax.cumsum(log_one_minus, axis=3, reverse=True)
        after = jnp.concatenate([rev[..., 1:], jnp.zeros_like(rev[..., :1])], axis=3)
        w = jnp.where(mask, jnp.exp(jax.nn.log_sigmoid(z) + after), 0.0)
        return jnp.einsum('bhqs,bshe->bqhe', w, vf)

    return sweep_query_blocks(block, q).astype(v.dtype)

def causal_softmax_attention(q, k, v, scale):
    s_len = k.shape[1]
    key_pos = jnp.arange(s_len, dtype=jnp.int32)
    kf = k.astype(F32)
    vf = v.astype(F32)

    def block(qb, t0):
        sc = jnp.einsum('bqhe,bshe->bhqs', qb.astype(F32), kf) * scale
        qpos = t0 + jnp.arange(Q_BLOCK, dtype=jnp.int32)
        mask = key_pos[None, :] <= qpos[:, None]
        w = jax.nn.softmax(jnp.where(mask, sc, -jnp.inf), axis=-1)
        return jnp.einsum('bhqs,bshe->bqhe', w, vf)

    return sweep_query_blocks(block, q).astype(v.dtype)

def apply_rope(x, positions):
    half = x.shape[-1] // 2
    inv_freq = ROPE_THETA ** (-jnp.arange(half, dtype=F32) / half)
    ang = positions.astype(F32)[:, :, None, None] * inv_freq
    cos, sin = jnp.cos(ang), jnp.sin(ang)
    xf = x.astype(F32)
    x1, x2 = xf[..., :half], xf[..., half:]
    return jnp.concatenate([x1 * cos - x2 * sin, x1 * sin + x2 * cos], axis=-1).astype(x.dtype)

def rwkv7_time_mix(proj, mu, w0, w2, a0, a2, g2, k_k, k_a, r_k, ln_w, ln_b):
    b, s, _ = proj.shape
    pf = proj.astype(F32)
    xm = pf + (shift_right(pf, 1) - pf) * mu
    r, k, v, wl, al, gl = jnp.split(
        xm, [RW_WIDTH, 2 * RW_WIDTH, 3 * RW_WIDTH, 3 * RW_WIDTH + RW_DECAY_LORA,
             3 * RW_WIDTH + RW_DECAY_LORA + RW_AAA_LORA], axis=-1)
    w = -jax.nn.softplus(-(w0 + jnp.tanh(wl) @ w2)) - 0.5
    decay = jnp.exp(-jnp.exp(w))
    a = jax.nn.sigmoid(a0 + al @ a2)
    g = jax.nn.sigmoid(gl) @ g2

    hd = lambda t: t.reshape(b, s, RW_HEADS, RW_HEAD_DIM)
    ph = lambda t: t.astype(F32).reshape(RW_HEADS, RW_HEAD_DIM)
    r, k, v, decay, a = hd(r), hd(k), hd(v), hd(decay), hd(a)
    kk = k * ph(k_k)
    kk = kk * lax.rsqrt(jnp.maximum(jnp.sum(kk * kk, axis=-1, keepdims=True), 1e-24))
    k = k * (1.0 + (a - 1.0) * ph(k_a))

    def step(state, inp):
        r_t, w_t, k_t, v_t, kk_t, a_t = inp
        sa = jnp.einsum('bhij,bhj->bhi', state, -kk_t)
        state = (state * w_t[:, :, None, :] + sa[..., None] * (kk_t * a_t)[:, :, None, :]
                 + v_t[..., None] * k_t[:, :, None, :])
        return state, jnp.einsum('bhij,bhj->bhi', state, r_t)

    tm = lambda t: jnp.moveaxis(t, 1, 0)
    state0 = jnp.zeros((b, RW_HEADS, RW_HEAD_DIM, RW_HEAD_DIM), F32)
    _, y = lax.scan(step, state0, (tm(r), tm(decay), tm(k), tm(v), tm(kk), tm(a)))
    y = jnp.moveaxis(y, 0, 1)

    mean = jnp.mean(y, axis=-1, keepdims=True)
    var = jnp.mean(jnp.square(y - mean), axis=-1, keepdims=True)
    y = (y - mean) * lax.rsqrt(var + RW_GN_EPS)
    y = y * ph(ln_w) + ph(ln_b)
    y = y + jnp.sum(r * k * r_k.astype(F32), axis=-1, keepdims=True) * v
    return (y.reshape(b, s, RW_WIDTH) * g).astype(proj.dtype)

def sb_rwkv_mixer(hn, w_in, w_out, mu, w0, w2, a0, a2, g2, k_k, k_a, r_k, ln_w, ln_b):
    b, s, _ = hn.shape
    proj = hn @ w_in
    qa, ka, va, rw = jnp.split(proj, [SB_WIDTH, 2 * SB_WIDTH, 3 * SB_WIDTH], axis=-1)
    hd = lambda t: t.reshape(b, s, SB_HEADS, SB_HEAD_DIM)
    o_a = stick_breaking_attention(hd(qa), hd(ka), hd(va)).reshape(b, s, SB_WIDTH)
    o_b = rwkv7_time_mix(rw, mu, w0, w2, a0, a2, g2, k_k, k_a, r_k, ln_w, ln_b)
    return jnp.concatenate([o_a, o_b.astype(o_a.dtype)], axis=-1) @ w_out

def mla_mixer(hn, positions, w_down, q_norm, kv_norm, w_uq, w_ukv, w_o):
    b, s, _ = hn.shape
    c = hn @ w_down
    cq, ckv, kr = jnp.split(c, [MLA_Q_RANK, MLA_Q_RANK + MLA_KV_RANK], axis=-1)
    q = (rmsnorm(cq, q_norm) @ w_uq).reshape(b, s, MLA_HEADS, MLA_NOPE + MLA_ROPE)
    kv = (rmsnorm(ckv, kv_norm) @ w_ukv).reshape(b, s, MLA_HEADS, MLA_NOPE + MLA_V)
    q_nope, q_rope = jnp.split(q, [MLA_NOPE], axis=-1)
    k_nope, v = jnp.split(kv, [MLA_NOPE], axis=-1)
    q = jnp.concatenate([q_nope, apply_rope(q_rope, positions)], axis=-1)
    k_rope = jnp.broadcast_to(apply_rope(kr[:, :, None, :], positions), (b, s, MLA_HEADS, MLA_ROPE))
    k = jnp.concatenate([k_nope, k_rope], axis=-1)
    o = causal_softmax_attention(q, k, v, 1.0 / math.sqrt(MLA_NOPE + MLA_ROPE))
    return o.reshape(b, s, MLA_HEADS * MLA_V) @ w_o

def conv_glu(hn, w_in, conv_w, conv_b, w_out):
    u, gate_in = jnp.split(hn @ w_in, 2, axis=-1)
    c = (conv_w[0] * shift_right(gate_in, 2) + conv_w[1] * shift_right(gate_in, 1)
         + conv_w[2] * gate_in + conv_b)
    return (jax.nn.gelu(c, approximate=False) * u) @ w_out

def second_inputs(seed: int = 0) -> dict:
    key = jax.random.key(seed)
    keys = jax.random.split(key, 48)
    counter = [0]

    def nk():
        kk = keys[counter[0]]
        counter[0] += 1
        return kk

    def nrm(shape, scale):
        return jax.random.normal(nk(), shape, F32) * scale

    def gain(shape):
        return 1.0 + nrm(shape, 0.05)

    x = nrm((BATCH, SEQ, D_MODEL), 1.0)
    p = nrm((DEPTH_2, BATCH, SEQ, PLE_DIM), 1.0)
    offset = jax.random.randint(nk(), (BATCH, 1), 0, 4096, dtype=jnp.int32)
    positions = offset + jnp.arange(SEQ, dtype=jnp.int32)[None, :]
    return {
        "x": x,
        "p": p,
        "positions": positions,
        "attn_norm": gain((DEPTH_2, D_MODEL)),
        "ffn_norm": gain((DEPTH_2, D_MODEL)),
        "ffn_w_in": nrm((DEPTH_2, D_MODEL, 2 * FFN_DIM), D_MODEL ** -0.5),
        "ffn_conv_w": nrm((DEPTH_2, CONV_WIDTH, FFN_DIM), CONV_WIDTH ** -0.5),
        "ffn_conv_b": nrm((DEPTH_2, FFN_DIM), 0.01),
        "ffn_w_out": nrm((DEPTH_2, FFN_DIM, D_MODEL), FFN_DIM ** -0.5),
        "ple_w_proj": nrm((DEPTH_2, PLE_DIM, D_MODEL), PLE_DIM ** -0.5),
        "ple_norm": gain((DEPTH_2, D_MODEL)),
        "ple_gate_norm": gain((DEPTH_2, D_MODEL)),
        "ple_w_gate": nrm((DEPTH_2, D_MODEL, D_MODEL), D_MODEL ** -0.5),
        "hyb_w_in": nrm((N_EVEN, D_MODEL, HYB_IN), D_MODEL ** -0.5),
        "hyb_w_out": nrm((N_EVEN, HYB_OUT, D_MODEL), HYB_OUT ** -0.5),
        "rw_mu": jax.random.uniform(nk(), (N_EVEN, RW_IN), F32),
        "rw_w0": jax.random.uniform(nk(), (N_EVEN, RW_WIDTH), F32, -6.0, 1.0),
        "rw_w2": nrm((N_EVEN, RW_DECAY_LORA, RW_WIDTH), RW_DECAY_LORA ** -0.5),
        "rw_a0": nrm((N_EVEN, RW_WIDTH), 0.1),
        "rw_a2": nrm((N_EVEN, RW_AAA_LORA, RW_WIDTH), RW_AAA_LORA ** -0.5),
        "rw_g2": nrm((N_EVEN, RW_GATE_LORA, RW_WIDTH), RW_GATE_LORA ** -0.5),
        "rw_k_k": 0.85 + nrm((N_EVEN, RW_WIDTH), 0.05),
        "rw_k_a": gain((N_EVEN, RW_WIDTH)),
        "rw_r_k": nrm((N_EVEN, RW_HEADS, RW_HEAD_DIM), 0.1),
        "rw_ln_w": gain((N_EVEN, RW_WIDTH)),
        "rw_ln_b": nrm((N_EVEN, RW_WIDTH), 0.01),
        "mla_w_down": nrm((N_ODD, D_MODEL, MLA_DOWN), D_MODEL ** -0.5),
        "mla_q_norm": gain((N_ODD, MLA_Q_RANK)),
        "mla_kv_norm": gain((N_ODD, MLA_KV_RANK)),
        "mla_w_uq": nrm((N_ODD, MLA_Q_RANK, MLA_HEADS * (MLA_NOPE + MLA_ROPE)), MLA_Q_RANK ** -0.5),
        "mla_w_ukv": nrm((N_ODD, MLA_KV_RANK, MLA_HEADS * (MLA_NOPE + MLA_V)), MLA_KV_RANK ** -0.5),
        "mla_w_o": nrm((N_ODD, MLA_HEADS * MLA_V, D_MODEL), (MLA_HEADS * MLA_V) ** -0.5),
        "final_norm": gain((D_MODEL,)),
    }

def second_block(x, p, positions, attn_norm, ffn_norm, ffn_w_in, ffn_conv_w, ffn_conv_b, ffn_w_out,
              ple_w_proj, ple_norm, ple_gate_norm, ple_w_gate,
              hyb_w_in, hyb_w_out, rw_mu, rw_w0, rw_w2, rw_a0, rw_a2, rw_g2, rw_k_k, rw_k_a,
              rw_r_k, rw_ln_w, rw_ln_b,
              mla_w_down, mla_q_norm, mla_kv_norm, mla_w_uq, mla_w_ukv, mla_w_o, final_norm):
    h = x
    for i in range(DEPTH_2):
        j = i // 2
        hn = rmsnorm(h, attn_norm[i])
        if i % 2 == 0:
            mix = sb_rwkv_mixer(hn, hyb_w_in[j], hyb_w_out[j], rw_mu[j], rw_w0[j], rw_w2[j],
                                rw_a0[j], rw_a2[j], rw_g2[j], rw_k_k[j], rw_k_a[j], rw_r_k[j],
                                rw_ln_w[j], rw_ln_b[j])
        else:
            mix = mla_mixer(hn, positions, mla_w_down[j], mla_q_norm[j], mla_kv_norm[j],
                            mla_w_uq[j], mla_w_ukv[j], mla_w_o[j])
        h = h + mix
        h = h + conv_glu(rmsnorm(h, ffn_norm[i]), ffn_w_in[i], ffn_conv_w[i], ffn_conv_b[i], ffn_w_out[i])
        e = rmsnorm(p[i] @ ple_w_proj[i], ple_norm[i])
        gate = jax.nn.sigmoid(rmsnorm(h, ple_gate_norm[i]) @ ple_w_gate[i])
        h = h + gate * e
    return rmsnorm(h, final_norm)


def setup_inputs(seed=0):
    out = dict(first_inputs(seed))
    for name, value in second_inputs(seed + 1).items():
        if name != "x":
            out[name + "_2"] = value
    return out


def reference(
    x, p, rel_bias, lb_param, norm_ffn1, w_ffn1_in, w_ffn1_out, norm_mix, w_in, attn_sinks,
    rec_norm, w_att_proj, w_rec_proj, w_out, norm_ffn2, w_ffn2_in, w_ffn2_out, norm_ple,
    w_ple_gate, w_ple_proj, norm_final, p_2, positions_2, attn_norm_2, ffn_norm_2, ffn_w_in_2,
    ffn_conv_w_2, ffn_conv_b_2, ffn_w_out_2, ple_w_proj_2, ple_norm_2, ple_gate_norm_2,
    ple_w_gate_2, hyb_w_in_2, hyb_w_out_2, rw_mu_2, rw_w0_2, rw_w2_2, rw_a0_2, rw_a2_2, rw_g2_2,
    rw_k_k_2, rw_k_a_2, rw_r_k_2, rw_ln_w_2, rw_ln_b_2, mla_w_down_2, mla_q_norm_2,
    mla_kv_norm_2, mla_w_uq_2, mla_w_ukv_2, mla_w_o_2, final_norm_2,
):
    x = first_block(
        x, p, rel_bias, lb_param, norm_ffn1, w_ffn1_in, w_ffn1_out, norm_mix, w_in, attn_sinks,
        rec_norm, w_att_proj, w_rec_proj, w_out, norm_ffn2, w_ffn2_in, w_ffn2_out, norm_ple,
        w_ple_gate, w_ple_proj, norm_final,
    )
    return second_block(
        x, p_2, positions_2, attn_norm_2, ffn_norm_2, ffn_w_in_2, ffn_conv_w_2, ffn_conv_b_2,
        ffn_w_out_2, ple_w_proj_2, ple_norm_2, ple_gate_norm_2, ple_w_gate_2, hyb_w_in_2,
        hyb_w_out_2, rw_mu_2, rw_w0_2, rw_w2_2, rw_a0_2, rw_a2_2, rw_g2_2, rw_k_k_2, rw_k_a_2,
        rw_r_k_2, rw_ln_w_2, rw_ln_b_2, mla_w_down_2, mla_q_norm_2, mla_kv_norm_2, mla_w_uq_2,
        mla_w_ukv_2, mla_w_o_2, final_norm_2,
    )


_drawn_inputs = setup_inputs


def setup_inputs(seed=0):
    import zlib

    import numpy as np

    out = dict(_drawn_inputs(seed))
    spreads = {}
    factors = {'rec_norm': 3.056,
     'norm_ple': 5.269,
     'ffn_conv_b_2': 8.0,
     'ple_gate_norm_2': 5.81,
     'rw_w2_2': 3.13,
     'rw_a0_2': 4.102,
     'rw_k_k_2': 4.266,
     'rw_k_a_2': 3.017,
     'rw_ln_w_2': 3.019,
     'rw_ln_b_2': 8.0,
     'mla_q_norm_2': 8.0,
     'mla_kv_norm_2': 5.951}
    for name, (base, spread) in spreads.items():
        noise = np.random.default_rng([zlib.crc32(name.encode()), seed]).standard_normal(out[name].shape)
        drawn = base * np.exp(spread * noise) if base else spread * noise
        out[name] = __import__('jax').numpy.asarray(drawn.astype(out[name].dtype))
    for name, factor in factors.items():
        out[name] = (out[name] * factor).astype(out[name].dtype)
    return out
```

```python
from contextlib import ExitStack

import numpy as np

import concourse.bass as bass
from concourse import mybir

F32 = mybir.dt.float32
I32 = mybir.dt.int32
U8 = mybir.dt.uint8
ALU = mybir.AluOpType
ACT = mybir.ActivationFunctionType
AX = mybir.AxisListType

P = 128
SEQ = 256
TT = SEQ // P
D = 1024
KD = D // P
F = 2816
KF = F // P
GROUPS = KF // 2
BAY = 2048
BAYS = 6
EPS = 1e-6
NEG = -1e30


class Signal:

    def __init__(self, ctx, nc, name, book, new):
        self.sem = ctx.enter_context(nc.semaphore(name))
        self.name, self.book, self.new, self.count = name, book, new, 0

    def inc(self, *event, by=1):
        self.count += by
        assert (self.name, event) not in self.new, (self.name, event)
        self.new[self.name, event] = self.count
        return self.sem, by

    def at(self, *event):
        if self.book:
            return self.sem, self.book[self.name, event]
        return self.sem, 1

    def last(self):
        return self.sem, self.count

    def repeated(self, loop, since, times):
        per = self.count - since
        self.new[self.name, ("per", loop)] = per
        self.count = since + per * times

    def at_group(self, i, f, g, *event):
        if not self.book:
            return self.sem, 1
        first = g if g < 4 or g == GROUPS - 1 else 2 + g % 2
        per = self.book[self.name, ("per", f)]
        value = self.book[self.name, (f, first, *event)] + (g - first) // 2 * per
        return self.sem, value if i is None else i * per + value


W_BLOCK, N_BUCKETS, MAX_DIST = 128, 32, 128
LEVELS = [1, 2, 4, 8, 16, 32, 64]
N_MASKS = 2 * len(LEVELS) + 3
EYE, BEFORE, UPTO = 2 * len(LEVELS), 2 * len(LEVELS) + 1, 2 * len(LEVELS) + 2


def host_constants():
    r, c = np.arange(P)[:, None], np.arange(P)[None, :]
    masks = np.zeros((P, N_MASKS, P), np.float32)
    for n, m in enumerate(LEVELS):
        pair = (r // (2 * m) == c // (2 * m)) & (r % (2 * m) < m) & (c % (2 * m) >= m)
        masks[:, n] = pair
        masks[:, len(LEVELS) + n] = pair.T
    masks[:, EYE] = r == c
    masks[:, BEFORE] = r < c
    masks[:, UPTO] = r <= c
    mats = np.zeros((P, 5, P), np.float32)
    mats[:, 0] = r == c
    mats[:, 1] = r // 64 == c // 64
    mats[:, 2] = np.where(c <= r, 0.0, NEG)
    mats[:, 3] = -1.0 * (r >= c)
    mats[:, 4] = -1.0
    dist = 255 - np.arange(383)
    n = np.maximum(dist, 0)
    exact = N_BUCKETS // 2
    large = exact + (np.log(np.maximum(n, 1) / exact) / np.log(MAX_DIST / exact)
                     * (N_BUCKETS - exact)).astype(np.int32)
    bucket = np.where(n < exact, n, np.minimum(large, N_BUCKETS - 1))
    hot = np.zeros((N_BUCKETS + 1, 384), np.float32)
    inside = (dist >= 0) & (dist < W_BLOCK)
    hot[bucket[inside], np.nonzero(inside)[0]] = 1.0
    hot[N_BUCKETS, :383][~inside] = 1.0
    freq = (10000.0 ** (-np.arange(16) / 16)).astype(np.float32)
    return {"masks": masks, "mats": mats, "hot": hot, "freq": freq}


STAGES = ["ffn1", "mix1", "ffn2", "ple1", "block1", "hyb", "conv0", "ple20", "mla", "conv1", "ple21", "all"]
LAST = "all"


def upto(stage):
    return STAGES.index(stage) <= STAGES.index(LAST)


def ktiles(w):
    return w.rearrange("(t p) n -> p t n", p=P)


def build(nc, I, scratch, out, book):
    new = {}
    ctx = ExitStack()
    with ctx:
        def sb(name, shape, dt=F32):
            return ctx.enter_context(nc.sbuf_tensor(name, shape, dt))

        def signal(name):
            return Signal(ctx, nc, name, book, new)

        bay = sb("weight_bays", [P, BAYS, BAY])
        h = sb("h", [P, TT, D])
        hn = sb("h_scaled", [P, TT, D])
        xT = sb("xT", [P, KD, SEQ])
        gpad = sb("conv_input", [P, 2, 2, SEQ + 2])
        cols = sb("vector_columns", [P, 3 * P])
        mats = sb("mats", [P, 5, P])
        masks = sb("masks", [P, N_MASKS, P], U8)
        pT = sb("pT", [P, 3, 2, SEQ])
        ssq = sb("square_sums", [P, 16])
        msq = sb("mean_squares", [P, 16])
        rstd = sb("rstd", [P, 16])
        minus_half = sb("minus_half", [P, 16])
        row_gain = sb("row_gains", [P, 2, D])
        arena = sb("arena", [P, ARENA])

        def carve(at, *shape):
            end = at + int(np.prod(shape))
            assert end <= ARENA, end
            view = arena[:, at:end]
            names = "abcd"[:len(shape)]
            if len(shape) > 1:
                view = view.rearrange(f"p ({' '.join(names)}) -> p {' '.join(names)}", **dict(zip(names, shape)))
            return view, end

        hidT, at = carve(0, 2, 2, SEQ)
        gatev, at = carve(at, 2, 2, SEQ)
        gluT, at = carve(at, 2, 2, SEQ)
        glu2, at = carve(at, 2, 2, SEQ)
        stack, start_at = carve(at, 3, P)
        pin, start_at = carve(start_at, 3, TT, 256)
        mask_rows, start_at = carve(start_at, N_MASKS, P)
        ident = mats[:, 0]
        ps = ctx.enter_context(nc.psum_tensor("ps", [P, 8, 512], F32))

        column, vectors = {}, []
        rows = 0
        for name, ap in [
            ("norm_ffn1", I["norm_ffn1"][0]), ("norm_mix", I["norm_mix"][0]),
            ("norm_ffn2", I["norm_ffn2"][0]), ("norm_ple", I["norm_ple"][0]),
            ("lb0", I["lb_param"][0]), ("lb1", I["lb_param"][1]), ("rec_norm", I["rec_norm"][0]),
            ("attn_norm0", I["attn_norm_2"][0]), ("attn_norm1", I["attn_norm_2"][1]),
            ("conv_norm0", I["ffn_norm_2"][0]), ("conv_norm1", I["ffn_norm_2"][1]),
            ("ple_gate_norm0", I["ple_gate_norm_2"][0]), ("ple_gate_norm1", I["ple_gate_norm_2"][1]),
            *[(f"conv_w{i}{k}", I["ffn_conv_w_2"][i, k]) for i in range(2) for k in range(3)],
            *[(f"conv_b{i}", I["ffn_conv_b_2"][i]) for i in range(2)],
            ("mu", I["rw_mu_2"][0, 0:14 * P]), ("mu_tail", I["rw_mu_2"][0, 14 * P:]),
            ("w0", I["rw_w0_2"][0]), ("a0", I["rw_a0_2"][0]), ("k_k", I["rw_k_k_2"][0]),
            ("k_a", I["rw_k_a_2"][0]), ("r_k", I["rw_r_k_2"][0].rearrange("h e -> (h e)")),
            ("ln_w", I["rw_ln_w_2"][0]), ("ln_b", I["rw_ln_b_2"][0]),
            ("q_norm", I["mla_q_norm_2"][0]), ("kv_norm", I["mla_kv_norm_2"][0]),
        ]:
            n = ap.shape[0]
            column[name] = rows
            c = min(n, P)
            src = ap.rearrange("(r c) -> r c", c=c)
            done = 0
            while done < n // c:
                k = min(n // c - done, P - rows % P)
                vectors.append((stack[rows % P:rows % P + k, rows // P, 0:c], src[done:done + k]))
                rows, done = rows + k, done + k
        assert rows <= 3 * P

        def col(name, j=0):
            return cols[:, column[name] + j:column[name] + j + 1]

        chunks, plan = {}, []

        def chunk(key, view, rows=slice(0, P)):
            chunks[key] = len(chunks)
            plan.append(("chunk", key, view, rows))

        def columns_chunk(key, w, c0, width=256):
            k = w.shape[0] // P
            chunk(key, (0, [k, width], ktiles(w)[:, :, c0:c0 + width]))

        def rows_chunks(key, w):
            for k in range(w.shape[0] // (2 * P)):
                chunk((key, k), (0, [2, D], ktiles(w)[:, 2 * k:2 * k + 2, :]))

        def ffn_chunks(f, w1, w2):
            first = len(chunks)
            plan.append(("ffn", f, ktiles(w1), ktiles(w2)))
            for n in range(3 * GROUPS):
                chunks[f, n] = first + n

        if upto("ffn1"):
            ffn_chunks("ffn1", I["w_ffn1_in"][0], I["w_ffn1_out"][0])
        if upto("mix1"):
            w = I["w_in"][0]
            for n in range(2):
                columns_chunk(("rf", n), w, 1280 + 256 * n)
            for n in range(2):
                columns_chunk(("rq", n), w, 768 + 256 * n)
            for n in range(2):
                columns_chunk(("ri", n), w, 1792 + 256 * n)
            for n in range(2):
                columns_chunk(("aq", n), w, 256 * n)
            columns_chunk("akv", w, 512)
            for n in range(2):
                columns_chunk(("rg", n), w, 2304 + 256 * n)
            for n in range(8):
                columns_chunk(("g", n), w, 2816 + 256 * n)
            rows_chunks("att_proj", I["w_att_proj"][0])
            rows_chunks("rec_proj", I["w_rec_proj"][0])
            rows_chunks("mix_out", I["w_out"][0])
        if upto("ffn2"):
            ffn_chunks("ffn2", I["w_ffn2_in"][0], I["w_ffn2_out"][0])
        if upto("ple1"):
            rows_chunks("ple1_proj", I["w_ple_proj"][0])
            rows_chunks("ple1_gate", I["w_ple_gate"][0])
        if upto("hyb"):
            w = I["hyb_w_in_2"][0]
            R0 = 1536
            for name, c0 in (("wk", R0 + 512), ("wr", R0)):
                for n in range(2):
                    columns_chunk((name, n), w, c0 + 256 * n)
            columns_chunk("lora_in", w, R0 + 1536)
            columns_chunk("lora_in_tail", w, R0 + 1792, 32)
            for n in range(2):
                columns_chunk(("wv", n), w, R0 + 1024 + 256 * n)
            columns_chunk(("sq", 0), w, 0)
            chunk("w2", (0, [1, 512], I["rw_w2_2"][0]), slice(0, 64))
            chunk("a2", (0, [1, 512], I["rw_a2_2"][0]), slice(64, P))
            columns_chunk(("sq", 1), w, 256)
            for n in range(2):
                columns_chunk(("sk", n), w, 512 + 256 * n)
            for n in range(2):
                columns_chunk(("sv", n), w, 1024 + 256 * n)
            chunk("g2", (0, [1, 512], I["rw_g2_2"][0, 0:P]))
            chunk("g2_tail", (0, [1, 512], I["rw_g2_2"][0, P:]), slice(0, 32))
            rows_chunks("hyb_out", I["hyb_w_out_2"][0])
        def ple_chunks(i):
            rows_chunks(f"ple2{i}_proj", I["ple_w_proj_2"][i])
            rows_chunks(f"ple2{i}_gate", I["ple_w_gate_2"][i])

        if upto("conv0"):
            ffn_chunks("conv0", I["ffn_w_in_2"][0], I["ffn_w_out_2"][0])
        if upto("ple20"):
            ple_chunks(0)
        if upto("mla"):
            w = I["mla_w_down_2"][0]
            for n in range(3):
                columns_chunk(("down", n), w, 256 * n, min(256, 672 - 256 * n))
            for n in range(3):
                columns_chunk(("uq", n), I["mla_w_uq_2"][0], 512 * n, 512)
            for n in range(2):
                columns_chunk(("ukv", n), I["mla_w_ukv_2"][0], 1024 * n, 1024)
            rows_chunks("mla_o", I["mla_w_o_2"][0])
        if upto("conv1"):
            ffn_chunks("conv1", I["ffn_w_in_2"][1], I["ffn_w_out_2"][1])
        if upto("ple21"):
            ple_chunks(1)

        landed = [signal(f"weights_landed{b}") for b in range(BAYS)]
        used = signal("weights_used")
        x_in = signal("x_in")
        consts_in = signal("constants_in")
        vectors_in = signal("vectors_in")
        masks_ready = signal("masks_ready")
        zeros = signal("zeros_written")
        cols_turned = signal("vectors_transposed")
        cols_ready = signal("vector_columns_ready")
        dve_step = signal("vector_step")
        act_step = signal("scalar_step")
        pool_step = signal("gpsimd_step")
        h_ready = signal("h_ready")
        squared = signal("squares_summed")
        mean_ready = signal("mean_squares_ready")
        rstd_ready = signal("rstd_ready")
        scaled_d = signal("scaled_by_vector")
        scaled_a = signal("scaled_by_scalar")
        turned = signal("h_transposed")
        x_d = signal("xT_by_vector")
        x_a = signal("xT_by_scalar")
        gate_act = signal("gate_activated")
        conv_out = signal("conv_ready")
        hid_ready = signal("hidden_ready")
        acc_ready = signal("projection_ready")
        stored = signal("output_stored")
        RH, LV = 4, LEVELS + [P]
        AH = 8
        rqT, at = carve(0, RH, SEQ)
        kT, at = carve(at, RH, SEQ)
        fT, at = carve(at, RH, SEQ)
        bT, at = carve(at, RH, SEQ)
        vR, at = carve(at, TT, 512)
        zT, at = carve(at, 2, RH, SEQ)
        orec, _ = carve(at - 2 * RH * SEQ, TT, 512)
        osq, _ = carve(at - RH * SEQ, TT, 512)
        AT, at = carve(at, 3, RH, P)
        sgT, at = carve(at, RH, SEQ)
        gT, at = carve(at, 16, SEQ)
        attT, at = carve(at, 4, SEQ)
        recT, at = carve(at, 4, SEQ)
        aqT, at = carve(at, 4, SEQ)
        akT, at = carve(at, 2, SEQ)
        av, at = carve(at, TT, P)
        sc, at = carve(at, AH, 384)
        pbT, at = carve(at, 3, 384)
        bias, at = carve(at, AH, 384)
        mT, _ = carve(0, KD, SEQ)
        mx = sb("score_max", [P, AH, 2])
        nmx = sb("minus_max", [P, AH, 2])
        den = sb("softmax_sum", [P, AH, 2])
        esink = sb("sink_exp", [P, AH, 2])
        sinkb = sb("sinks", [P, AH])
        lbc = sb("lower_bound", [P, RH])
        lbd = sb("lower_bound_logit", [P, RH])
        omlb = sb("one_minus_lower_bound", [P, RH])
        tab = sb("bias_table", [N_BUCKETS + 1, AH])
        hot_rows, start_at = carve(start_at, 384)
        hot = hot_rows[0:N_BUCKETS + 1]
        tabd_rows, start_at = carve(start_at, 384)
        tabd = tabd_rows[0:AH]
        assert start_at <= ARENA - AH * 384
        ones = sb("ones", [P, SEQ])
        tab_in = signal("bias_table_in")
        tab_out = signal("bias_by_distance_stored")
        bias_in = signal("bias_in")
        bias_p = signal("bias_by_distance")
        bias_d = signal("bias_by_distance_copied")
        lb_d = signal("lower_bound_by_vector")
        lb_a = signal("lower_bound_by_scalar")
        proj_d = signal("projection_kept_by_vector")
        proj_a = signal("projection_kept_by_scalar")
        ak_swapped = signal("keys_swapped")
        att_p = signal("attention_by_tensor")
        att_d = signal("attention_by_vector")
        att_a = signal("attention_by_scalar")
        rec_p = signal("recurrence_by_tensor")
        rec_d = signal("recurrence_by_vector")
        rec_a = signal("recurrence_by_scalar")
        rec_g = signal("recurrence_by_gpsimd")
        pgate, at = carve(0, TT, D)
        pemb, at = carve(at, TT, D)
        pscr, at = carve(at, TT, D)
        ple_p = signal("embedding_projected")
        ple_a = signal("embedding_by_scalar")
        ple_d = signal("embedding_by_vector")
        gains_in = signal("row_gains_in")
        KAPPA = float(np.exp(-0.5))
        RWT = 4
        G, _ = carve(0, 2, 8, 4, P)
        pfT, at = carve(0, 15, SEQ + 1)
        lw, a1 = carve(0, RWT, SEQ)
        cc, a1 = carve(a1, RWT, SEQ)
        dm, a1 = carve(a1, RWT, SEQ)
        assert a1 <= at
        dm0, at = carve(at, RWT, SEQ)
        aT, at = carve(at, RWT, SEQ)
        kk, at = carve(at, RWT, SEQ)
        ktmp, at = carve(at, RWT, SEQ)
        at = max(at, 8192)
        xm, at = carve(at, 15, SEQ)
        obT = xm[:, 0:4]
        bonus = xm[:, 4:8]
        AR, at = carve(at, RWT, 2, 2, P)
        Bk, at_k = carve(at, RWT, SEQ)
        Kk, at_k = carve(at_k, RWT, SEQ)
        M1, _ = carve(at, 4, 4, P)
        at = at_k
        X, at = carve(at, 4, 4, P)
        Y, at = carve(at, 4, 4, P)
        rs, _ = carve(at - 2048 - 2048, 2, 4, 64)
        us, _ = carve(at - 2048 - 2048 + 512, 2, 4, 64)
        yv, _ = carve(at - 2048 - 2048 + 1024, 2, 8, 64)
        qaT, at = carve(at, 4, SEQ)
        kaT, at = carve(at, 4, SEQ)
        va, at = carve(at, TT, 512)
        lsp, at = carve(at, 2, 2, 384)
        wst, at = carve(at, 2, 2, 384)
        ysq, _ = carve(at - 3072, 2, 8, 64)
        oaT, at = carve(at, 4, SEQ)
        vtok = hn[:, 0].rearrange("p (t n) -> p t n", t=TT)
        btok, ktok = hn[:, 1, 0:512], hn[:, 1, 512:1024]
        s0 = sb("state", [P, 4, 64])
        sfac = sb("state_decay", [P, 4])
        gmean = sb("group_mean", [P, 16])
        rw_in = signal("rwkv_projection_kept")
        mix_g = signal("shift_difference")
        mix_d = signal("token_mix")
        pre_d = signal("rwkv_prepared_by_vector")
        pre_a = signal("rwkv_prepared_by_scalar")
        pre_p = signal("rwkv_prepared_by_tensor")
        stick_in = signal("stick_projection_kept")
        stick_p = signal("stick_by_tensor")
        stick_a = signal("stick_by_scalar")
        stick_d = signal("stick_by_vector")
        stick_g = signal("stick_by_gpsimd")
        inv_p = signal("inverse_by_tensor")
        inv_a = signal("inverse_by_scalar")
        inv_d = signal("inverse_by_vector")
        sol_p = signal("solve_by_tensor")
        sol_a = signal("solve_by_scalar")
        sol_d = signal("solve_by_vector")
        LEVEL_N = len(LEVELS)
        MIXES = [(("wk", 0), 4, 2, P), (("wk", 1), 6, 2, P), (("wr", 0), 0, 2, P), (("wr", 1), 2, 2, P),
                 ("lora_in", 12, 2, P), ("lora_in_tail", 14, 1, 32), (("wv", 0), 8, 2, P), (("wv", 1), 10, 2, P)]

        def head(t, hd):
            return t[64 * (hd % 2):64 * (hd % 2) + 64, hd // 2]
        MH, QH = 16, 96
        MSCALE = float(1.0 / np.sqrt(96.0))
        ctok, at = carve(0, TT, 672)
        clT, at = carve(at, 5, SEQ)
        qtok, at = carve(at, TT, MH, QH)
        ktok2, at = carve(at, TT, MH, QH)
        vtk, at = carve(at, TT, MH, 64)
        rt, at = carve(at, 4, TT * MH * 16)
        qkT, at = carve(at, 3, 2, SEQ)
        msc, at = carve(at, 6, 384)
        mpb, at = carve(at, 2, 384)
        moT, at = carve(at, KD, SEQ)
        mlsq, at = carve(at, TT, 640)
        mmax = sb("mla_max", [P, 6, 2])
        mden = sb("mla_sum", [P, 6, 2])
        cosv = sb("cos", [P, TT, 16])
        sinv = sb("sin", [P, TT, 16])
        freq = sb("rotary_frequency", [P, 16])
        posi = sb("positions", [P, TT], I32)
        posf = sb("positions_float", [P, TT])
        ang = sb("angles", [P, TT, 16])
        turns = sb("whole_turns", [P, TT, 16])
        rot_in = signal("rotary_in")
        rot_d = signal("angles_ready")
        rot_a = signal("cos_and_sin_ready")
        lat_a = signal("latent_by_scalar")
        lat_d = signal("latent_by_vector")
        lat_p = signal("latent_transposed")
        up_a = signal("heads_kept_by_scalar")
        up_d = signal("heads_kept_by_vector")
        mla_p = signal("mla_by_tensor")
        mla_a = signal("mla_by_scalar")
        mla_d = signal("mla_by_vector")
        mla_g = signal("mla_by_gpsimd")
        UQ = {(n, t): 2 * n + t for n in range(3) for t in range(TT)}
        UKV = {(n, t, half): (6 + 4 * n + 2 * t + half) % 8 for n in range(2) for t in range(TT) for half in range(2)}
        LAG_S, LAG_T, LAG_V = 1, 4, 5

        def wait_up(eng, bank_no, event):
            eng.wait_ge(*(up_a if bank_no % 2 == 0 else up_d).at(*event))
        def keep_up(eng, parity):
            done = (up_a, up_d)[parity]

            def copy(dst, src):
                return nc.scalar.activation(dst, src, ACT.Copy) if parity == 0 else nc.vector.tensor_copy(dst, src)

            for (n, t), b in UQ.items():
                if b % 2 == parity:
                    eng.wait_ge(*used_up_to(("uq", n)))
                    dst = qtok[:, t].rearrange("p a b -> p (a b)")[:, n * 512:(n + 1) * 512]
                    copy(dst, bank(b)).then_inc(*done.inc("q", b // 2, b % 2))
            for (n, t, half), b in UKV.items():
                if b % 2 == parity:
                    eng.wait_ge(*used_up_to(("ukv", n)))
                    src = bank(b).rearrange("p (a b) -> p a b", a=4)
                    heads = slice(8 * n + 4 * half, 8 * n + 4 * half + 4)
                    copy(ktok2[:, t, heads, 0:64], src[:, :, 0:64])
                    ins = copy(vtk[:, t, heads], src[:, :, 64:128])
            ins.then_inc(*done.inc("last"))
        block = ctx.enter_context(nc.Block())

        def bay_view(key, offset, shape):
            b = bay[:, chunks[key] % BAYS, offset:offset + int(np.prod(shape))]
            return b.rearrange("p (a b) -> p a b", a=shape[0]) if len(shape) == 2 else b

        def bank(b, n=512):
            return ps[:, b, 0:n]

        def used_up_to(key, i=None):
            n = chunks[key] + 1
            return used.sem, n if i is None else i * BAYS + n

        OUT = range(0, 4)

        def ffn_slot(n):
            if n < 2:
                return ("gate", "up")[n], 0
            g, k = (n - 2) // 3 + 1, (n - 2) % 3
            return (("gate", g), ("up", g), ("out", g - 1))[k] if g < GROUPS else ("out", GROUPS - 1)

        def ffn_chunk(kind, g):
            if kind == "out":
                return 3 * g + 4 if g < GROUPS - 1 else 3 * GROUPS - 1
            return 3 * g - (g > 0) + (kind == "up")

        LOOP0, ROUNDS = 2, (GROUPS - 3) // 2

        @block.sync
        def _(sp):
            sp.dma_start(h[:], I["x"][0].rearrange("(t p) d -> p t d", p=P)).then_inc(*x_in.inc("x", by=16))
            sp.dma_start(mats[:], I["mats"]).then_inc(*consts_in.inc("mats", by=16))

            def load(c, dst, src, i=None):
                if i is not None:
                    sp.wait_ge(used.sem, i * BAYS + max(c - BAYS + 1, 1))
                elif c >= BAYS:
                    sp.wait_ge(used.sem, c - BAYS + 1)
                sp.dma_start(dst, src).then_inc(landed[c % BAYS].sem, 16)

            for kind, key, *rest in plan:
                if kind == "chunk":
                    (offset, shape, src), part = rest
                    load(chunks[key], bay_view(key, offset, shape)[part] if shape[0] > 1 else bay[part, chunks[key] % BAYS, 0:shape[1]], src)
                    continue
                w1, w2 = rest
                c0 = chunks[key, 0]

                def group_load(n, i=None):
                    kind, g = ffn_slot(n)
                    if kind == "out":
                        at = sp.snap(i * 4 + 2 * g) if i is not None else 2 * g
                        load(c0 + n, bay_view((key, n), 0, [2, D]), w2[:, bass.ds(at, 2), :], i)
                    else:
                        first = (kind == "up") * F + g * 256
                        at = sp.snap(i * 512 + first) if i is not None else first
                        load(c0 + n, bay_view((key, n), 0, [KD, 256]), w1[:, :, bass.ds(at, 256)], i)

                n0 = ffn_chunk("gate", LOOP0)
                for n in range(n0):
                    group_load(n)
                with sp.Fori(0, ROUNDS) as i:
                    for n in range(n0, n0 + BAYS):
                        group_load(n, i)
                for n in range(n0 + BAYS * ROUNDS, 3 * GROUPS):
                    group_load(n)

        @block.tensor
        def _(pe):
            def weights(key, i=None):
                c = chunks[key]
                count = 16 * (c // BAYS + 1)
                pe.wait_ge(landed[c % BAYS].sem, count if i is None else i * 16 + count)

            def through(mm, key, i=None):
                if i is None:
                    assert not book or used.count == chunks[key], (key, used.count, chunks[key])
                mm.then_inc(*used.inc(key))

            pe.wait_ge(consts_in.sem, 16 * N_CONSTS)
            pe.wait_ge(vectors_in.sem, 16 * len(vectors))
            pe.wait_ge(*zeros.at("stack"))
            for t in range(3):
                mm = nc.tensor.transpose(ps[:, 0, t * P:(t + 1) * P], stack[:, t], ident)
            mm.then_inc(*cols_turned.inc("cols"))
            for n in range(3):
                for k in range(2):
                    for t in range(TT):
                        mm = nc.tensor.transpose(ps[:, 1 + n, k * SEQ + t * P:k * SEQ + (t + 1) * P],
                                                 pin[:, n, t, k * P:(k + 1) * P], ident)
            mm.then_inc(*cols_turned.inc("p"))
            pe.wait_ge(*cols_ready.at("p"))

            def norm(n):
                pe.wait_ge(*scaled_d.at(n))
                for k in range(KD):
                    nc.tensor.transpose(ps[:, 4 + k // 2, (k % 2) * SEQ:(k % 2) * SEQ + P], hn[:, 0, k * P:(k + 1) * P], ident)
                pe.wait_ge(*scaled_a.at(n))
                for k in range(KD):
                    mm = nc.tensor.transpose(ps[:, 4 + k // 2, (k % 2) * SEQ + P:(k % 2 + 1) * SEQ], hn[:, 1, k * P:(k + 1) * P], ident)
                    if k % 2:
                        mm.then_inc(*turned.inc(n, k // 2))
                pe.wait_ge(*x_d.at(n))
                pe.wait_ge(*x_a.at(n))

            def features(dst, lhs, n=KD, rhs=None, **kw):
                for k in range(n):
                    mm = nc.tensor.matmul(dst, lhs(k), xT[:, k] if rhs is None else rhs(k), start=(k == 0), stop=(k == n - 1), **kw)
                return mm

            def ffn(f):
                def into_hidden(g, i=None):
                    gate, up = (f, ffn_chunk("gate", g)), (f, ffn_chunk("up", g))
                    wg, wu = bay_view(gate, 0, [KD, 256]), bay_view(up, 0, [KD, 256])
                    weights(gate, i)
                    if g >= 2:
                        pe.wait_ge(*hid_ready.at_group(i, f, g - 2))
                    for j in range(2):
                        b = 4 + 2 * (g % 2) + j
                        mm = features(ps[:, b, 0:SEQ], lambda k: wg[:, k, j * P:(j + 1) * P])
                        if j == 1:
                            through(mm, gate, i)
                        if j == 0:
                            weights(up, i)
                        mm = features(ps[:, b, SEQ:2 * SEQ], lambda k: wu[:, k, j * P:(j + 1) * P])
                    through(mm, up, i)

                def out_of_hidden(g, i=None):
                    key = (f, ffn_chunk("out", g))
                    w = bay_view(key, 0, [2, D])
                    weights(key, i)
                    pe.wait_ge(*hid_ready.at_group(i, f, g))
                    for t in range(TT):
                        for half in range(2):
                            for j in range(2):
                                mm = nc.tensor.matmul(bank(2 * t + half), hidT[:, g % 2, j, t * P:(t + 1) * P],
                                                      w[:, j, half * 512:(half + 1) * 512],
                                                      start=(g == 0 and j == 0), stop=(g == GROUPS - 1 and j == 1))
                        if g == GROUPS - 1 and t == 0:
                            mm.then_inc(*acc_ready.inc(f, 0))
                    through(mm, key, i)

                into_hidden(0)
                into_hidden(1)
                out_of_hidden(0)
                with pe.Fori(0, ROUNDS) as i:
                    since = used.count
                    for g in (2, 3):
                        into_hidden(g, i)
                        out_of_hidden(g - 1, i)
                    used.repeated(f, since, ROUNDS)
                into_hidden(GROUPS - 1)
                out_of_hidden(GROUPS - 2)
                out_of_hidden(GROUPS - 1)

            def pair_of_features(key, b, tiles=2):
                weights(key)
                w = bay_view(key, 0, [KD, 256])
                for j in range(tiles):
                    mm = features(ps[:, b, j * SEQ:(j + 1) * SEQ], lambda k: w[:, k, j * P:(j + 1) * P])
                through(mm, key)

            def pair_of_tokens(key, b, c0=0, width=256):
                w = bay_view(key, 0, [KD, 256])
                for t in range(TT):
                    for k in range(KD):
                        mm = nc.tensor.matmul(ps[:, b, t * width:(t + 1) * width], xT[:, k, t * P:(t + 1) * P],
                                              w[:, k, c0:c0 + width], start=(k == 0), stop=(k == KD - 1))
                return mm

            def project_features(name, srcT, b0):
                weights((name, 0))
                weights((name, 1))
                w = [bay_view((name, n), 0, [2, D]) for n in range(2)]
                for j in range(KD):
                    for k in range(4):
                        mm = nc.tensor.matmul(ps[:, b0 + j // 2, j % 2 * SEQ:(j % 2 + 1) * SEQ], w[k // 2][:, k % 2, j * P:(j + 1) * P],
                                              srcT[:, k], start=(k == 0), stop=(k == 3))
                        if j == KD - 1 and k == 1:
                            through(mm, (name, 0))
                    if j % 2 and j < KD - 1:
                        mm.then_inc(*att_p.inc(name, j // 2))
                through(mm, (name, 1))

            def project_tokens(name, srcT, key, b0=0, at_chunk={}):
                for n in range(4):
                    if n in at_chunk:
                        at_chunk[n]()
                    weights((name, n))
                    w = bay_view((name, n), 0, [2, D])
                    for t in range(TT):
                        for half in range(2):
                            for j in range(2):
                                k = 2 * n + j
                                mm = nc.tensor.matmul(bank(b0 + 2 * t + half), (srcT(k) if callable(srcT) else srcT[:, k])[:, t * P:(t + 1) * P], w[:, j, half * 512:(half + 1) * 512],
                                                      start=(k == 0), stop=(k == KD - 1))
                        if n == 3 and t == 0:
                            mm.then_inc(*acc_ready.inc(key, 0))
                    through(mm, (name, n))

            def mix1():
                pair_of_features(("rf", 0), 0)
                pair_of_features(("rf", 1), 1)
                pair_of_features(("rq", 0), 2)
                pair_of_features(("rq", 1), 3)
                for n in range(2):
                    weights(("ri", n))
                    pe.wait_ge(*proj_a.at("rf", n))
                    through(pair_of_tokens(("ri", n), n), ("ri", n))
                for n in range(2):
                    pe.wait_ge(*proj_d.at("rq", n))
                    pair_of_features(("aq", n), 2 + n)
                weights("akv")
                pe.wait_ge(*proj_a.at("ri", 0))
                w = bay_view("akv", 0, [KD, 256])
                features(ps[:, 0, 0:SEQ], lambda k: w[:, k, 0:P])
                for t in range(TT):
                    for k in range(KD):
                        mm = nc.tensor.matmul(ps[:, 0, SEQ + t * P:SEQ + (t + 1) * P], xT[:, k, t * P:(t + 1) * P], w[:, k, P:2 * P],
                                              start=(k == 0), stop=(k == KD - 1))
                through(mm, "akv")
                pe.wait_ge(*proj_a.at("ri", 1))
                pair_of_features(("rg", 0), 1)
                pe.wait_ge(*proj_d.at("aq", 0))
                pair_of_features(("rg", 1), 2)
                pe.wait_ge(*proj_d.at("akv"))
                pe.wait_ge(ak_swapped.sem, 32)
                for hd in range(AH):
                    r, j, b = slice(64 * (hd % 2), 64 * (hd % 2) + 64), hd // 2, 4 + hd % 4
                    ak = akT[r, (hd // 4 + hd) % 2]
                    if hd >= 4:
                        pe.wait_ge(*att_d.at("biased", hd - 4))
                    nc.tensor.matmul(ps[:, b, 0:256], aqT[r, j, P:2 * P], ak[:, 0:256], start=True, stop=True)
                    nc.tensor.matmul(ps[:, b, 256:384], aqT[r, j, 0:P], ak[:, 0:P], start=True, stop=True).then_inc(*att_p.inc("scores", hd))
                pe.wait_ge(*att_d.at("biased", AH - 1))
                for n in range(len(LV) + 1):
                    b = 4 + n % 2 * 2
                    if n >= 2:
                        pe.wait_ge(*rec_d.at("placed", n - 2))
                    if n == 0:
                        pe.wait_ge(*rec_d.at("q_and_k"))
                    else:
                        pe.wait_ge(*rec_d.at("decayed", n - 1))
                        z = zT[:, (n - 1) % 2]
                    for t in range(TT if n < len(LV) else 1):
                        for hd in range(RH):
                            o = ps[:, b + t, hd * P:(hd + 1) * P]
                            if n == 0:
                                a, c = kT[:, hd, t * P:(t + 1) * P], rqT[:, hd, t * P:(t + 1) * P]
                            elif n < len(LV):
                                a = c = z[:, hd, t * P:(t + 1) * P]
                            else:
                                a, c = z[:, hd, 0:P], z[:, hd, P:2 * P]
                            mm = nc.tensor.matmul(o, a, c, start=True, stop=True)
                    mm.then_inc(*rec_p.inc("scores", n))
                    if n < 8:
                        pb = (3 + n) % 4
                        if n == 0:
                            pe.wait_ge(*proj_d.at("aq", 1))
                        elif n == 1:
                            pe.wait_ge(*proj_d.at("akv"))
                        elif n < 4:
                            pe.wait_ge(*proj_a.at("rg", n - 2))
                        else:
                            pe.wait_ge(*proj_a.at("g", n - 4))
                        pair_of_features(("g", n), pb)
                pe.wait_ge(*rec_d.at("placed", len(LV)))
                for hd in range(RH):
                    c = slice(hd * P, (hd + 1) * P)
                    mm = nc.tensor.matmul(ps[:, 6, c], AT[:, 0, hd], vR[:, 0, c], start=True, stop=True)
                mm.then_inc(*rec_p.inc("out", 0))
                for hd in range(RH):
                    c = slice(hd * P, (hd + 1) * P)
                    nc.tensor.matmul(ps[:, 7, c], AT[:, 2, hd], vR[:, 0, c], start=True, stop=False)
                    mm = nc.tensor.matmul(ps[:, 7, c], AT[:, 1, hd], vR[:, 1, c], start=False, stop=True)
                mm.then_inc(*rec_p.inc("out", 1))
                pe.wait_ge(*proj_a.at("g", 7))

                def turn(hd):
                    pe.wait_ge(*att_d.at("probs", hd))
                    if hd >= 2:
                        pe.wait_ge(*att_a.at("turned", hd - 2))
                    for n in range(3):
                        mm = nc.tensor.transpose(ps[:, 4 + hd % 2, n * P:(n + 1) * P], sc[:, hd, n * P:(n + 1) * P], ident)
                    mm.then_inc(*att_p.inc("turned", hd))

                turn(0)
                for hd in range(AH):
                    if hd + 1 < AH:
                        turn(hd + 1)
                    pe.wait_ge(*att_a.at("turned", hd))
                    r, kv = slice(64 * (hd % 2), 64 * (hd % 2) + 64), slice(64 * (hd // 4), 64 * (hd // 4) + 64)
                    q = pbT[:, hd % 3]
                    nc.tensor.matmul(ps[r, hd // 2, P:2 * P], av[:, 0, kv], q[:, 0:P], start=True, stop=False)
                    nc.tensor.matmul(ps[r, hd // 2, P:2 * P], av[:, 1, kv], q[:, P:2 * P], start=False, stop=True)
                    nc.tensor.matmul(ps[r, hd // 2, 0:P], av[:, 0, kv], q[:, 2 * P:3 * P], start=True, stop=True).then_inc(*att_p.inc("out", hd))
                for t in range(TT):
                    pe.wait_ge(*rec_d.at("normed", t))
                for k in range(4):
                    for t in range(TT):
                        mm = nc.tensor.transpose(ps[:, 6 + k // 2, k % 2 * SEQ + t * P:k % 2 * SEQ + (t + 1) * P], orec[:, t, k * P:(k + 1) * P], ident)
                    if k % 2:
                        mm.then_inc(*rec_p.inc("turned", k // 2))
                pe.wait_ge(*att_d.at("outT", 3))
                project_features("att_proj", attT, 0)
                pe.wait_ge(*rec_d.at("recT", 1))
                project_features("rec_proj", recT, 4)
                pe.wait_ge(*att_d.at("merged", 3))
                project_tokens("mix_out", mT, "mix1")

            def ple(stage, n):
                key = (f"{stage}_proj", 0)
                weights(key)
                w = bay_view(key, 0, [2, D])
                for t in range(TT):
                    pe.wait_ge(*h_ready.at(stage, t))
                    for half in range(2):
                        for k in range(2):
                            mm = nc.tensor.matmul(bank(2 * t + half), pT[:, n, k, t * P:(t + 1) * P], w[:, k, half * 512:(half + 1) * 512],
                                                  start=(k == 0), stop=(k == 1))
                through(mm, key)
                norm(stage)
                project_tokens(f"{stage}_gate", xT, stage, b0=4)

            def hyb():
                norm("hyb")
                pair_of_features(("wk", 0), 0)
                pair_of_features(("wk", 1), 1)
                pair_of_features(("wr", 0), 2)
                pair_of_features(("wr", 1), 3)
                pe.wait_ge(*rw_in.at(("wk", 0)))
                pair_of_features("lora_in", 0)
                weights("lora_in_tail")
                pe.wait_ge(*rw_in.at(("wk", 1)))
                w = bay_view("lora_in_tail", 0, [KD, 32])
                through(features(ps[0:32, 1, 0:SEQ], lambda k: w[:, k, :]), "lora_in_tail")
                pe.wait_ge(*rw_in.at(("wr", 0)))
                pair_of_features(("wv", 0), 2)
                pe.wait_ge(*rw_in.at(("wr", 1)))
                pair_of_features(("wv", 1), 3)
                pe.wait_ge(*rw_in.at("lora_in"))
                pair_of_features(("sq", 0), 0)
                pe.wait_ge(*pre_a.at("tanh"))
                for key, r, b in (("w2", slice(0, 64), 4), ("a2", slice(64, P), 6)):
                    weights(key)
                    w = bay[r, chunks[key] % BAYS, 0:512]
                    for j in range(RWT):
                        mm = nc.tensor.matmul(ps[:, b + j // 2, j % 2 * SEQ:(j % 2 + 1) * SEQ], w[:, j * P:(j + 1) * P], xm[r, 12],
                                              start=True, stop=True)
                    through(mm, key)
                pe.wait_ge(*rw_in.at("lora_in_tail"))
                pair_of_features(("sq", 1), 1)
                pe.wait_ge(*rw_in.at(("wv", 0)))
                pair_of_features(("sk", 0), 2)
                pe.wait_ge(*pre_d.at("kk_squares"))
                pe.wait_ge(*pre_a.at("decay"))
                for j in range(RWT):
                    mm = nc.tensor.matmul(ps[:, 4 + j // 2, j % 2 * SEQ:(j % 2 + 1) * SEQ], mats[:, 1], dm0[:, j], start=True, stop=True)
                mm.then_inc(*pre_p.inc("kk_sums"))
                pe.wait_ge(*rw_in.at(("wv", 1)))
                pair_of_features(("sk", 1), 3)
                pe.wait_ge(*mix_d.at(("wv", 1)))
                pe.wait_ge(*pre_a.at("rate"))
                for t in range(TT):
                    for j in range(4):
                        mm = nc.tensor.transpose(ps[:, 6 + t, j * P:(j + 1) * P], xm[:, 8 + j, t * P:(t + 1) * P], ident)
                mm.then_inc(*pre_p.inc("v_turned"))
                pe.wait_ge(*stick_in.at("sq", 0))
                weights(("sv", 0))
                through(pair_of_tokens(("sv", 0), 0), ("sv", 0))
                pe.wait_ge(*stick_in.at("sq", 1))
                weights(("sv", 1))
                through(pair_of_tokens(("sv", 1), 1), ("sv", 1))
                pe.wait_ge(*pre_d.at("bonus_terms"))
                pe.wait_ge(*pre_d.at("kk_norm"))
                for j in range(RWT):
                    mm = nc.tensor.matmul(ps[:, 4 + j // 2, j % 2 * SEQ:(j % 2 + 1) * SEQ], mats[:, 1], xm[:, j], start=True, stop=True)
                mm.then_inc(*pre_p.inc("bonus"))
                pe.wait_ge(*pre_d.at("bk"))
                pe.wait_ge(*pre_a.at("vtok"))
                for n, t in enumerate((Bk, Kk)):
                    for j in range(4):
                        mm = nc.tensor.transpose(ps[:, 6 + n, j * P:(j + 1) * P], t[:, j, 0:P], ident)
                mm.then_inc(*pre_p.inc("bk_turned"))
                for n in range(16):
                    c, hd, b = n // 8, n % 8, n % 4
                    if n < 4:
                        pe.wait_ge(*(stick_in.at("sv", n) if n < 2 else stick_in.at("sk", n - 2)))
                    else:
                        pe.wait_ge(*inv_d.at("scores", n - 4))
                    ar = head(AR, hd)[:, c].rearrange("p a t -> p (a t)")
                    nc.tensor.matmul(ps[:, b, 0:256], head(Bk, hd)[:, c * P:(c + 1) * P], ar, start=True, stop=True)
                    nc.tensor.matmul(ps[:, b, 256:512], head(Kk, hd)[:, c * P:(c + 1) * P], ar, start=True, stop=True).then_inc(*inv_p.inc("scores", n))

                def stick_scores(g):
                    if g == 0:
                        pe.wait_ge(*pre_d.at("bonus"))
                    if g == 1:
                        pe.wait_ge(*pre_a.at("bk_turned"))
                    if g >= 2:
                        pe.wait_ge(*stick_a.at("out", g - 2))
                    for n in range(2):
                        b, q, k = 4 + 2 * (g % 2) + n, head(qaT, 2 * g + n), head(kaT, 2 * g + n)
                        nc.tensor.matmul(ps[:, b, 0:256], k[:, 0:P], q, start=True, stop=False, skip_group_check=True)
                        mm = nc.tensor.matmul(ps[:, b, 256:384], k[:, P:2 * P], q[:, P:2 * P], start=False, stop=False, skip_group_check=True)
                    mm.then_inc(*stick_p.inc("scores", g))

                def stick_sums(g):
                    pe.wait_ge(*stick_g.at("softplus", g))
                    for n in range(2):
                        b, s = 4 + 2 * (g % 2) + n, lsp[:, g % 2, n]
                        nc.tensor.matmul(ps[:, b, 0:384], mats[:, 3], s, start=False, stop=False, skip_group_check=True)
                        mm = nc.tensor.matmul(ps[:, b, P:2 * P], mats[:, 4], s[:, 256:384], start=False, stop=True, skip_group_check=True)
                    mm.then_inc(*stick_p.inc("sums", g))

                def stick_out(g):
                    pe.wait_ge(*stick_g.at("weights", g))
                    for n in range(2):
                        hd = 2 * g + n
                        o, w = ps[64 * n:64 * n + 64, 4 + 2 * (g % 2), 0:256], wst[:, g % 2, n]
                        nc.tensor.matmul(o, va[:, 0, hd * 64:(hd + 1) * 64], w[:, 0:256], start=True, stop=False, skip_group_check=True)
                        mm = nc.tensor.matmul(o[:, P:2 * P], va[:, 1, hd * 64:(hd + 1) * 64], w[:, 256:384], start=False, stop=True, skip_group_check=True)
                    mm.then_inc(*stick_p.inc("out", g))

                def level(n):
                    if n:
                        for g in range(4):
                            pe.wait_ge(*inv_d.at("X", n - 1, g))
                            for i in range(4):
                                mm = nc.tensor.matmul(ps[:, g, i * P:(i + 1) * P], G[:, g // 2, g % 2 * 4 + i, 0], X[:, g, i], start=True, stop=True)
                            mm.then_inc(*inv_p.inc("M1", n, g))
                        for g in range(4):
                            pe.wait_ge(*inv_a.at("M1", n, g))
                            for i in range(4):
                                mm = nc.tensor.matmul(ps[:, g, i * P:(i + 1) * P], M1[:, g, i], Y[:, g, i], start=True, stop=True)
                            mm.then_inc(*inv_p.inc("Y", n, g))
                    if n < LEVEL_N - 1:
                        for g in range(4):
                            pe.wait_ge(*inv_d.at("Y", n, g))
                            for i in range(4):
                                mm = nc.tensor.transpose(ps[:, g, i * P:(i + 1) * P], Y[:, g, i], ident)
                            mm.then_inc(*inv_p.inc("X", n, g))

                pe.wait_ge(*inv_d.at("scores", 15))
                stick_scores(0)
                level(0)
                stick_scores(1)
                level(1)
                stick_sums(0)
                level(2)
                stick_out(0)
                stick_sums(1)
                stick_scores(2)
                level(3)
                stick_out(1)
                stick_scores(3)
                stick_sums(2)
                level(4)
                stick_out(2)
                stick_sums(3)
                level(5)
                stick_out(3)
                level(6)

                def cols64(b, hd):
                    return ps[:, b, hd // 2 * 64:hd // 2 * 64 + 64]

                for c in range(2):
                    if c == 0:
                        pe.wait_ge(*stick_a.at("out", 2))
                        pe.wait_ge(*stick_a.at("out", 3))
                    else:
                        pe.wait_ge(*sol_d.at("state"))
                    for hd in range(8):
                        o, vv = cols64(4 + hd % 2, hd), vtok[:, c, hd * 64:(hd + 1) * 64]
                        if c:
                            nc.tensor.matmul(o, head(AR, hd)[:, c, 0], head(s0, hd), start=True, stop=False)
                        mm = nc.tensor.matmul(o, G[:, c, hd, 2], vv, start=(c == 0), stop=True)
                    mm.then_inc(*sol_p.inc("rhs", c))
                    pe.wait_ge(*sol_a.at("rhs", c))
                    if c == 0:
                        for g in range(4):
                            pe.wait_ge(*inv_d.at("Y", LEVEL_N - 1, g))
                    for hd in range(8):
                        mm = nc.tensor.matmul(ps[:, 6, (hd % 2 * 4 + hd // 2) * 64:(hd % 2 * 4 + hd // 2 + 1) * 64],
                                              Y[:, c * 2 + hd // 4, hd % 4], rs[:, hd % 2, hd // 2], start=True, stop=True)
                    mm.then_inc(*sol_p.inc("u", c))
                    pe.wait_ge(*sol_a.at("u", c))
                    if c == 0:
                        for hd in range(8):
                            o = ps[64 * (hd % 2):64 * (hd % 2) + 64, 7, hd // 2 * 64:hd // 2 * 64 + 64]
                            nc.tensor.matmul(o, btok[:, hd * 64:(hd + 1) * 64], us[:, hd % 2, hd // 2], start=True, stop=False)
                            mm = nc.tensor.matmul(o, ktok[:, hd * 64:(hd + 1) * 64], vtok[:, 0, hd * 64:(hd + 1) * 64], start=False, stop=True)
                        mm.then_inc(*sol_p.inc("state"))
                    for hd in range(8):
                        o = cols64(4 + hd % 2, hd)
                        if c:
                            nc.tensor.matmul(o, head(AR, hd)[:, c, 1], head(s0, hd), start=True, stop=False)
                        nc.tensor.matmul(o, G[:, c, hd, 1], us[:, hd % 2, hd // 2], start=(c == 0), stop=False)
                        mm = nc.tensor.matmul(o, G[:, c, hd, 3], vtok[:, c, hd * 64:(hd + 1) * 64], start=False, stop=True)
                    mm.then_inc(*sol_p.inc("y", c))
                    if c == 0:
                        pe.wait_ge(*sol_a.at("y", 0))
                pe.wait_ge(*sol_a.at("u", 1))
                weights("g2")
                weights("g2_tail")
                w, wt = bay[:, chunks["g2"] % BAYS, 0:512], bay[0:32, chunks["g2_tail"] % BAYS, 0:512]
                pe.wait_ge(*sol_d.at("state"))
                for j in range(RWT):
                    o = ps[:, 6 + j // 2, j % 2 * SEQ:(j % 2 + 1) * SEQ]
                    nc.tensor.matmul(o, w[:, j * P:(j + 1) * P], xm[:, 13], start=True, stop=False)
                    mm = nc.tensor.matmul(o, wt[:, j * P:(j + 1) * P], xm[0:32, 14], start=False, stop=True)
                mm.then_inc(*used.inc("g2", by=2))

                def turn_y():
                    pe.wait_ge(*sol_d.at("normed"))
                    for k in range(4):
                        for t in range(TT):
                            mm = nc.tensor.transpose(ps[:, 4 + k // 2, k % 2 * SEQ + t * P:k % 2 * SEQ + (t + 1) * P],
                                                     yv[:, t].rearrange("p a b -> p (a b)")[:, k * P:(k + 1) * P], ident)
                    mm.then_inc(*sol_p.inc("turned"))

                def rwkv_part():
                    turn_y()
                    pe.wait_ge(*sol_d.at("ob"))

                for g in range(4):
                    pe.wait_ge(*inv_d.at("Y", LEVEL_N - 1, g))
                project_tokens("hyb_out", lambda k: oaT[:, k] if k < 4 else obT[:, k - 4], "hyb", at_chunk={2: rwkv_part})

            def mla():
                norm("mla")
                for n in range(3):
                    key, width = ("down", n), min(256, 672 - 256 * n)
                    weights(key)
                    w = bay_view(key, 0, [KD, width])
                    for t in range(TT):
                        o = ps[:, t + n // 2 * 2, n % 2 * 256:n % 2 * 256 + width]
                        for k in range(KD):
                            mm = nc.tensor.matmul(o, xT[:, k, t * P:(t + 1) * P], w[:, k, :], start=(k == 0), stop=(k == KD - 1))
                    through(mm, key)
                pe.wait_ge(*lat_d.at("scaled"))
                for j in range(5):
                    for t in range(TT):
                        mm = nc.tensor.transpose(ps[:, 4 + j // 2, j % 2 * SEQ + t * P:j % 2 * SEQ + (t + 1) * P],
                                                 ctok[:, t, j * P:(j + 1) * P], ident)
                mm.then_inc(*lat_p.inc("turned"))
                pe.wait_ge(*lat_d.at("q"))
                pe.wait_ge(*lat_a.at("kv"))
                for n in range(3):
                    key = ("uq", n)
                    weights(key)
                    w = bay_view(key, 0, [3, 512])
                    for t in range(TT):
                        for k in range(3):
                            mm = nc.tensor.matmul(bank(UQ[n, t]), clT[:, k, t * P:(t + 1) * P], w[:, k, :], start=(k == 0), stop=(k == 2))
                    through(mm, key)
                for n in range(2):
                    key = ("ukv", n)
                    weights(key)
                    w = bay_view(key, 0, [2, 1024])
                    for t in range(TT):
                        for half in range(2):
                            b = UKV[n, t, half]
                            if b < 6:
                                wait_up(pe, b, ("q", b // 2, b % 2))
                            for k in range(2):
                                mm = nc.tensor.matmul(bank(b), clT[:, 3 + k, t * P:(t + 1) * P], w[:, k, half * 512:(half + 1) * 512],
                                                      start=(k == 0), stop=(k == 1))
                    through(mm, key)
                pe.wait_ge(*up_a.at("last"))
                pe.wait_ge(*up_d.at("last"))
                pe.wait_ge(*mla_d.at("rotated"))
                for i in range(MH + LAG_V):
                    if i < MH:
                        if i >= 2:
                            pe.wait_ge(*(mla_a if i % 2 == 0 else mla_d).at("turned", i - 2))
                        for n, s in enumerate((qtok, ktok2)):
                            for t in range(TT):
                                mm = nc.tensor.transpose(ps[0:QH, 4 + i % 2, n * SEQ + t * P:n * SEQ + (t + 1) * P], s[:, t, i], ident)
                        mm.then_inc(*mla_p.inc("turned", i))
                    hd = i - LAG_S
                    if 0 <= hd < MH:
                        pe.wait_ge(*(mla_a if hd % 2 == 0 else mla_d).at("turned", hd))
                        if hd >= 2:
                            pe.wait_ge(*mla_d.at("masked", hd - 2))
                        q, k, b = qkT[0:QH, hd % 3, 0], qkT[0:QH, hd % 3, 1], 6 + hd % 2
                        nc.tensor.matmul(ps[:, b, 0:256], q[:, P:2 * P], k, start=True, stop=True)
                        nc.tensor.matmul(ps[:, b, 256:384], q[:, 0:P], k[:, 0:P], start=True, stop=True).then_inc(*mla_p.inc("scores", hd))
                    hd = i - LAG_T
                    if 0 <= hd < MH:
                        pe.wait_ge(*mla_g.at("probs", hd))
                        if hd >= 2:
                            pe.wait_ge(*mla_a.at("probs", hd - 2))
                        for n in range(3):
                            mm = nc.tensor.transpose(ps[:, hd % 2, n * P:(n + 1) * P], msc[:, hd % 6, n * P:(n + 1) * P], ident)
                        mm.then_inc(*mla_p.inc("probs", hd))
                    hd = i - LAG_V
                    if 0 <= hd < MH:
                        pe.wait_ge(*mla_a.at("probs", hd))
                        if hd % 2 == 0 and hd >= 4:
                            pe.wait_ge(*mla_a.at("out", hd // 2 - 2))
                        r, b, q = slice(64 * (hd % 2), 64 * (hd % 2) + 64), 2 + hd // 2 % 2, mpb[:, hd % 2]
                        nc.tensor.matmul(ps[r, b, P:2 * P], vtk[:, 0, hd], q[:, 0:P], start=True, stop=False)
                        nc.tensor.matmul(ps[r, b, P:2 * P], vtk[:, 1, hd], q[:, P:2 * P], start=False, stop=True)
                        nc.tensor.matmul(ps[r, b, 0:P], vtk[:, 0, hd], q[:, 2 * P:3 * P], start=True, stop=True).then_inc(*mla_p.inc("out", hd))
                pe.wait_ge(*mla_a.at("out", MH // 2 - 1))
                project_tokens("mla_o", moT, "mla")

            if upto("ffn1"):
                norm("ffn1")
                ffn("ffn1")
            pe.wait_ge(tab_in.sem, 32)
            pe.wait_ge(*zeros.at("tab"))
            nc.tensor.matmul(ps[0:AH, 7, 0:384], tab[:], hot[:], start=True, stop=True).then_inc(*bias_p.inc("t"))
            pe.wait_ge(*bias_d.at("t"))
            if upto("mix1"):
                norm("mix1")
                mix1()
            if upto("ffn2"):
                norm("ffn2")
                ffn("ffn2")
            if upto("ple1"):
                ple("ple1", 0)
            if upto("hyb"):
                hyb()
            if upto("conv0"):
                norm("conv0")
                ffn("conv0")
            if upto("ple20"):
                ple("ple20", 1)
            if upto("mla"):
                mla()
            if upto("conv1"):
                norm("conv1")
                ffn("conv1")
            if upto("ple21"):
                ple("ple21", 2)

        @block.scalar
        def _(act):
            def step(ins):
                ins.then_inc(*act_step.inc(act_step.count))
                act.wait_ge(*act_step.last())

            act.dma_start(mask_rows, I["masks"]).then_inc(consts_in.sem, 16)
            act.wait_ge(*zeros.at("stack"))
            for dst, src in vectors:
                act.dma_start(dst, src).then_inc(vectors_in.sem, 16)
            act.dma_start(pin[:, 0], I["p"][0, 0].rearrange("(t p) d -> p t d", p=P)).then_inc(consts_in.sem, 16)
            for i in range(2):
                act.dma_start(pin[:, 1 + i], I["p_2"][i, 0].rearrange("(t p) d -> p t d", p=P)).then_inc(consts_in.sem, 16)
            act.dma_start(sinkb[:], I["attn_sinks"][0].partition_broadcast(P)).then_inc(consts_in.sem, 16)
            act.dma_start(tab[0:N_BUCKETS, :], I["rel_bias"]).then_inc(tab_in.sem, 16)
            act.dma_start(hot[:], I["hot"]).then_inc(tab_in.sem, 16)
            act.dma_start(row_gain[:, 0], I["norm_final"].partition_broadcast(P)).then_inc(gains_in.sem, 16)
            act.dma_start(row_gain[:, 1], I["ple_norm_2"][0].partition_broadcast(P)).then_inc(gains_in.sem, 16)
            with nc.allow_non_contiguous_dma(reason="256 positions, one to a partition and tile"):
                act.dma_start(posi[:], I["positions_2"][0].rearrange("(t p) -> p t", p=P)).then_inc(rot_in.sem, 16)
            act.dma_start(freq[:], I["freq"].partition_broadcast(P)).then_inc(rot_in.sem, 16)

            def norm(n, gain):
                for t in range(TT):
                    if n == "ffn1":
                        act.wait_ge(*x_in.at("x"))
                    else:
                        act.wait_ge(*h_ready.at(n, t))
                    nc.scalar.activation(hn[:, t], h[:, t], ACT.Square, accum_out=ssq[:, t:t + 1]).then_inc(*squared.inc(n, t))
                act.wait_ge(*rstd_ready.at(n))
                nc.scalar.activation(hn[:, 1], h[:, 1], ACT.Copy, scale=rstd[:, 1:2]).then_inc(*scaled_a.inc(n))
                for k in range(KD // 2, KD):
                    if k % 2 == 0:
                        act.wait_ge(*turned.at(n, k // 2))
                    ins = nc.scalar.activation(xT[:, k], ps[:, 4 + k // 2, k % 2 * SEQ:(k % 2 + 1) * SEQ], ACT.Copy,
                                               scale=col(gain, k))
                ins.then_inc(*x_a.inc(n))

            def ffn(f, conv):
                def group(g, i=None):
                    act.wait_ge(*used_up_to((f, ffn_chunk("up", g)), i))
                    gate = ps[:, 4 + 2 * (g % 2):6 + 2 * (g % 2), 0:SEQ]
                    if not conv:
                        if g >= 2:
                            act.wait_ge(*hid_ready.at_group(i, f, g - 2))
                        nc.scalar.activation(gatev[:, g % 2], gate, ACT.Sigmoid).then_inc(*gate_act.inc(f, g))
                    else:
                        gin = ps[:, 4 + 2 * (g % 2):6 + 2 * (g % 2), SEQ:2 * SEQ]
                        if g >= 2:
                            act.wait_ge(*hid_ready.at_group(i, f, g - 2))
                        nc.scalar.activation(gpad[:, g % 2, :, 2:2 + SEQ], gin, ACT.Copy).then_inc(*gate_act.inc(f, g))
                        act.wait_ge(*conv_out.at_group(i, f, g))
                        nc.scalar.activation(gatev[:, g % 2], gluT[:, g % 2], ACT.Gelu).then_inc(*gate_act.inc(f, g, "gelu"))

                group(0)
                group(1)
                with act.Fori(0, ROUNDS) as i:
                    since = gate_act.count
                    group(2, i)
                    group(3, i)
                    gate_act.repeated(f, since, ROUNDS)
                group(GROUPS - 1)

            def keep(dst, b, key, *event, c=slice(0, 512), func=ACT.Copy):
                act.wait_ge(*used_up_to(key))
                src = ps[:, b, c]
                if len(dst.shape) == 3:
                    src = src.rearrange("p (a b) -> p a b", a=dst.shape[1])
                nc.scalar.activation(dst, src, func).then_inc(*proj_a.inc(*event))

            def mix1():
                for n in range(2):
                    keep(fT[:, 2 * n:2 * n + 2], n, ("rf", n), "rf", n, func=ACT.Sigmoid)
                for n in range(2):
                    keep(vR[:, :, n * 256:(n + 1) * 256], n, ("ri", n), "ri", n)
                act.wait_ge(*rec_d.at("f"))
                nc.scalar.activation(bT[:], fT[:], ACT.Ln).then_inc(*rec_a.inc("log"))
                act.wait_ge(*proj_d.at("akT"))
                act.dma_start(akT[0:64, 1], akT[64:P, 0]).then_inc(ak_swapped.sem, 16)
                act.dma_start(akT[64:P, 1], akT[0:64, 0]).then_inc(ak_swapped.sem, 16)
                for n in range(2):
                    keep(sgT[:, 2 * n:2 * n + 2], 1 + n, ("rg", n), "rg", n)
                act.wait_ge(*att_d.at("minus_max"))
                nc.scalar.activation(esink[:], esink[:], ACT.Exp).then_inc(*att_a.inc("sink"))
                for hd in range(AH):
                    for n, c in enumerate((slice(0, 256), slice(256, 384))):
                        ins = nc.scalar.activation(sc[:, hd, c], sc[:, hd, c], ACT.Exp, bias=nmx[:, hd, n:n + 1], accum_out=den[:, hd, n:n + 1])
                    ins.then_inc(*att_a.inc("exp", hd))
                for n in range(len(LV)):
                    act.wait_ge(*rec_g.at("differences", n))
                    nc.scalar.activation(zT[:, n % 2], zT[:, n % 2], ACT.Exp).then_inc(*rec_a.inc("decay", n))
                    keep(gT[:, 2 * n:2 * n + 2], (3 + n) % 4, ("g", n), "g", n)
                act.wait_ge(*proj_a.last())
                nc.scalar.activation(sgT[:], sgT[:], ACT.Sigmoid).then_inc(*att_a.inc("gate_r"))
                nc.scalar.activation(gT[:], gT[:], ACT.Sigmoid).then_inc(*att_a.inc("gates"))
                for hd in range(2):
                    turned_probs(hd)
                for t in range(TT):
                    act.wait_ge(*rec_p.at("out", t))
                    if t == 0:
                        act.wait_ge(*rec_d.at("placed", len(LV)))
                    nc.scalar.activation(osq[:, t], ps[:, 6 + t], ACT.Square).then_inc(*rec_a.inc("squares", t))
                for hd in range(2, AH):
                    turned_probs(hd)

            def turned_probs(hd):
                act.wait_ge(*att_p.at("turned", hd))
                if hd >= 3:
                    act.wait_ge(*att_p.at("out", hd - 3))
                nc.scalar.activation(pbT[:, hd % 3], ps[:, 4 + hd % 2, 0:384], ACT.Copy).then_inc(*att_a.inc("turned", hd))

            def ple(stage, gain, normed):
                norm(stage, gain)
                if normed:
                    act.wait_ge(*used_up_to((f"{stage}_proj", 0)))
                    for t in range(TT):
                        ins = nc.scalar.activation(pscr[:, t], ps[:, 2 * t:2 * t + 2].rearrange("p a b -> p (a b)"), ACT.Square,
                                                   accum_out=ssq[:, 2 + t:3 + t])
                    ins.then_inc(*ple_a.inc(stage, "squares"))
                for t in range(TT):
                    act.wait_ge(*(acc_ready.at(stage, 0) if t == 0 else used_up_to((f"{stage}_gate", 3))))
                    nc.scalar.activation(pgate[:, t], ps[:, 4 + 2 * t:6 + 2 * t].rearrange("p a b -> p (a b)"), ACT.Sigmoid).then_inc(*ple_a.inc(stage, t))

            def squares_of_h(n):
                for t in range(TT):
                    act.wait_ge(*h_ready.at(n, t))
                    nc.scalar.activation(hn[:, t], h[:, t], ACT.Square, accum_out=ssq[:, t:t + 1]).then_inc(*squared.inc(n, t))

            def hyb():
                norm("hyb", "attn_norm0")

                def keep_rw(key, tile, b, tiles=2, rows=P):
                    act.wait_ge(*used_up_to(key))
                    if key == ("wk", 0):
                        act.wait_ge(*mix_g.at("zero"))
                    nc.scalar.activation(pfT[0:rows, tile:tile + tiles, 1:], ps[0:rows, b, 0:tiles * SEQ].rearrange("p (a b) -> p a b", a=tiles),
                                         ACT.Copy).then_inc(*rw_in.inc(key))

                def keep_stick(name, n, b, dst, scale=1.0):
                    act.wait_ge(*used_up_to((name, n)))
                    src = ps[:, b].rearrange("p (a b) -> p a b", a=2)
                    nc.scalar.activation(dst, src, ACT.Copy, scale=scale).then_inc(*stick_in.inc(name, n))

                keep_rw(("wk", 0), 4, 0)
                keep_rw(("wk", 1), 6, 1)
                keep_rw(("wr", 0), 0, 2)
                keep_rw(("wr", 1), 2, 3)
                keep_rw("lora_in", 12, 0)
                keep_rw("lora_in_tail", 14, 1, 1, 32)
                act.wait_ge(*mix_d.at("lora_in"))
                nc.scalar.activation(xm[0:64, 12], xm[0:64, 12], ACT.Tanh).then_inc(*pre_a.inc("tanh"))
                nc.scalar.activation(xm[:, 13], xm[:, 13], ACT.Sigmoid)
                act.wait_ge(*mix_d.at("lora_in_tail"))
                nc.scalar.activation(xm[0:32, 14], xm[0:32, 14], ACT.Sigmoid)
                keep_rw(("wv", 0), 8, 2)
                keep_rw(("wv", 1), 10, 3)
                keep_stick("sq", 0, 0, qaT[:, 0:2], 0.125)
                act.wait_ge(*mix_d.at(("wv", 1)))
                for key, dst, b, bias_name, event in (("w2", lw, 4, "w0", "decay"), ("a2", aT, 6, "a0", "rate")):
                    act.wait_ge(*used_up_to(key))
                    for j in range(RWT):
                        ins = nc.scalar.activation(dst[:, j], ps[:, b + j // 2, j % 2 * SEQ:(j % 2 + 1) * SEQ], ACT.Sigmoid, bias=col(bias_name, j))
                    ins.then_inc(*pre_a.inc(event))
                keep_stick("sq", 1, 1, qaT[:, 2:4], 0.125)
                act.wait_ge(*pre_d.at("kk_sums"))
                nc.scalar.activation(ktmp[:], ktmp[:], ACT.Sqrt).then_inc(*pre_a.inc("kk_norm"))
                keep_stick("sk", 0, 2, kaT[:, 0:2])
                act.wait_ge(*pre_d.at("dm"))
                nc.scalar.activation(cc[:], dm[:], ACT.Exp, scale=KAPPA)
                nc.scalar.activation(dm[:], dm[:], ACT.Exp, scale=-KAPPA)
                nc.scalar.activation(dm0[:], dm0[:], ACT.Exp, scale=-KAPPA)
                nc.scalar.activation(sfac[:], sfac[:], ACT.Exp, scale=-KAPPA).then_inc(*pre_a.inc("exps"))
                keep_stick("sk", 1, 3, kaT[:, 2:4])
                act.wait_ge(*pre_p.at("v_turned"))
                nc.scalar.activation(vtok[:], ps[:, 6:8], ACT.Copy).then_inc(*pre_a.inc("vtok"))
                keep_stick("sv", 0, 0, va[:, :, 0:256])
                keep_stick("sv", 1, 1, va[:, :, 256:512])
                act.wait_ge(*pre_p.at("bk_turned"))
                nc.scalar.activation(hn[:, 1], ps[:, 6:8].rearrange("p a b -> p (a b)"), ACT.Copy).then_inc(*pre_a.inc("bk_turned"))

                def stick_softplus(g):
                    act.wait_ge(*stick_p.at("scores", g))
                    z = ps[:, 4 + 2 * (g % 2):6 + 2 * (g % 2), 0:384]
                    s = lsp[:, g % 2]
                    step(nc.scalar.activation(s, z, ACT.Abs))
                    step(nc.scalar.activation(s, s, ACT.Exp, scale=-1.0))
                    nc.scalar.activation(s, s, ACT.Ln, bias=1.0).then_inc(*stick_a.inc("log", g))

                def stick_weights(g):
                    act.wait_ge(*stick_p.at("sums", g))
                    nc.scalar.activation(wst[:, g % 2], ps[:, 4 + 2 * (g % 2):6 + 2 * (g % 2), 0:384], ACT.Exp).then_inc(*stick_a.inc("weights", g))

                def stick_keep(g):
                    act.wait_ge(*stick_p.at("out", g))
                    nc.scalar.activation(oaT[:, g], ps[:, 4 + 2 * (g % 2), 0:256], ACT.Copy).then_inc(*stick_a.inc("out", g))

                def level(n):
                    for g in range(4):
                        act.wait_ge(*inv_p.at("M1", n, g))
                        nc.scalar.activation(M1[:, g], ps[:, g].rearrange("p (a b) -> p a b", a=4), ACT.Copy).then_inc(*inv_a.inc("M1", n, g))

                stick_softplus(0)
                level(1)
                stick_softplus(1)
                level(2)
                stick_weights(0)
                stick_keep(0)
                stick_weights(1)
                stick_softplus(2)
                level(3)
                stick_keep(1)
                stick_softplus(3)
                stick_weights(2)
                level(4)
                stick_keep(2)
                stick_weights(3)
                level(5)
                stick_keep(3)
                level(6)
                for c in range(2):
                    act.wait_ge(*sol_p.at("rhs", c))
                    for n in range(2):
                        ins = nc.scalar.activation(rs[:, n], ps[:, 4 + n, 0:256].rearrange("p (a b) -> p a b", a=4), ACT.Copy)
                    ins.then_inc(*sol_a.inc("rhs", c))
                    act.wait_ge(*sol_p.at("u", c))
                    nc.scalar.activation(us[:].rearrange("p a b c -> p (a b c)"), ps[:, 6], ACT.Copy).then_inc(*sol_a.inc("u", c))
                    act.wait_ge(*sol_p.at("y", c))
                    for n in range(2):
                        dst = yv[:, c].rearrange("p (a b) e -> p b a e", b=2)[:, n]
                        ins = nc.scalar.activation(dst, ps[:, 4 + n, 0:256].rearrange("p (a b) -> p a b", a=4), ACT.Copy)
                    ins.then_inc(*sol_a.inc("y", c))
                act.wait_ge(*sol_d.at("centred"))
                nc.scalar.activation(ysq[:], yv[:], ACT.Square).then_inc(*sol_a.inc("squares"))

            def mla():
                norm("mla", "attn_norm1")
                act.wait_ge(*used_up_to(("down", 1)))
                nc.scalar.activation(ctok[:, :, 0:512], ps[:, 0:2], ACT.Copy)
                act.wait_ge(*used_up_to(("down", 2)))
                step(nc.scalar.activation(ctok[:, :, 512:672], ps[:, 2:4, 0:160], ACT.Copy))
                for t in range(TT):
                    nc.scalar.activation(mlsq[:, t, 0:384], ctok[:, t, 0:384], ACT.Square, accum_out=ssq[:, t:t + 1])
                    ins = nc.scalar.activation(mlsq[:, t, 384:640], ctok[:, t, 384:640], ACT.Square, accum_out=ssq[:, 2 + t:3 + t])
                ins.then_inc(*lat_a.inc("squares"))
                act.wait_ge(*lat_p.at("turned"))
                nc.scalar.activation(clT[:, 4], ps[:, 6, 0:SEQ], ACT.Copy, scale=col("kv_norm", 1)).then_inc(*lat_a.inc("kv"))
                keep_up(act, 0)
                for i in range(MH + LAG_V):
                    if i < MH and i % 2 == 0:
                        act.wait_ge(*mla_p.at("turned", i))
                        if i >= 3:
                            act.wait_ge(*mla_p.at("scores", i - 3))
                        nc.scalar.activation(qkT[0:QH, i % 3].rearrange("p a b -> p (a b)"), ps[0:QH, 4 + i % 2], ACT.Copy).then_inc(*mla_a.inc("turned", i))
                    hd = i - LAG_T
                    if 0 <= hd < MH:
                        act.wait_ge(*mla_p.at("probs", hd))
                        if hd >= 2:
                            act.wait_ge(*mla_p.at("out", hd - 2))
                        nc.scalar.activation(mpb[:, hd % 2], ps[:, hd % 2, 0:384], ACT.Copy).then_inc(*mla_a.inc("probs", hd))
                    hd = i - LAG_S
                    if 0 <= hd < MH:
                        act.wait_ge(*mla_d.at("minus_max", hd))
                        for n, c in enumerate((slice(0, 256), slice(256, 384))):
                            s = msc[:, hd % 6, c]
                            ins = nc.scalar.activation(s, s, ACT.Exp, bias=mmax[:, hd % 6, n:n + 1], scale=MSCALE, accum_out=mden[:, hd % 6, n:n + 1])
                        ins.then_inc(*mla_a.inc("exp", hd))
                    hd = i - LAG_V
                    if hd >= 0 and hd % 2:
                        act.wait_ge(*mla_p.at("out", hd))
                        nc.scalar.activation(moT[:, hd // 2], ps[:, 2 + hd // 2 % 2, 0:256], ACT.Copy).then_inc(*mla_a.inc("out", hd // 2))

            act.wait_ge(*cols_ready.at("cols"))
            if upto("ffn1"):
                norm("ffn1", "norm_ffn1")
                ffn("ffn1", False)
            act.wait_ge(*lb_d.at("logit"))
            nc.scalar.activation(lbc[:], lbd[:], ACT.Sigmoid).then_inc(*lb_a.inc("lb"))
            act.wait_ge(*bias_d.at("t"))
            act.dma_start(scratch, tabd[:].unsqueeze(1).to_broadcast([AH, P, 384])).then_inc(tab_out.sem, 16)
            act.wait_ge(tab_out.sem, 16)
            shifted = [bass.AP(tensor=scratch.tensor, offset=127 + o, ap=[[383, P], [384 * P, AH], [1, n]]) for o, n in ((0, 256), (P, P))]
            act.dma_start(bias[:, :, 0:256], shifted[0]).then_inc(bias_in.sem, 16)
            act.dma_start(bias[:, :, 256:384], shifted[1]).then_inc(bias_in.sem, 16)
            if upto("mix1"):
                norm("mix1", "norm_mix")
                mix1()
            if upto("ffn2"):
                norm("ffn2", "norm_ffn2")
                ffn("ffn2", False)
            if upto("ple1"):
                ple("ple1", "norm_ple", False)
            if upto("block1"):
                squares_of_h("block1")
            if upto("hyb"):
                hyb()
            act.wait_ge(*rot_d.at("angles"))
            nc.scalar.activation(cosv[:], cosv[:], ACT.Sin)
            nc.scalar.activation(sinv[:], sinv[:], ACT.Sin).then_inc(*rot_a.inc("rot"))
            if upto("conv0"):
                norm("conv0", "conv_norm0")
                ffn("conv0", True)
            if upto("ple20"):
                act.dma_start(row_gain[:, 0], I["ple_norm_2"][1].partition_broadcast(P)).then_inc(gains_in.sem, 16)
                ple("ple20", "ple_gate_norm0", True)
                act.wait_ge(*ple_d.at("ple20", "e"))
                act.wait_ge(gains_in.sem, 48)
                act.dma_start(row_gain[:, 1], I["final_norm_2"].partition_broadcast(P)).then_inc(gains_in.sem, 16)
            if upto("mla"):
                mla()
            if upto("conv1"):
                norm("conv1", "conv_norm1")
                ffn("conv1", True)
            if upto("ple21"):
                ple("ple21", "ple_gate_norm1", True)
            if upto("all"):
                squares_of_h("all")
            for t in range(TT):
                act.wait_ge(*h_ready.at("out", t))
                act.dma_start(out[0, t * P:(t + 1) * P, :], h[:, t]).then_inc(stored.sem, 16)
            act.wait_ge(stored.sem, 16 * TT)

        @block.gpsimd
        def _(pool):
            def step(ins):
                ins.then_inc(*pool_step.inc(pool_step.count))
                pool.wait_ge(*pool_step.last())

            nc.gpsimd.memset(stack[:], 0.0).then_inc(*zeros.inc("stack"))
            nc.gpsimd.memset(minus_half[:], -0.5).then_inc(*zeros.inc("half"))
            nc.gpsimd.memset(gpad[:, :, :, 0:2], 0.0).then_inc(*zeros.inc("gpad"))
            pool.wait_ge(*zeros.last())
            nc.gpsimd.memset(tab[N_BUCKETS:N_BUCKETS + 1, :], NEG).then_inc(*zeros.inc("tab"))
            pool.wait_ge(*zeros.last())
            nc.gpsimd.memset(ones[:], 1.0).then_inc(*zeros.inc("ones"))
            pool.wait_ge(*zeros.last())

            def power(n, width):
                pool.wait_ge(*mean_ready.at(n))
                nc.gpsimd.tensor_tensor(rstd[:, 0:width], msq[:, 0:width], minus_half[:, 0:width], ALU.pow).then_inc(*rstd_ready.inc(n))

            def mix1():
                pool.wait_ge(*mean_ready.at("mix1"))
                nc.gpsimd.memset(AT[:], 0.0).then_inc(*rec_g.inc("zero"))
                for n, m in enumerate(LV):
                    z = zT[:, n % 2].rearrange("p a s -> p (a s)").rearrange("p (b m) -> p b m", m=2 * m)
                    b = bT.rearrange("p a s -> p (a s)").rearrange("p (b m) -> p b m", m=2 * m)
                    mid = b[:, :, m - 1:m].to_broadcast([P, RH * SEQ // (2 * m), m])
                    if n == 0:
                        pool.wait_ge(*rec_d.at("sums"))
                    if n >= 2:
                        pool.wait_ge(*rec_p.at("scores", n - 1))
                    nc.gpsimd.tensor_tensor(z[:, :, 0:m], mid, b[:, :, 0:m], ALU.subtract)
                    nc.gpsimd.tensor_tensor(z[:, :, m:2 * m], b[:, :, m:2 * m], mid, ALU.subtract).then_inc(*rec_g.inc("differences", n))

            def power2(n):
                pool.wait_ge(*mean_ready.at(n, "e"))
                nc.gpsimd.tensor_tensor(rstd[:, 2:4], msq[:, 2:4], minus_half[:, 2:4], ALU.pow).then_inc(*rstd_ready.inc(n, "e"))

            def hyb():
                pool.wait_ge(*h_ready.at("hyb", 1))
                nc.gpsimd.memset(pfT[:, :, 0:1], 0.0).then_inc(*mix_g.inc("zero"))
                for key, tile, tiles, rows in MIXES:
                    pool.wait_ge(*rw_in.at(key))
                    t = slice(tile, tile + tiles)
                    nc.gpsimd.tensor_tensor(xm[0:rows, t], pfT[0:rows, t, 0:SEQ], pfT[0:rows, t, 1:], ALU.subtract).then_inc(*mix_g.inc(key))

                pool.wait_ge(*pre_d.at("bonus"))
                nc.gpsimd.memset(G[:].rearrange("p a b c d -> p (a b c d)"), 0.0).then_inc(*mix_g.inc("G"))

                def before(t, *event):
                    for n in range(2):
                        tiles = t[:, n].rearrange("p (b c) -> p b c", b=3)[:, 0::2, :]
                        ins = nc.gpsimd.affine_select(out=tiles, in_=tiles, compare_op=ALU.is_gt, fill=0.0, base=0,
                                                      pattern=[[0, 2], [1, P]], channel_multiplier=-1)
                    ins.then_inc(*stick_g.inc(*event))

                def softplus(g):
                    pool.wait_ge(*stick_d.at("softplus", g))
                    before(lsp[:, g % 2], "softplus", g)

                def weights(g):
                    pool.wait_ge(*stick_a.at("weights", g))
                    before(wst[:, g % 2], "weights", g)

                softplus(0)
                softplus(1)
                weights(0)
                weights(1)
                softplus(2)
                weights(2)
                softplus(3)
                weights(3)

            def mla():
                for hd in range(MH):
                    pool.wait_ge(*mla_d.at("inverse_sum", hd))
                    for n, c in enumerate((slice(0, 256), slice(256, 384))):
                        s = msc[:, hd % 6, c]
                        ins = nc.gpsimd.tensor_scalar(s, s, mden[:, hd % 6, n:n + 1], None, ALU.mult)
                    ins.then_inc(*mla_g.inc("probs", hd))

            if upto("ffn1"):
                power("ffn1", 2)
            pool.wait_ge(consts_in.sem, 16 * N_CONSTS)
            nc.gpsimd.tensor_copy(masks[:], mask_rows).then_inc(*masks_ready.inc())
            pool.wait_ge(*masks_ready.at())
            if upto("mix1"):
                power("mix1", 2)
                mix1()
                power("rec", 8)
            if upto("ffn2"):
                power("ffn2", 2)
            if upto("ple1"):
                power("ple1", 2)
            if upto("block1"):
                power("block1", 2)
            if upto("hyb"):
                power("hyb", 2)
                hyb()
                power("gn", 16)
            if upto("conv0"):
                power("conv0", 2)
            if upto("ple20"):
                power("ple20", 2)
                power2("ple20")
            if upto("mla"):
                power("mla", 2)
                power("latent", 4)
                mla()
            if upto("conv1"):
                power("conv1", 2)
            if upto("ple21"):
                power("ple21", 2)
                power2("ple21")
            if upto("all"):
                power("all", 2)

        @block.vector
        def _(dve):
            v = nc.vector

            def step(ins):
                ins.then_inc(*dve_step.inc(dve_step.count))
                dve.wait_ge(*dve_step.last())

            dve.wait_ge(*cols_turned.at("cols"))
            v.tensor_copy(cols[:], ps[:, 0, 0:3 * P]).then_inc(*cols_ready.inc("cols"))
            dve.wait_ge(*cols_turned.at("p"))
            v.tensor_copy(pT[:].rearrange("p n k s -> p n (k s)"), ps[:, 1:4]).then_inc(*cols_ready.inc("p"))
            dve.wait_ge(*cols_ready.at("p"))

            def norm(n, gain):
                dve.wait_ge(*squared.at(n, 1))
                v.tensor_scalar(msq[:, 0:2], ssq[:, 0:2], 1.0 / D, EPS, ALU.mult, ALU.add).then_inc(*mean_ready.inc(n))
                dve.wait_ge(*rstd_ready.at(n))
                v.tensor_scalar(hn[:, 0], h[:, 0], rstd[:, 0:1], None, ALU.mult).then_inc(*scaled_d.inc(n))
                for k in range(KD // 2):
                    if k % 2 == 0:
                        dve.wait_ge(*turned.at(n, k // 2))
                    ins = v.tensor_scalar(xT[:, k], ps[:, 4 + k // 2, k % 2 * SEQ:(k % 2 + 1) * SEQ], col(gain, k), None, ALU.mult)
                ins.then_inc(*x_d.inc(n))

            def residual(key, scale, after):
                for t in range(TT):
                    if t == 0:
                        dve.wait_ge(*acc_ready.at(key, 0))
                    else:
                        dve.wait_ge(*used_up_to(after))
                    for half in range(2):
                        part = h[:, t, half * 512:(half + 1) * 512]
                        ins = v.scalar_tensor_tensor(part, bank(2 * t + half), scale, part, ALU.mult, ALU.add)
                    ins.then_inc(*h_ready.inc(key_after(key), t))

            def ffn(f, conv):
                def group(g, i=None):
                    two = slice(4 + 2 * (g % 2), 6 + 2 * (g % 2))
                    s = g % 2
                    first, second = ps[:, two, 0:SEQ], ps[:, two, SEQ:2 * SEQ]
                    if g >= 2:
                        dve.wait_ge(*used_up_to((f, ffn_chunk("out", g - 2)), i))
                    dve.wait_ge(*gate_act.at_group(i, f, g))
                    if not conv:
                        v.tensor_tensor(gluT[:, s], first, gatev[:, s], ALU.mult).then_inc(*conv_out.inc(f, g))
                        dve.wait_ge(*conv_out.at_group(i, f, g))
                        v.tensor_tensor(hidT[:, s], gluT[:, s], second, ALU.mult).then_inc(*hid_ready.inc(f, g))
                        return
                    layer = f[-1]

                    def tap(name, j):
                        c = column[name] + 2 * g + j
                        return cols[:, c:c + 1] if i is None else cols[:, bass.ds(i * 4 + c, 1)]

                    for n, j in enumerate(range(2)):
                        v.tensor_scalar(glu2[:, s, j], gpad[:, s, j, 2:2 + SEQ], tap(f"conv_w{layer}2", j),
                                        tap(f"conv_b{layer}", j), ALU.mult, ALU.add).then_inc(*conv_out.inc(f, g, j, 0))
                    for j in range(2):
                        dve.wait_ge(*conv_out.at_group(i, f, g, j, 0))
                        v.scalar_tensor_tensor(gluT[:, s, j], gpad[:, s, j, 1:1 + SEQ], tap(f"conv_w{layer}1", j),
                                               glu2[:, s, j], ALU.mult, ALU.add).then_inc(*conv_out.inc(f, g, j, 1))
                    for j in range(2):
                        dve.wait_ge(*conv_out.at_group(i, f, g, j, 1))
                        ins = v.scalar_tensor_tensor(gluT[:, s, j], gpad[:, s, j, 0:SEQ], tap(f"conv_w{layer}0", j),
                                                     gluT[:, s, j], ALU.mult, ALU.add)
                    ins.then_inc(*conv_out.inc(f, g))
                    dve.wait_ge(*gate_act.at_group(i, f, g, "gelu"))
                    v.tensor_tensor(hidT[:, s], gatev[:, s], first, ALU.mult).then_inc(*hid_ready.inc(f, g))

                group(0)
                group(1)
                with dve.Fori(0, ROUNDS) as i:
                    since = [(s, s.count) for s in (conv_out, hid_ready)]
                    group(2, i)
                    group(3, i)
                    for s, c in since:
                        s.repeated(f, c, ROUNDS)
                group(GROUPS - 1)
                residual(f, 1.0 if conv else 0.5, (f, 3 * GROUPS - 1))

            def keep(dst, b, key, *event, c=slice(0, 512), scale=None):
                dve.wait_ge(*used_up_to(key))
                src = ps[:, b, c]
                if len(dst.shape) == 3:
                    src = src.rearrange("p (a b) -> p a b", a=dst.shape[1])
                if scale is None:
                    v.tensor_copy(dst, src).then_inc(*proj_d.inc(*event))
                else:
                    v.tensor_scalar(dst, src, scale, None, ALU.mult).then_inc(*proj_d.inc(*event))

            def mix1():
                dve.wait_ge(*masks_ready.at())
                for n in range(2):
                    dve.wait_ge(*proj_a.at("rf", n))
                    if n == 0:
                        dve.wait_ge(*lb_d.at("one_minus"))
                    for hd in (2 * n, 2 * n + 1):
                        ins = v.tensor_scalar(fT[:, hd], fT[:, hd], omlb[:, hd:hd + 1], lbc[:, hd:hd + 1], ALU.mult, ALU.add)
                ins.then_inc(*rec_d.inc("f"))
                for n in range(2):
                    keep(rqT[:, 2 * n:2 * n + 2], 2 + n, ("rq", n), "rq", n)
                dve.wait_ge(*rec_d.at("f"))
                v.tensor_scalar(kT[:], fT[:], -1.0, 1.0, ALU.mult, ALU.add).then_inc(*rec_d.inc("q_and_k"))
                dve.wait_ge(*rec_a.at("log"))
                dve.wait_ge(*zeros.at("ones"))
                dve.wait_ge(*rec_d.at("q_and_k"))
                for hd in range(RH):
                    ins = v.tensor_tensor_scan(fT[:, hd], ones[:], bT[:, hd], 0.0, ALU.mult, ALU.add)
                ins.then_inc(*rec_d.inc("scan"))
                for n in range(2):
                    keep(aqT[:, 2 * n:2 * n + 2], 2 + n, ("aq", n), "aq", n, scale=0.125)
                dve.wait_ge(*rec_d.at("scan"))
                v.tensor_copy(bT[:], fT[:]).then_inc(*rec_d.inc("sums"))
                dve.wait_ge(*used_up_to("akv"))
                v.tensor_copy(akT[:, 0], ps[:, 0, 0:SEQ]).then_inc(*proj_d.inc("akT"))
                keep(av[:], 0, "akv", "akv", c=slice(256, 512))
                dve.wait_ge(bias_in.sem, 32)
                for hd in range(AH):
                    dve.wait_ge(*att_p.at("scores", hd))
                    v.tensor_tensor(sc[:, hd], ps[:, 4 + hd % 4, 0:384], bias[:, hd], ALU.add).then_inc(*att_d.inc("biased", hd))
                    dve.wait_ge(*att_d.at("biased", hd))
                    v.tensor_reduce(mx[:, hd, 0:1], sc[:, hd, 0:256], AX.X, ALU.max)
                    ins = v.tensor_reduce(mx[:, hd, 1:2], sc[:, hd, 256:384], AX.X, ALU.max)
                step(ins)
                sink = sinkb[:].unsqueeze(2).to_broadcast([P, AH, 2])
                dve.wait_ge(consts_in.sem, 16 * N_CONSTS)
                step(v.tensor_tensor(mx[:], mx[:], sink, ALU.max))
                step(v.tensor_scalar(nmx[:], mx[:], -1.0, None, ALU.mult))
                v.tensor_tensor(esink[:], nmx[:], sink, ALU.add).then_inc(*att_d.inc("minus_max"))

                def place(n):
                    dve.wait_ge(*rec_p.at("scores", n))
                    b = 4 + n % 2 * 2
                    if n:
                        dve.wait_ge(*rec_d.at("placed", n - 1))
                    if n == len(LV):
                        v.tensor_copy(AT[:, 2], ps[:, b].rearrange("p (a b) -> p a b", a=RH)).then_inc(*rec_d.inc("placed", n))
                        return
                    if n == 0:
                        dve.wait_ge(*rec_g.at("zero"))
                    mask = masks[:, EYE if n == 0 else n - 1].unsqueeze(1).to_broadcast([P, RH, P])
                    for t in range(TT):
                        ins = v.copy_predicated(AT[:, t], mask, ps[:, b + t].rearrange("p (a b) -> p a b", a=RH))
                    ins.then_inc(*rec_d.inc("placed", n))

                for n, m in enumerate(LV):
                    dve.wait_ge(*rec_a.at("decay", n))
                    z, k, q = (t.rearrange("p a s -> p (a s)").rearrange("p (b m) -> p b m", m=2 * m) for t in (zT[:, n % 2], kT, rqT))
                    v.tensor_tensor(z[:, :, 0:m], z[:, :, 0:m], k[:, :, 0:m], ALU.mult)
                    v.tensor_tensor(z[:, :, m:2 * m], z[:, :, m:2 * m], q[:, :, m:2 * m], ALU.mult).then_inc(*rec_d.inc("decayed", n))
                    place(n)
                    if n == 3:
                        normalize_probs()
                place(len(LV))
                for t in range(TT):
                    dve.wait_ge(*rec_a.at("squares", t))
                    ins = v.tensor_reduce(ssq[:, 4 * t:4 * t + 4], osq[:, t].rearrange("p (a b) -> p a b", a=RH), AX.X, ALU.add)
                step(ins)
                v.tensor_scalar(msq[:, 0:8], ssq[:, 0:8], 1.0 / P, EPS, ALU.mult, ALU.add).then_inc(*mean_ready.inc("rec"))
                dve.wait_ge(*rstd_ready.at("rec"))
                for t in range(TT):
                    v.tensor_tensor(orec[:, t].rearrange("p (a b) -> p a b", a=RH), ps[:, 6 + t].rearrange("p (a b) -> p a b", a=RH),
                                    rstd[:, 4 * t:4 * t + 4].unsqueeze(2).to_broadcast([P, RH, P]), ALU.mult).then_inc(*rec_d.inc("normed", t))
                for j in range(4):
                    dve.wait_ge(*att_p.at("out", 2 * j + 1))
                    v.tensor_copy(attT[:, j], ps[:, j, 0:SEQ]).then_inc(*att_d.inc("outT", j))
                dve.wait_ge(*att_a.at("gate_r"))
                for n in range(2):
                    dve.wait_ge(*rec_p.at("turned", n))
                    v.scalar_tensor_tensor(recT[:, 2 * n:2 * n + 2], ps[:, 6 + n].rearrange("p (a b) -> p a b", a=2), col("rec_norm"),
                                           sgT[:, 2 * n:2 * n + 2], ALU.mult, ALU.mult).then_inc(*rec_d.inc("recT", n))
                dve.wait_ge(*att_a.at("gates"))
                for n in range(4):
                    dve.wait_ge(*(att_p.at("att_proj", n) if n < 3 else used_up_to(("att_proj", 1))))
                    ins = v.tensor_tensor(mT[:, 2 * n:2 * n + 2], ps[:, n].rearrange("p (a b) -> p a b", a=2), gT[:, 2 * n:2 * n + 2], ALU.mult)
                for n in range(4):
                    dve.wait_ge(*(att_p.at("rec_proj", n) if n < 3 else used_up_to(("rec_proj", 1))))
                    g = gT[:, 8 + 2 * n:10 + 2 * n]
                    step(v.tensor_tensor(g, ps[:, 4 + n].rearrange("p (a b) -> p a b", a=2), g, ALU.mult))
                    v.tensor_tensor(mT[:, 2 * n:2 * n + 2], mT[:, 2 * n:2 * n + 2], g, ALU.add).then_inc(*att_d.inc("merged", n))
                residual("mix1", 1.0, ("mix_out", 3))

            def normalize_probs():
                dve.wait_ge(*att_a.at("sink"))
                dve.wait_ge(*att_a.at("exp", AH - 1))
                step(v.tensor_tensor(den[:], den[:], esink[:], ALU.add))
                step(v.reciprocal(den[:], den[:]))
                for hd in range(AH):
                    for n, c in enumerate((slice(0, 256), slice(256, 384))):
                        ins = v.tensor_scalar(sc[:, hd, c], sc[:, hd, c], den[:, hd, n:n + 1], None, ALU.mult)
                    ins.then_inc(*att_d.inc("probs", hd))

            def ple(stage, gain, slot):
                norm(stage, gain)
                if slot is None:
                    dve.wait_ge(*used_up_to((f"{stage}_proj", 0)))
                else:
                    dve.wait_ge(*ple_a.at(stage, "squares"))
                    v.tensor_scalar(msq[:, 2:4], ssq[:, 2:4], 1.0 / D, EPS, ALU.mult, ALU.add).then_inc(*mean_ready.inc(stage, "e"))
                    dve.wait_ge(*rstd_ready.at(stage, "e"))
                    dve.wait_ge(gains_in.sem, 48 if stage == "ple21" else 32)
                    for t in range(TT):
                        ins = v.scalar_tensor_tensor(pemb[:, t], ps[:, 2 * t:2 * t + 2].rearrange("p a b -> p (a b)"), rstd[:, 2 + t:3 + t],
                                                     row_gain[:, slot], ALU.mult, ALU.mult)
                    ins.then_inc(*ple_d.inc(stage, "e"))
                    dve.wait_ge(*ple_d.at(stage, "e"))
                for t in range(TT):
                    dve.wait_ge(*ple_a.at(stage, t))
                    e = ps[:, 2 * t:2 * t + 2].rearrange("p a b -> p (a b)") if slot is None else pemb[:, t]
                    step(v.tensor_tensor(pgate[:, t], pgate[:, t], e, ALU.mult))
                    v.tensor_tensor(h[:, t], h[:, t], pgate[:, t], ALU.add).then_inc(*h_ready.inc(key_after(stage), t))

            def final_norm(n, slot, gains):
                dve.wait_ge(*squared.at(n, 1))
                v.tensor_scalar(msq[:, 0:2], ssq[:, 0:2], 1.0 / D, EPS, ALU.mult, ALU.add).then_inc(*mean_ready.inc(n))
                dve.wait_ge(*rstd_ready.at(n))
                dve.wait_ge(gains_in.sem, gains)
                for t in range(TT):
                    v.scalar_tensor_tensor(h[:, t], h[:, t], rstd[:, t:t + 1], row_gain[:, slot], ALU.mult, ALU.mult).then_inc(*h_ready.inc(key_after(n), t))

            def hyb():
                norm("hyb", "attn_norm0")

                def mix(key, tile, tiles, rows):
                    dve.wait_ge(*mix_g.at(key))
                    for j in range(tile, tile + tiles):
                        mu = col("mu", j) if j < 14 else col("mu_tail")
                        ins = v.scalar_tensor_tensor(xm[0:rows, j], xm[0:rows, j], mu[0:rows], pfT[0:rows, j, 1:], ALU.mult, ALU.add)
                    ins.then_inc(*mix_d.inc(key))

                def flat(t):
                    return t.rearrange("p a s -> p (a s)")

                for m in MIXES[:2]:
                    mix(*m)
                dve.wait_ge(*mix_d.last())
                for j in range(RWT):
                    ins = v.tensor_scalar(kk[:, j], xm[:, 4 + j], col("k_k", j), None, ALU.mult)
                step(ins)
                v.tensor_tensor(dm0[:], kk[:], kk[:], ALU.mult).then_inc(*pre_d.inc("kk_squares"))
                for m in MIXES[2:]:
                    mix(*m)
                dve.wait_ge(*pre_a.at("decay"))
                for j in range(RWT):
                    for c in range(2):
                        s = slice(c * P, (c + 1) * P)
                        ins = v.tensor_tensor_scan(cc[:, j, s], ones[:, 0:P], lw[:, j, s], 0.0, ALU.mult, ALU.add)
                step(ins)
                c3, d3 = (t.rearrange("p a (c s) -> p (a c) s", c=2) for t in (cc, dm))
                step(v.tensor_tensor(d3, c3, c3[:, :, 63:64].to_broadcast([P, 8, P]), ALU.subtract))
                v.tensor_tensor(sfac[:], dm[:, :, P - 1:P].rearrange("p a b -> p (a b)"), cc[:, :, P + 63:P + 64].rearrange("p a b -> p (a b)"), ALU.add)
                dve.wait_ge(*pre_p.at("kk_sums"))
                v.tensor_scalar(ktmp[:], ps[:, 4:6].rearrange("p b (a s) -> p (b a) s", a=2), 1e-24, None, ALU.max).then_inc(*pre_d.inc("kk_sums"))
                v.tensor_tensor(dm0[:], dm[:], lw[:], ALU.subtract).then_inc(*pre_d.inc("dm"))
                dve.wait_ge(*pre_a.at("kk_norm"))
                step(v.reciprocal(ktmp[:], ktmp[:]))
                v.tensor_tensor(kk[:], kk[:], ktmp[:], ALU.mult).then_inc(*pre_d.inc("kk_norm"))
                dve.wait_ge(*pre_a.at("rate"))
                dve.wait_ge(*pre_d.at("kk_norm"))
                for j in range(RWT):
                    v.tensor_scalar(ktmp[:, j], aT[:, j], 1.0, col("k_a", j), ALU.subtract, ALU.mult)
                step(v.scalar_tensor_tensor(flat(Bk), flat(kk), -1.0, flat(aT), ALU.mult, ALU.mult))
                step(v.scalar_tensor_tensor(xm[:, 4:8], ktmp[:], 1.0, xm[:, 4:8], ALU.add, ALU.mult))
                dve.wait_ge(*pre_a.at("exps"))
                ar = AR.rearrange("p a c n s -> p (a c) n s")
                two = lambda t: t.rearrange("p a (c s) -> p (a c) s", c=2)
                v.tensor_tensor(ar[:, :, 0], two(kk), two(dm0), ALU.mult)
                step(v.tensor_tensor(ar[:, :, 1], two(xm[:, 0:4]), two(dm), ALU.mult))
                for j in range(RWT):
                    ins = v.scalar_tensor_tensor(xm[:, j], xm[:, j], col("r_k", j), xm[:, 4 + j], ALU.mult, ALU.mult)
                ins.then_inc(*pre_d.inc("bonus_terms"))
                v.tensor_tensor(Bk[:], Bk[:], cc[:], ALU.mult)
                v.tensor_tensor(Kk[:], xm[:, 4:8], cc[:], ALU.mult).then_inc(*pre_d.inc("bk"))
                dve.wait_ge(*pre_p.at("bonus"))
                dve.wait_ge(*pre_d.at("bk"))
                v.tensor_tensor(bonus[:], ps[:, 4:6].rearrange("p b (a s) -> p (b a) s", a=2), xm[:, 8:12], ALU.mult).then_inc(*pre_d.inc("bonus"))
                dve.wait_ge(*mix_g.at("G"))
                two_masks = masks[:, BEFORE:UPTO + 1].rearrange("p a b -> p (a b)").unsqueeze(1).to_broadcast([P, 2, 2 * P])
                for n in range(16):
                    dve.wait_ge(*inv_p.at("scores", n))
                    v.copy_predicated(G[:, n // 8, n % 8].rearrange("p (a b) c -> p a (b c)", a=2), two_masks,
                                      ps[:, n % 4].rearrange("p (a b) -> p a b", a=2)).then_inc(*inv_d.inc("scores", n))

                def stick_softplus(g):
                    dve.wait_ge(*stick_a.at("log", g))
                    s = lsp[:, g % 2]
                    v.scalar_tensor_tensor(s, ps[:, 4 + 2 * (g % 2):6 + 2 * (g % 2), 0:384], 0.0, s, ALU.max, ALU.add).then_inc(*stick_d.inc("softplus", g))

                def level(n):
                    mask = masks[:, n].unsqueeze(1).to_broadcast([P, 4, P])
                    if n == 0:
                        dve.wait_ge(*inv_d.at("scores", 15))
                        step(v.tensor_copy(Y[:].rearrange("p a b c -> p (a b) c"), ident.unsqueeze(1).to_broadcast([P, 16, P])))
                    for g in range(4):
                        if n == 0:
                            data = G[:, g // 2, g % 2 * 4:g % 2 * 4 + 4, 0]
                        else:
                            dve.wait_ge(*inv_p.at("Y", n, g))
                            data = ps[:, g].rearrange("p (a b) -> p a b", a=4)
                        v.copy_predicated(Y[:, g], mask, data).then_inc(*inv_d.inc("Y", n, g))
                    if n < LEVEL_N - 1:
                        for g in range(4):
                            dve.wait_ge(*inv_p.at("X", n, g))
                            v.tensor_copy(X[:, g], ps[:, g].rearrange("p (a b) -> p a b", a=4)).then_inc(*inv_d.inc("X", n, g))

                level(0)
                stick_softplus(0)
                level(1)
                stick_softplus(1)
                level(2)
                stick_softplus(2)
                level(3)
                stick_softplus(3)
                level(4)
                level(5)
                level(6)
                dve.wait_ge(*sol_p.at("state"))
                dve.wait_ge(*pre_a.at("exps"))
                v.tensor_tensor(s0[:], ps[:, 7, 0:256].rearrange("p (a b) -> p a b", a=4), sfac[:].unsqueeze(2).to_broadcast([P, 4, 64]),
                                ALU.mult).then_inc(*sol_d.inc("state"))
                y16, q16 = yv.rearrange("p c a b -> p (c a) b"), ysq.rearrange("p c a b -> p (c a) b")
                dve.wait_ge(*sol_a.at("y", 0))
                dve.wait_ge(*sol_a.at("y", 1))
                step(v.tensor_reduce(gmean[:], y16, AX.X, ALU.add))
                step(v.tensor_scalar(gmean[:], gmean[:], 1.0 / 64, None, ALU.mult))
                v.tensor_tensor(y16, y16, gmean[:].unsqueeze(2).to_broadcast([P, 16, 64]), ALU.subtract).then_inc(*sol_d.inc("centred"))
                dve.wait_ge(*sol_a.at("squares"))
                step(v.tensor_reduce(ssq[:], q16, AX.X, ALU.add))
                v.tensor_scalar(msq[:], ssq[:], 1.0 / 64, 64e-5, ALU.mult, ALU.add).then_inc(*mean_ready.inc("gn"))
                dve.wait_ge(*rstd_ready.at("gn"))
                v.tensor_tensor(y16, y16, rstd[:].unsqueeze(2).to_broadcast([P, 16, 64]), ALU.mult).then_inc(*sol_d.inc("normed"))
                dve.wait_ge(*sol_p.at("turned"))
                for j in range(RWT):
                    ins = v.tensor_scalar(obT[:, j], ps[:, 4 + j // 2, j % 2 * SEQ:(j % 2 + 1) * SEQ], col("ln_w", j), col("ln_b", j), ALU.mult, ALU.add)
                step(ins)
                step(v.tensor_tensor(obT[:], obT[:], bonus[:], ALU.add))
                dve.wait_ge(*used.at("g2"))
                v.tensor_tensor(obT[:], obT[:], ps[:, 6:8].rearrange("p b (a s) -> p (b a) s", a=2), ALU.mult).then_inc(*sol_d.inc("ob"))
                residual("hyb", 1.0, ("hyb_out", 3))

            def rotary_angles():
                two_pi = 2 * np.pi
                c1 = 6.28125
                c2 = float(np.float32(np.round((two_pi - c1) * 2.0 ** 20) / 2.0 ** 20))
                c3 = float(two_pi - c1 - c2)
                magic = 1.5 * 2.0 ** 23
                dve.wait_ge(rot_in.sem, 32)
                step(v.tensor_copy(posf[:], posi[:]))
                for t in range(TT):
                    ins = v.tensor_scalar(ang[:, t], freq[:], posf[:, t:t + 1], None, ALU.mult)
                step(ins)
                step(v.tensor_scalar(turns[:], ang[:], float(1 / two_pi), magic, ALU.mult, ALU.add))
                step(v.tensor_scalar(turns[:], turns[:], magic, None, ALU.subtract))
                for c in (c1, c2, c3):
                    step(v.scalar_tensor_tensor(ang[:], turns[:], -c, ang[:], ALU.mult, ALU.add))
                step(v.tensor_scalar(sinv[:], ang[:], 3.1415925, -3.1415925, ALU.min, ALU.max))
                step(v.tensor_scalar(turns[:], sinv[:], -1.0, None, ALU.mult))
                step(v.tensor_tensor(turns[:], turns[:], sinv[:], ALU.max))
                v.tensor_scalar(cosv[:], turns[:], -1.0, float(np.pi / 2), ALU.mult, ALU.add).then_inc(*rot_d.inc("angles"))

            def rotate(x, shape, c, s):
                n = int(np.prod(shape[1:]))
                view = lambda k: (rt[:, k, 0:n].rearrange("p (a b c) -> p a b c", a=shape[1], b=shape[2]) if len(shape) == 4
                                  else rt[:, k, 0:n].rearrange("p (a b) -> p a b", a=shape[1]))
                x1, x2 = x[..., 0:16], x[..., 16:32]
                v.tensor_tensor(view(0), x1, c, ALU.mult)
                v.tensor_tensor(view(1), x2, s, ALU.mult)
                v.tensor_tensor(view(2), x1, s, ALU.mult)
                step(v.tensor_tensor(view(3), x2, c, ALU.mult))
                v.tensor_tensor(x1, view(0), view(1), ALU.subtract)
                return v.tensor_tensor(x2, view(2), view(3), ALU.add)

            def mla():
                norm("mla", "attn_norm1")
                dve.wait_ge(*lat_a.at("squares"))
                v.tensor_scalar(msq[:, 0:2], ssq[:, 0:2], 1.0 / 384, EPS, ALU.mult, ALU.add)
                v.tensor_scalar(msq[:, 2:4], ssq[:, 2:4], 1.0 / 256, EPS, ALU.mult, ALU.add).then_inc(*mean_ready.inc("latent"))
                dve.wait_ge(*rstd_ready.at("latent"))
                for t in range(TT):
                    v.tensor_scalar(ctok[:, t, 0:384], ctok[:, t, 0:384], rstd[:, t:t + 1], None, ALU.mult)
                    ins = v.tensor_scalar(ctok[:, t, 384:640], ctok[:, t, 384:640], rstd[:, 2 + t:3 + t], None, ALU.mult)
                ins.then_inc(*lat_d.inc("scaled"))
                dve.wait_ge(*rot_a.at("rot"))
                step(rotate(ctok[:, :, 640:672], [P, TT, 16], cosv[:], sinv[:]))
                v.tensor_copy(ktok2[:, :, :, 64:96], ctok[:, :, 640:672].unsqueeze(2).to_broadcast([P, TT, MH, 32])).then_inc(*lat_d.inc("rotary_key"))
                dve.wait_ge(*lat_p.at("turned"))
                for j in range(4):
                    gain = col("q_norm", j) if j < 3 else col("kv_norm", 0)
                    ins = v.tensor_scalar(clT[:, j], ps[:, 4 + j // 2, j % 2 * SEQ:(j % 2 + 1) * SEQ], gain, None, ALU.mult)
                ins.then_inc(*lat_d.inc("q"))
                keep_up(dve, 1)
                dve.wait_ge(*up_a.at("q", 2, 0))
                dve.wait_ge(*up_d.at("q", 2, 1))
                cs, sn = (t.unsqueeze(2).to_broadcast([P, TT, MH, 16]) for t in (cosv[:], sinv[:]))
                rotate(qtok[:, :, :, 64:96], [P, TT, MH, 16], cs, sn).then_inc(*mla_d.inc("rotated"))
                mask = mats[:, 2].unsqueeze(1).to_broadcast([P, 2, P])
                for i in range(MH + 2):
                    if i < MH and i % 2:
                        dve.wait_ge(*mla_p.at("turned", i))
                        if i >= 3:
                            dve.wait_ge(*mla_p.at("scores", i - 3))
                        v.tensor_copy(qkT[0:QH, i % 3].rearrange("p a b -> p (a b)"), ps[0:QH, 4 + i % 2]).then_inc(*mla_d.inc("turned", i))
                    hd = i - LAG_S
                    if 0 <= hd < MH:
                        s, b = msc[:, hd % 6], 6 + hd % 2
                        dve.wait_ge(*mla_p.at("scores", hd))
                        if hd >= 6:
                            dve.wait_ge(*mla_p.at("probs", hd - 6))
                        v.tensor_copy(s[:, 0:P], ps[:, b, 0:P])
                        v.tensor_tensor(s[:, P:3 * P].rearrange("p (a b) -> p a b", a=2), ps[:, b, P:3 * P].rearrange("p (a b) -> p a b", a=2), mask,
                                        ALU.add).then_inc(*mla_d.inc("masked", hd))
                        dve.wait_ge(*mla_d.at("masked", hd))
                        v.tensor_reduce(mmax[:, hd % 6, 0:1], s[:, 0:256], AX.X, ALU.max)
                        step(v.tensor_reduce(mmax[:, hd % 6, 1:2], s[:, 256:384], AX.X, ALU.max))
                        v.tensor_scalar(mmax[:, hd % 6], mmax[:, hd % 6], -MSCALE, None, ALU.mult).then_inc(*mla_d.inc("minus_max", hd))
                    hd = i - 2
                    if 0 <= hd < MH:
                        dve.wait_ge(*mla_a.at("exp", hd))
                        v.reciprocal(mden[:, hd % 6], mden[:, hd % 6]).then_inc(*mla_d.inc("inverse_sum", hd))
                residual("mla", 1.0, ("mla_o", 3))

            if upto("ffn1"):
                norm("ffn1", "norm_ffn1")
                ffn("ffn1", False)
            v.tensor_tensor(lbd[:], cols[:, column["lb0"]:column["lb0"] + RH], cols[:, column["lb1"]:column["lb1"] + RH], ALU.subtract).then_inc(*lb_d.inc("logit"))
            dve.wait_ge(*bias_p.at("t"))
            v.tensor_copy(tabd[:], ps[0:AH, 7, 0:384]).then_inc(*bias_d.inc("t"))
            dve.wait_ge(*lb_a.at("lb"))
            v.tensor_scalar(omlb[:], lbc[:], -1.0, 1.0, ALU.mult, ALU.add).then_inc(*lb_d.inc("one_minus"))
            if upto("mix1"):
                norm("mix1", "norm_mix")
                mix1()
            if upto("ffn2"):
                norm("ffn2", "norm_ffn2")
                ffn("ffn2", False)
            if upto("ple1"):
                ple("ple1", "norm_ple", None)
            if upto("block1"):
                final_norm("block1", 0, 32)
            if upto("hyb"):
                hyb()
            rotary_angles()
            if upto("conv0"):
                norm("conv0", "conv_norm0")
                ffn("conv0", True)
            if upto("ple20"):
                ple("ple20", "ple_gate_norm0", 1)
            if upto("mla"):
                mla()
            if upto("conv1"):
                norm("conv1", "conv_norm1")
                ffn("conv1", True)
            if upto("ple21"):
                ple("ple21", "ple_gate_norm1", 0)
            if upto("all"):
                final_norm("all", 1, 64)

    return new


def key_after(key):
    if key == LAST or LAST == "all" and key == "all":
        return "out"
    return STAGES[STAGES.index(key) + 1]


ARENA = 27392
N_CONSTS = 6


def kernel(**inputs):
    import concourse.bacc as bacc
    from concourse.bass_utils import run_bass_kernel_spmd

    arrays = {name: np.ascontiguousarray(a) for name, a in inputs.items()}
    arrays.update(host_constants())

    def program(book):
        nc = bacc.Bacc("TRN2", target_bir_lowering=False, num_devices=1)
        aps = {name: nc.dram_tensor(f"in_{name}", a.shape, mybir.dt.from_np(a.dtype), kind="ExternalInput").ap()
               for name, a in arrays.items()}
        scratch = nc.dram_tensor("bias_by_distance", (8, P, 384), F32, kind="Internal").ap()
        out = nc.dram_tensor("out", (1, SEQ, D), F32, kind="ExternalOutput").ap()
        return nc, build(nc, aps, scratch, out, book)

    _, book = program({})
    nc, _ = program(book)
    r = run_bass_kernel_spmd(nc, [{f"in_{n}": a for n, a in arrays.items()}], core_ids=[0])
    return r.results[0]["out"]
```

```python
from contextlib import ExitStack

import numpy as np

import concourse.bass as bass
from concourse import mybir

F32 = mybir.dt.float32
F32R = mybir.dt.float32r
I32 = mybir.dt.int32
U8 = mybir.dt.uint8
ALU = mybir.AluOpType
ACT = mybir.ActivationFunctionType
AX = mybir.AxisListType

P = 128
SEQ = 256
TT = SEQ // P
D = 1024
KD = D // P
F = 2816
KF = F // P
GROUPS = KF // 2
BAY = 2048
BAYS = 6
HI_BAYS = 3
EPS = 1e-6
NEG = -1e30


class Signal:

    def __init__(self, ctx, nc, name, book, new):
        self.sem = ctx.enter_context(nc.semaphore(name))
        self.name, self.book, self.new, self.count = name, book, new, 0

    def inc(self, *event, by=1):
        self.count += by
        assert (self.name, event) not in self.new, (self.name, event)
        self.new[self.name, event] = self.count
        return self.sem, by

    def at(self, *event):
        if self.book:
            return self.sem, self.book[self.name, event]
        return self.sem, 1

    def last(self):
        return self.sem, self.count

    def repeated(self, loop, since, times):
        per = self.count - since
        self.new[self.name, ("per", loop)] = per
        self.count = since + per * times

    def at_group(self, i, f, g, *event):
        if not self.book:
            return self.sem, 1
        first = g if g < 4 or g == GROUPS - 1 else 2 + g % 2
        per = self.book[self.name, ("per", f)]
        value = self.book[self.name, (f, first, *event)] + (g - first) // 2 * per
        return self.sem, value if i is None else i * per + value


W_BLOCK, N_BUCKETS, MAX_DIST = 128, 32, 128
LEVELS = [1, 2, 4, 8, 16, 32, 64]
N_MASKS = 2 * len(LEVELS) + 3
EYE, BEFORE, UPTO = 2 * len(LEVELS), 2 * len(LEVELS) + 1, 2 * len(LEVELS) + 2


def host_constants():
    r, c = np.arange(P)[:, None], np.arange(P)[None, :]
    masks = np.zeros((P, N_MASKS, P), np.float32)
    for n, m in enumerate(LEVELS):
        pair = (r // (2 * m) == c // (2 * m)) & (r % (2 * m) < m) & (c % (2 * m) >= m)
        masks[:, n] = pair
        masks[:, len(LEVELS) + n] = pair.T
    masks[:, EYE] = r == c
    masks[:, BEFORE] = r < c
    masks[:, UPTO] = r <= c
    mats = np.zeros((P, 5, P), np.float32)
    mats[:, 0] = r == c
    mats[:, 1] = r // 64 == c // 64
    mats[:, 2] = np.where(c <= r, 0.0, NEG)
    mats[:, 3] = -1.0 * (r >= c)
    mats[:, 4] = -1.0
    dist = 255 - np.arange(383)
    n = np.maximum(dist, 0)
    exact = N_BUCKETS // 2
    large = exact + (np.log(np.maximum(n, 1) / exact) / np.log(MAX_DIST / exact)
                     * (N_BUCKETS - exact)).astype(np.int32)
    bucket = np.where(n < exact, n, np.minimum(large, N_BUCKETS - 1))
    hot = np.zeros((N_BUCKETS + 1, 384), np.float32)
    inside = (dist >= 0) & (dist < W_BLOCK)
    hot[bucket[inside], np.nonzero(inside)[0]] = 1.0
    hot[N_BUCKETS, :383][~inside] = 1.0
    freq = (10000.0 ** (-np.arange(16) / 16)).astype(np.float32)
    return {"masks": masks, "mats": mats, "hot": hot, "freq": freq}


ARENA = 27392
N_CONSTS = 5
FFN_BEFORE = {"ple1": "ffn2", "ple20": "conv0", "ple21": "conv1"}
STAGES = ["ffn1", "mix1", "ffn2", "ple1", "block1", "hyb", "conv0", "ple20", "mla", "conv1", "ple21", "all"]
SPLIT = ("ffn1", "ffn2", "ple1", "conv0", "ple20", "conv1", "ple21")


def ktiles(w):
    return w.rearrange("(t p) n -> p t n", p=P)


def build(nc, I, scratch, out, book):
    new = {}
    ctx = ExitStack()
    with ctx:
        def sb(name, shape, dt=F32):
            return ctx.enter_context(nc.sbuf_tensor(name, shape, dt))

        def signal(name):
            return Signal(ctx, nc, name, book, new)

        bay = sb("weight_bays", [P, BAYS, BAY])
        bay_lo = nc.alloc_sbuf_tensor_at("weights_second_parts", [P, BAYS, BAY], F32R, offset=nc.sbuf_base - 4 * BAYS * BAY)
        h = sb("h", [P, TT, D])
        hn = sb("h_scaled", [P, TT, D])
        xT = sb("xT", [P, KD, SEQ])
        gpad = sb("conv_input", [P, 2, 2, SEQ + 2])
        cols = sb("vector_columns", [P, 3 * P])
        first_gains = sb("first_gains", [P, KD])
        mats = sb("mats", [P, 5, P])
        masks = sb("masks", [P, N_MASKS, P], U8)
        pT = sb("pT", [P, 3, 2, SEQ])
        ssq = sb("square_sums", [P, 16])
        msq = sb("mean_squares", [P, 16])
        rstd = sb("rstd", [P, 16])
        minus_half = sb("minus_half", [P, 16])
        row_gain = sb("row_gains", [P, 2, D])
        arena = sb("arena", [P, ARENA])
        arena_byte = nc.sbuf_base - 4 * ARENA

        def carve_split(at, name, *shape):
            end = at + int(np.prod(shape))
            assert end <= ARENA, end
            return nc.alloc_sbuf_tensor_at(name, [P, *shape], F32R, offset=arena_byte + 4 * at), end

        def carve(at, *shape):
            end = at + int(np.prod(shape))
            assert end <= ARENA, end
            view = arena[:, at:end]
            names = "abcd"[:len(shape)]
            if len(shape) > 1:
                view = view.rearrange(f"p ({' '.join(names)}) -> p {' '.join(names)}", **dict(zip(names, shape)))
            return view, end

        hidT, at = carve(0, 2, 2, SEQ)
        gatev, at = carve(at, 2, 2, SEQ)
        gluT, at = carve(at, 2, 2, SEQ)
        glu2, at = carve(at, 2, 2, SEQ)
        stack, start_at = carve(at, 3, P)
        pin, start_at = carve(start_at, 3, TT, 256)
        mask_rows, start_at = carve(start_at, N_MASKS, P)
        first_rows, start_at = carve(start_at, P)
        first_rows = first_rows[0:KD]
        split_at = 10240
        w_hi, split_at = carve_split(split_at, "weights_first_parts", HI_BAYS, BAY)
        x_hi, split_at = carve_split(split_at, "x_first_part", KD, SEQ)
        x_lo, split_at = carve_split(split_at, "x_second_part", KD, SEQ)
        hid_hi, split_at = carve_split(split_at, "hidden_first_part", 2, 2, SEQ)
        hid_lo, split_at = carve_split(split_at, "hidden_second_part", 2, 2, SEQ)
        ident = mats[:, 0]
        ps = ctx.enter_context(nc.psum_tensor("ps", [P, 8, 512], F32))

        column, vectors = {}, []
        rows = 0
        for name, ap in [
            ("norm_mix", I["norm_mix"][0]),
            ("norm_ffn2", I["norm_ffn2"][0]), ("norm_ple", I["norm_ple"][0]),
            ("lb0", I["lb_param"][0]), ("lb1", I["lb_param"][1]), ("rec_norm", I["rec_norm"][0]),
            ("attn_norm0", I["attn_norm_2"][0]), ("attn_norm1", I["attn_norm_2"][1]),
            ("conv_norm0", I["ffn_norm_2"][0]), ("conv_norm1", I["ffn_norm_2"][1]),
            ("ple_gate_norm0", I["ple_gate_norm_2"][0]), ("ple_gate_norm1", I["ple_gate_norm_2"][1]),
            *[(f"conv_w{i}{k}", I["ffn_conv_w_2"][i, k]) for i in range(2) for k in range(3)],
            *[(f"conv_b{i}", I["ffn_conv_b_2"][i]) for i in range(2)],
            ("mu", I["rw_mu_2"][0, 0:14 * P]), ("mu_tail", I["rw_mu_2"][0, 14 * P:]),
            ("w0", I["rw_w0_2"][0]), ("a0", I["rw_a0_2"][0]), ("k_k", I["rw_k_k_2"][0]),
            ("k_a", I["rw_k_a_2"][0]), ("r_k", I["rw_r_k_2"][0].rearrange("h e -> (h e)")),
            ("ln_w", I["rw_ln_w_2"][0]), ("ln_b", I["rw_ln_b_2"][0]),
            ("q_norm", I["mla_q_norm_2"][0]), ("kv_norm", I["mla_kv_norm_2"][0]),
        ]:
            n = ap.shape[0]
            column[name] = rows
            c = min(n, P)
            src = ap.rearrange("(r c) -> r c", c=c)
            done = 0
            while done < n // c:
                k = min(n // c - done, P - rows % P)
                vectors.append((stack[rows % P:rows % P + k, rows // P, 0:c], src[done:done + k]))
                rows, done = rows + k, done + k
        assert rows <= 3 * P

        def col(name, j=0):
            if name == "norm_ffn1":
                return first_gains[:, j:j + 1]
            return cols[:, column[name] + j:column[name] + j + 1]

        chunks, plan = {}, []

        def chunk(key, view, rows=slice(0, P)):
            chunks[key] = len(chunks)
            plan.append(("chunk", key, view, rows))

        def columns_chunk(key, w, c0, width=256):
            k = w.shape[0] // P
            chunk(key, (0, [k, width], ktiles(w)[:, :, c0:c0 + width]))

        def rows_chunks(key, w):
            for k in range(w.shape[0] // (2 * P)):
                chunk((key, k), (0, [2, D], ktiles(w)[:, 2 * k:2 * k + 2, :]))

        def ffn_chunks(f, w1, w2):
            first = len(chunks)
            plan.append(("ffn", f, ktiles(w1), ktiles(w2)))
            for n in range(3 * GROUPS):
                chunks[f, n] = first + n

        ffn_chunks("ffn1", I["w_ffn1_in"][0], I["w_ffn1_out"][0])
        w = I["w_in"][0]
        for n in range(2):
            columns_chunk(("rf", n), w, 1280 + 256 * n)
        for n in range(2):
            columns_chunk(("rq", n), w, 768 + 256 * n)
        for n in range(2):
            columns_chunk(("ri", n), w, 1792 + 256 * n)
        for n in range(2):
            columns_chunk(("aq", n), w, 256 * n)
        columns_chunk("akv", w, 512)
        for n in range(2):
            columns_chunk(("rg", n), w, 2304 + 256 * n)
        for n in range(8):
            columns_chunk(("g", n), w, 2816 + 256 * n)
        rows_chunks("att_proj", I["w_att_proj"][0])
        rows_chunks("rec_proj", I["w_rec_proj"][0])
        rows_chunks("mix_out", I["w_out"][0])
        ffn_chunks("ffn2", I["w_ffn2_in"][0], I["w_ffn2_out"][0])
        rows_chunks("ple1_proj", I["w_ple_proj"][0])
        rows_chunks("ple1_gate", I["w_ple_gate"][0])
        w = I["hyb_w_in_2"][0]
        R0 = 1536
        for name, c0 in (("wk", R0 + 512), ("wr", R0)):
            for n in range(2):
                columns_chunk((name, n), w, c0 + 256 * n)
        columns_chunk("lora_in", w, R0 + 1536)
        columns_chunk("lora_in_tail", w, R0 + 1792, 32)
        for n in range(2):
            columns_chunk(("wv", n), w, R0 + 1024 + 256 * n)
        columns_chunk(("sq", 0), w, 0)
        chunk("w2", (0, [1, 512], I["rw_w2_2"][0]), slice(0, 64))
        chunk("a2", (0, [1, 512], I["rw_a2_2"][0]), slice(64, P))
        columns_chunk(("sq", 1), w, 256)
        for n in range(2):
            columns_chunk(("sk", n), w, 512 + 256 * n)
        for n in range(2):
            columns_chunk(("sv", n), w, 1024 + 256 * n)
        chunk("g2", (0, [1, 512], I["rw_g2_2"][0, 0:P]))
        chunk("g2_tail", (0, [1, 512], I["rw_g2_2"][0, P:]), slice(0, 32))
        rows_chunks("hyb_out", I["hyb_w_out_2"][0])

        def ple_chunks(i):
            rows_chunks(f"ple2{i}_proj", I["ple_w_proj_2"][i])
            rows_chunks(f"ple2{i}_gate", I["ple_w_gate_2"][i])

        ffn_chunks("conv0", I["ffn_w_in_2"][0], I["ffn_w_out_2"][0])
        ple_chunks(0)
        w = I["mla_w_down_2"][0]
        for n in range(3):
            columns_chunk(("down", n), w, 256 * n, min(256, 672 - 256 * n))
        for n in range(3):
            columns_chunk(("uq", n), I["mla_w_uq_2"][0], 512 * n, 512)
        for n in range(2):
            columns_chunk(("ukv", n), I["mla_w_ukv_2"][0], 1024 * n, 1024)
        rows_chunks("mla_o", I["mla_w_o_2"][0])
        ffn_chunks("conv1", I["ffn_w_in_2"][1], I["ffn_w_out_2"][1])
        ple_chunks(1)

        landed = [signal(f"weights_landed{b}") for b in range(BAYS)]
        used = signal("weights_used")
        x_in = signal("x_in")
        consts_in = signal("constants_in")
        mats_in = signal("mats_in")
        first_in = signal("first_gains_in")
        vectors_in = signal("vectors_in")
        masks_ready = signal("masks_ready")
        zeros = signal("zeros_written")
        cols_turned = signal("vectors_transposed")
        cols_ready = signal("vector_columns_ready")
        dve_step = signal("vector_step")
        act_step = signal("scalar_step")
        pool_step = signal("gpsimd_step")
        h_ready = signal("h_ready")
        squared = signal("squares_summed")
        mean_ready = signal("mean_squares_ready")
        rstd_ready = signal("rstd_ready")
        scaled_d = signal("scaled_by_vector")
        scaled_a = signal("scaled_by_scalar")
        turned = signal("h_transposed")
        x_d = signal("xT_by_vector")
        x_a = signal("xT_by_scalar")
        gate_act = signal("gate_activated")
        conv_out = signal("conv_ready")
        hid_ready = signal("hidden_ready")
        hid_hi_ready = signal("hidden_first_part_ready")
        hid_lo_ready = signal("hidden_second_part_ready")
        w_hi_ready = signal("weights_first_part_ready")
        w_lo_g = signal("weights_second_part_by_gpsimd")
        w_lo_d = signal("weights_second_part_by_vector")
        x_hi_d = signal("x_first_part_by_vector")
        x_hi_a = signal("x_first_part_by_scalar")
        x_lo_d = signal("x_second_part_by_vector")
        acc_ready = signal("projection_ready")
        stored = signal("output_stored")
        RH, LV = 4, LEVELS + [P]
        AH = 8
        rqT, at = carve(0, RH, SEQ)
        kT, at = carve(at, RH, SEQ)
        fT, at = carve(at, RH, SEQ)
        bT, at = carve(at, RH, SEQ)
        vR, at = carve(at, TT, 512)
        zT, at = carve(at, 2, RH, SEQ)
        orec, _ = carve(at - 2 * RH * SEQ, TT, 512)
        osq, _ = carve(at - RH * SEQ, TT, 512)
        AT, at = carve(at, 3, RH, P)
        sgT, at = carve(at, RH, SEQ)
        gT, at = carve(at, 16, SEQ)
        attT, at = carve(at, 4, SEQ)
        recT, at = carve(at, 4, SEQ)
        aqT, at = carve(at, 4, SEQ)
        akT, at = carve(at, 2, SEQ)
        av, at = carve(at, TT, P)
        sc, at = carve(at, AH, 384)
        pbT, at = carve(at, 3, 384)
        bias, at = carve(at, AH, 384)
        mT, _ = carve(0, KD, SEQ)
        mx = sb("score_max", [P, AH, 2])
        nmx = sb("minus_max", [P, AH, 2])
        den = sb("softmax_sum", [P, AH, 2])
        esink = sb("sink_exp", [P, AH, 2])
        sinkb = sb("sinks", [P, AH])
        lbc = sb("lower_bound", [P, RH])
        lbd = sb("lower_bound_logit", [P, RH])
        omlb = sb("one_minus_lower_bound", [P, RH])
        tab = sb("bias_table", [N_BUCKETS + 1, AH])
        hot_rows, start_at = carve(start_at, 384)
        hot = hot_rows[0:N_BUCKETS + 1]
        tabd_rows, start_at = carve(start_at, 384)
        tabd = tabd_rows[0:AH]
        assert start_at <= ARENA - AH * 384
        ones = sb("ones", [P, SEQ])
        tab_in = signal("bias_table_in")
        tab_out = signal("bias_by_distance_stored")
        bias_in = signal("bias_in")
        bias_p = signal("bias_by_distance")
        bias_d = signal("bias_by_distance_copied")
        lb_d = signal("lower_bound_by_vector")
        lb_a = signal("lower_bound_by_scalar")
        proj_d = signal("projection_kept_by_vector")
        proj_a = signal("projection_kept_by_scalar")
        ak_swapped = signal("keys_swapped")
        att_p = signal("attention_by_tensor")
        att_d = signal("attention_by_vector")
        att_a = signal("attention_by_scalar")
        rec_p = signal("recurrence_by_tensor")
        rec_d = signal("recurrence_by_vector")
        rec_a = signal("recurrence_by_scalar")
        rec_g = signal("recurrence_by_gpsimd")
        pgate, at = carve(0, TT, D)
        pemb, at = carve(at, TT, D)
        pscr, at = carve(at, TT, D)
        ple_p = signal("embedding_projected")
        ple_a = signal("embedding_by_scalar")
        ple_d = signal("embedding_by_vector")
        gains_in = signal("row_gains_in")

        def ple_views(key):
            c = chunks[key] % BAYS
            return bay[:, c], w_hi[:, key[1] % HI_BAYS], bay_lo[:, c]

        KAPPA = float(np.exp(-0.5))
        RWT = 4
        G, _ = carve(0, 2, 8, 4, P)
        pfT, at = carve(0, 15, SEQ + 1)
        lw, a1 = carve(0, RWT, SEQ)
        cc, a1 = carve(a1, RWT, SEQ)
        dm, a1 = carve(a1, RWT, SEQ)
        assert a1 <= at
        dm0, at = carve(at, RWT, SEQ)
        aT, at = carve(at, RWT, SEQ)
        kk, at = carve(at, RWT, SEQ)
        ktmp, at = carve(at, RWT, SEQ)
        at = max(at, 8192)
        xm, at = carve(at, 15, SEQ)
        obT = xm[:, 0:4]
        bonus = xm[:, 4:8]
        AR, at = carve(at, RWT, 2, 2, P)
        Bk, at_k = carve(at, RWT, SEQ)
        Kk, at_k = carve(at_k, RWT, SEQ)
        M1, _ = carve(at, 4, 4, P)
        at = at_k
        X, at = carve(at, 4, 4, P)
        Y, at = carve(at, 4, 4, P)
        rs, _ = carve(at - 2048 - 2048, 2, 4, 64)
        us, _ = carve(at - 2048 - 2048 + 512, 2, 4, 64)
        yv, _ = carve(at - 2048 - 2048 + 1024, 2, 8, 64)
        qaT, at = carve(at, 4, SEQ)
        kaT, at = carve(at, 4, SEQ)
        va, at = carve(at, TT, 512)
        lsp, at = carve(at, 2, 2, 384)
        wst, at = carve(at, 2, 2, 384)
        ysq, _ = carve(at - 3072, 2, 8, 64)
        oaT, at = carve(at, 4, SEQ)
        vtok = hn[:, 0].rearrange("p (t n) -> p t n", t=TT)
        btok, ktok = hn[:, 1, 0:512], hn[:, 1, 512:1024]
        s0 = sb("state", [P, 4, 64])
        sfac = sb("state_decay", [P, 4])
        gmean = sb("group_mean", [P, 16])
        rw_in = signal("rwkv_projection_kept")
        mix_g = signal("shift_difference")
        mix_d = signal("token_mix")
        pre_d = signal("rwkv_prepared_by_vector")
        pre_a = signal("rwkv_prepared_by_scalar")
        pre_p = signal("rwkv_prepared_by_tensor")
        stick_in = signal("stick_projection_kept")
        stick_p = signal("stick_by_tensor")
        stick_a = signal("stick_by_scalar")
        stick_d = signal("stick_by_vector")
        stick_g = signal("stick_by_gpsimd")
        inv_p = signal("inverse_by_tensor")
        inv_a = signal("inverse_by_scalar")
        inv_d = signal("inverse_by_vector")
        sol_p = signal("solve_by_tensor")
        sol_a = signal("solve_by_scalar")
        sol_d = signal("solve_by_vector")
        LEVEL_N = len(LEVELS)
        MIXES = [(("wk", 0), 4, 2, P), (("wk", 1), 6, 2, P), (("wr", 0), 0, 2, P), (("wr", 1), 2, 2, P),
                 ("lora_in", 12, 2, P), ("lora_in_tail", 14, 1, 32), (("wv", 0), 8, 2, P), (("wv", 1), 10, 2, P)]

        def head(t, hd):
            return t[64 * (hd % 2):64 * (hd % 2) + 64, hd // 2]
        MH, QH = 16, 96
        MSCALE = float(1.0 / np.sqrt(96.0))
        ctok, at = carve(0, TT, 672)
        clT, at = carve(at, 5, SEQ)
        qtok, at = carve(at, TT, MH, QH)
        ktok2, at = carve(at, TT, MH, QH)
        vtk, at = carve(at, TT, MH, 64)
        rt, at = carve(at, 4, TT * MH * 16)
        qkT, at = carve(at, 3, 2, SEQ)
        msc, at = carve(at, 6, 384)
        mpb, at = carve(at, 2, 384)
        moT, at = carve(at, KD, SEQ)
        mlsq, at = carve(at, TT, 640)
        mmax = sb("mla_max", [P, 6, 2])
        mden = sb("mla_sum", [P, 6, 2])
        cosv = sb("cos", [P, TT, 16])
        sinv = sb("sin", [P, TT, 16])
        freq = sb("rotary_frequency", [P, 16])
        posi = sb("positions", [P, TT], I32)
        posf = sb("positions_float", [P, TT])
        ang = sb("angles", [P, TT, 16])
        turns = sb("whole_turns", [P, TT, 16])
        rot_in = signal("rotary_in")
        rot_d = signal("angles_ready")
        rot_a = signal("cos_and_sin_ready")
        lat_a = signal("latent_by_scalar")
        lat_d = signal("latent_by_vector")
        lat_p = signal("latent_transposed")
        up_a = signal("heads_kept_by_scalar")
        up_d = signal("heads_kept_by_vector")
        mla_p = signal("mla_by_tensor")
        mla_a = signal("mla_by_scalar")
        mla_d = signal("mla_by_vector")
        mla_g = signal("mla_by_gpsimd")
        UQ = {(n, t): 2 * n + t for n in range(3) for t in range(TT)}
        UKV = {(n, t, half): (6 + 4 * n + 2 * t + half) % 8 for n in range(2) for t in range(TT) for half in range(2)}
        LAG_S, LAG_T, LAG_V = 1, 4, 5

        def wait_up(eng, bank_no, event):
            eng.wait_ge(*(up_a if bank_no % 2 == 0 else up_d).at(*event))
        def keep_up(eng, parity):
            done = (up_a, up_d)[parity]

            def copy(dst, src):
                return nc.scalar.activation(dst, src, ACT.Copy) if parity == 0 else nc.vector.tensor_copy(dst, src)

            for (n, t), b in UQ.items():
                if b % 2 == parity:
                    eng.wait_ge(*used_up_to(("uq", n)))
                    dst = qtok[:, t].rearrange("p a b -> p (a b)")[:, n * 512:(n + 1) * 512]
                    copy(dst, bank(b)).then_inc(*done.inc("q", b // 2, b % 2))
            for (n, t, half), b in UKV.items():
                if b % 2 == parity:
                    eng.wait_ge(*used_up_to(("ukv", n)))
                    src = bank(b).rearrange("p (a b) -> p a b", a=4)
                    heads = slice(8 * n + 4 * half, 8 * n + 4 * half + 4)
                    copy(ktok2[:, t, heads, 0:64], src[:, :, 0:64])
                    ins = copy(vtk[:, t, heads], src[:, :, 64:128])
            ins.then_inc(*done.inc("last"))
        block = ctx.enter_context(nc.Block())

        def bay_view(key, offset, shape):
            b = bay[:, chunks[key] % BAYS, offset:offset + int(np.prod(shape))]
            return b.rearrange("p (a b) -> p a b", a=shape[0]) if len(shape) == 2 else b

        def bank(b, n=512):
            return ps[:, b, 0:n]

        def used_up_to(key, i=None):
            n = chunks[key] + 1
            return used.sem, n if i is None else i * BAYS + n

        def wait_weights(eng, key, i=None):
            c = chunks[key]
            count = 16 * (c // BAYS + 1)
            eng.wait_ge(landed[c % BAYS].sem, count if i is None else i * 16 + count)

        def split_steps(g):
            steps = [("gate", 0)] if g == 0 else []
            steps.append(("up", g))
            if g:
                steps.append(("out", g - 1))
            steps.append(("gate", g + 1) if g < GROUPS - 1 else ("out", g))
            return steps

        def wait_split(eng, signals, f, kind, g, i=None):
            step = {"gate": max(g - 1, 0), "up": g, "out": min(g + 1, GROUPS - 1)}[kind]
            for s in signals:
                eng.wait_ge(*s.at_group(i, f, step, kind, g - step))

        def wait_hidden(eng, signal, f, g, i=None):
            eng.wait_ge(*(signal.at_group(i, f, g + 1, "before") if g < GROUPS - 1 else signal.at(f, "last")))

        def split_views(f, kind, g):
            c = ffn_chunk(kind, g)
            raw = bay[:, chunks[f, c] % BAYS]
            return raw, w_hi[:, c % HI_BAYS], bay_lo[:, chunks[f, c] % BAYS]


        def ffn_slot(n):
            if n < 2:
                return ("gate", "up")[n], 0
            g, k = (n - 2) // 3 + 1, (n - 2) % 3
            return (("gate", g), ("up", g), ("out", g - 1))[k] if g < GROUPS else ("out", GROUPS - 1)

        def ffn_chunk(kind, g):
            if kind == "out":
                return 3 * g + 4 if g < GROUPS - 1 else 3 * GROUPS - 1
            return 3 * g - (g > 0) + (kind == "up")

        LOOP0, ROUNDS = 2, (GROUPS - 3) // 2

        @block.sync
        def _(sp):
            sp.dma_start(h[:], I["x"][0].rearrange("(t p) d -> p t d", p=P)).then_inc(*x_in.inc("x", by=16))
            sp.dma_start(mats[:], I["mats"]).then_inc(*mats_in.inc("mats", by=16))

            def small_inputs():
                sp.wait_ge(*zeros.at("stack"))
                for dst, src in vectors:
                    sp.dma_start(dst, src).then_inc(vectors_in.sem, 16)
                sp.dma_start(pin[:, 0], I["p"][0, 0].rearrange("(t p) d -> p t d", p=P)).then_inc(consts_in.sem, 16)
                for i in range(2):
                    sp.dma_start(pin[:, 1 + i], I["p_2"][i, 0].rearrange("(t p) d -> p t d", p=P)).then_inc(consts_in.sem, 16)
                sp.dma_start(mask_rows, I["masks"]).then_inc(consts_in.sem, 16)
                sp.dma_start(sinkb[:], I["attn_sinks"][0].partition_broadcast(P)).then_inc(consts_in.sem, 16)
                sp.dma_start(tab[0:N_BUCKETS, :], I["rel_bias"]).then_inc(tab_in.sem, 16)
                sp.dma_start(hot[:], I["hot"]).then_inc(tab_in.sem, 16)
                sp.dma_start(row_gain[:, 0], I["norm_final"].partition_broadcast(P)).then_inc(gains_in.sem, 16)
                sp.dma_start(row_gain[:, 1], I["ple_norm_2"][0].partition_broadcast(P)).then_inc(gains_in.sem, 16)
                with nc.allow_non_contiguous_dma(reason="256 positions, one to a partition and tile"):
                    sp.dma_start(posi[:], I["positions_2"][0].rearrange("(t p) -> p t", p=P)).then_inc(rot_in.sem, 16)
                sp.dma_start(freq[:], I["freq"].partition_broadcast(P)).then_inc(rot_in.sem, 16)

            def load(c, dst, src, i=None):
                if i is not None:
                    sp.wait_ge(used.sem, i * BAYS + max(c - BAYS + 1, 1))
                elif c >= BAYS:
                    sp.wait_ge(used.sem, c - BAYS + 1)
                sp.dma_start(dst, src).then_inc(landed[c % BAYS].sem, 16)

            for kind, key, *rest in plan:
                if kind == "chunk":
                    (offset, shape, src), part = rest
                    load(chunks[key], bay_view(key, offset, shape)[part] if shape[0] > 1 else bay[part, chunks[key] % BAYS, 0:shape[1]], src)
                    continue
                w1, w2 = rest
                c0 = chunks[key, 0]

                def group_load(n, i=None):
                    kind, g = ffn_slot(n)
                    if kind == "out":
                        at = sp.snap(i * 4 + 2 * g) if i is not None else 2 * g
                        load(c0 + n, bay_view((key, n), 0, [2, D]), w2[:, bass.ds(at, 2), :], i)
                    else:
                        first = (kind == "up") * F + g * 256
                        at = sp.snap(i * 512 + first) if i is not None else first
                        load(c0 + n, bay_view((key, n), 0, [KD, 256]), w1[:, :, bass.ds(at, 256)], i)

                n0 = ffn_chunk("gate", LOOP0)
                for n in range(n0):
                    group_load(n)
                if key == "ffn1":
                    small_inputs()
                with sp.Fori(0, ROUNDS) as i:
                    for n in range(n0, n0 + BAYS):
                        group_load(n, i)
                for n in range(n0 + BAYS * ROUNDS, 3 * GROUPS):
                    group_load(n)

        @block.tensor
        def _(pe):
            def weights(key, i=None):
                c = chunks[key]
                count = 16 * (c // BAYS + 1)
                pe.wait_ge(landed[c % BAYS].sem, count if i is None else i * 16 + count)

            def through(mm, key, i=None):
                if i is None:
                    assert not book or used.count == chunks[key], (key, used.count, chunks[key])
                mm.then_inc(*used.inc(key))

            pe.wait_ge(mats_in.sem, 16)
            pe.wait_ge(first_in.sem, 16)
            nc.tensor.transpose(ps[:, 0, 0:KD], first_rows, ident[0:KD, 0:KD]).then_inc(*cols_turned.inc("first"))

            def turn_small_inputs():
                pe.wait_ge(consts_in.sem, 16 * N_CONSTS)
                pe.wait_ge(vectors_in.sem, 16 * len(vectors))
                for t in range(3):
                    mm = nc.tensor.transpose(ps[:, 4, t * P:(t + 1) * P], stack[:, t], ident)
                mm.then_inc(*cols_turned.inc("cols"))
                for n in range(3):
                    for k in range(2):
                        for t in range(TT):
                            mm = nc.tensor.transpose(ps[:, 5 + n, k * SEQ + t * P:k * SEQ + (t + 1) * P],
                                                     pin[:, n, t, k * P:(k + 1) * P], ident)
                mm.then_inc(*cols_turned.inc("p"))

            def norm(n):
                pe.wait_ge(*scaled_d.at(n, 0))
                for k in range(KD):
                    nc.tensor.transpose(ps[:, 4 + k // 2, (k % 2) * SEQ:(k % 2) * SEQ + P], hn[:, 0, k * P:(k + 1) * P], ident)
                pe.wait_ge(*scaled_d.at(n, 1))
                for k in range(KD):
                    if k == KD // 2:
                        pe.wait_ge(*scaled_a.at(n))
                    mm = nc.tensor.transpose(ps[:, 4 + k // 2, (k % 2) * SEQ + P:(k % 2 + 1) * SEQ], hn[:, 1, k * P:(k + 1) * P], ident)
                    if k % 2:
                        mm.then_inc(*turned.inc(n, k // 2))
                pe.wait_ge(*(x_hi_d if n in SPLIT else x_d).at(n))
                pe.wait_ge(*(x_hi_a if n in SPLIT else x_a).at(n))
                if n in SPLIT:
                    pe.wait_ge(*x_lo_d.at(n, 0))

            def features(dst, lhs, n=KD, rhs=None, **kw):
                for k in range(n):
                    mm = nc.tensor.matmul(dst, lhs(k), xT[:, k] if rhs is None else rhs(k), start=(k == 0), stop=(k == n - 1), **kw)
                return mm

            def split_features(dst, hi, lo, j, first=None):
                for n, (w, x) in enumerate(((hi, x_hi), (lo, x_hi), (hi, x_lo))):
                    if n == 2 and first:
                        pe.wait_ge(*x_lo_d.at(first, 3))
                    for k in range(KD):
                        mm = nc.tensor.matmul(dst, w[:, k, j * P:(j + 1) * P], x[:, k], start=(n + k == 0), stop=(n == 2 and k == KD - 1))
                return mm

            def ffn(f):
                def into_hidden(g, i=None):
                    gate, up = (f, ffn_chunk("gate", g)), (f, ffn_chunk("up", g))
                    parts = {kind: [t.rearrange("p (a b) -> p a b", a=KD) for t in split_views(f, kind, g)[1:]] for kind in ("gate", "up")}
                    if g >= 2:
                        pe.wait_ge(*hid_ready.at_group(i, f, g - 2))
                    for n, key in enumerate((gate, up)):
                        wait_split(pe, (w_hi_ready, w_lo_g), f, ("gate", "up")[n], g, i)
                        for j in range(2):
                            mm = split_features(ps[:, 4 + 2 * (g % 2) + j, n * SEQ:(n + 1) * SEQ], *parts[("gate", "up")[n]], j,
                                                f if g == 0 and n + j == 0 else None)
                        through(mm, key, i)

                def out_of_hidden(g, i=None):
                    key = (f, ffn_chunk("out", g))
                    hi, lo = (t.rearrange("p (a b) -> p a b", a=2) for t in split_views(f, "out", g)[1:])
                    wait_split(pe, (w_hi_ready, w_lo_d), f, "out", g, i)
                    wait_hidden(pe, hid_hi_ready, f, g, i)
                    wait_hidden(pe, hid_lo_ready, f, g, i)
                    if f == "ffn1" and g == GROUPS - 1:
                        turn_small_inputs()
                    for t in range(TT):
                        for half in range(2):
                            for n, (x, w) in enumerate(((hid_hi, hi), (hid_lo, hi), (hid_hi, lo))):
                                for j in range(2):
                                    mm = nc.tensor.matmul(bank(2 * t + half), x[:, g % 2, j, t * P:(t + 1) * P],
                                                          w[:, j, half * 512:(half + 1) * 512],
                                                          start=(g == 0 and n + j == 0), stop=(g == GROUPS - 1 and n == 2 and j == 1))
                        if g == GROUPS - 1 and t == 0:
                            mm.then_inc(*acc_ready.inc(f, 0))
                    through(mm, key, i)

                into_hidden(0)
                into_hidden(1)
                out_of_hidden(0)
                with pe.Fori(0, ROUNDS) as i:
                    since = used.count
                    for g in (2, 3):
                        into_hidden(g, i)
                        out_of_hidden(g - 1, i)
                    used.repeated(f, since, ROUNDS)
                into_hidden(GROUPS - 1)
                out_of_hidden(GROUPS - 2)
                out_of_hidden(GROUPS - 1)

            def pair_of_features(key, b, tiles=2):
                weights(key)
                w = bay_view(key, 0, [KD, 256])
                for j in range(tiles):
                    mm = features(ps[:, b, j * SEQ:(j + 1) * SEQ], lambda k: w[:, k, j * P:(j + 1) * P])
                through(mm, key)

            def pair_of_tokens(key, b, c0=0, width=256):
                w = bay_view(key, 0, [KD, 256])
                for t in range(TT):
                    for k in range(KD):
                        mm = nc.tensor.matmul(ps[:, b, t * width:(t + 1) * width], xT[:, k, t * P:(t + 1) * P],
                                              w[:, k, c0:c0 + width], start=(k == 0), stop=(k == KD - 1))
                return mm

            def project_features(name, srcT, b0):
                weights((name, 0))
                weights((name, 1))
                w = [bay_view((name, n), 0, [2, D]) for n in range(2)]
                for j in range(KD):
                    for k in range(4):
                        mm = nc.tensor.matmul(ps[:, b0 + j // 2, j % 2 * SEQ:(j % 2 + 1) * SEQ], w[k // 2][:, k % 2, j * P:(j + 1) * P],
                                              srcT[:, k], start=(k == 0), stop=(k == 3))
                        if j == KD - 1 and k == 1:
                            through(mm, (name, 0))
                    if j % 2 and j < KD - 1:
                        mm.then_inc(*att_p.inc(name, j // 2))
                through(mm, (name, 1))

            def project_tokens(name, srcT, key, b0=0, at_chunk={}):
                for n in range(4):
                    if n in at_chunk:
                        at_chunk[n]()
                    weights((name, n))
                    w = bay_view((name, n), 0, [2, D])
                    for t in range(TT):
                        for half in range(2):
                            for j in range(2):
                                k = 2 * n + j
                                mm = nc.tensor.matmul(bank(b0 + 2 * t + half), (srcT(k) if callable(srcT) else srcT[:, k])[:, t * P:(t + 1) * P], w[:, j, half * 512:(half + 1) * 512],
                                                      start=(k == 0), stop=(k == KD - 1))
                        if n == 3 and t == 0:
                            mm.then_inc(*acc_ready.inc(key, 0))
                    through(mm, (name, n))

            def mix1():
                pair_of_features(("rf", 0), 0)
                pair_of_features(("rf", 1), 1)
                pair_of_features(("rq", 0), 2)
                pe.wait_ge(*bias_d.at("t"))
                pair_of_features(("rq", 1), 3)
                for n in range(2):
                    weights(("ri", n))
                    pe.wait_ge(*proj_a.at("rf", n))
                    through(pair_of_tokens(("ri", n), n), ("ri", n))
                for n in range(2):
                    pe.wait_ge(*proj_d.at("rq", n))
                    pair_of_features(("aq", n), 2 + n)
                weights("akv")
                pe.wait_ge(*proj_a.at("ri", 0))
                w = bay_view("akv", 0, [KD, 256])
                features(ps[:, 0, 0:SEQ], lambda k: w[:, k, 0:P])
                for t in range(TT):
                    for k in range(KD):
                        mm = nc.tensor.matmul(ps[:, 0, SEQ + t * P:SEQ + (t + 1) * P], xT[:, k, t * P:(t + 1) * P], w[:, k, P:2 * P],
                                              start=(k == 0), stop=(k == KD - 1))
                through(mm, "akv")
                pe.wait_ge(*proj_a.at("ri", 1))
                pair_of_features(("rg", 0), 1)
                pe.wait_ge(*proj_d.at("aq", 0))
                pair_of_features(("rg", 1), 2)
                pe.wait_ge(*proj_d.at("akv"))
                pe.wait_ge(ak_swapped.sem, 32)
                for hd in range(AH):
                    r, j, b = slice(64 * (hd % 2), 64 * (hd % 2) + 64), hd // 2, 4 + hd % 4
                    ak = akT[r, (hd // 4 + hd) % 2]
                    if hd >= 4:
                        pe.wait_ge(*att_d.at("biased", hd - 4))
                    nc.tensor.matmul(ps[:, b, 0:256], aqT[r, j, P:2 * P], ak[:, 0:256], start=True, stop=True)
                    nc.tensor.matmul(ps[:, b, 256:384], aqT[r, j, 0:P], ak[:, 0:P], start=True, stop=True).then_inc(*att_p.inc("scores", hd))
                pe.wait_ge(*att_d.at("biased", AH - 1))
                for n in range(len(LV) + 1):
                    b = 4 + n % 2 * 2
                    if n >= 2:
                        pe.wait_ge(*rec_d.at("placed", n - 2))
                    if n == 0:
                        pe.wait_ge(*rec_d.at("q_and_k"))
                    else:
                        pe.wait_ge(*rec_d.at("decayed", n - 1))
                        z = zT[:, (n - 1) % 2]
                    for t in range(TT if n < len(LV) else 1):
                        for hd in range(RH):
                            o = ps[:, b + t, hd * P:(hd + 1) * P]
                            if n == 0:
                                a, c = kT[:, hd, t * P:(t + 1) * P], rqT[:, hd, t * P:(t + 1) * P]
                            elif n < len(LV):
                                a = c = z[:, hd, t * P:(t + 1) * P]
                            else:
                                a, c = z[:, hd, 0:P], z[:, hd, P:2 * P]
                            mm = nc.tensor.matmul(o, a, c, start=True, stop=True)
                    mm.then_inc(*rec_p.inc("scores", n))
                    if n < 8:
                        pb = (3 + n) % 4
                        if n == 0:
                            pe.wait_ge(*proj_d.at("aq", 1))
                        elif n == 1:
                            pe.wait_ge(*proj_d.at("akv"))
                        elif n < 4:
                            pe.wait_ge(*proj_a.at("rg", n - 2))
                        else:
                            pe.wait_ge(*proj_a.at("g", n - 4))
                        pair_of_features(("g", n), pb)
                pe.wait_ge(*rec_d.at("placed", len(LV)))
                for hd in range(RH):
                    c = slice(hd * P, (hd + 1) * P)
                    mm = nc.tensor.matmul(ps[:, 6, c], AT[:, 0, hd], vR[:, 0, c], start=True, stop=True)
                mm.then_inc(*rec_p.inc("out", 0))
                for hd in range(RH):
                    c = slice(hd * P, (hd + 1) * P)
                    nc.tensor.matmul(ps[:, 7, c], AT[:, 2, hd], vR[:, 0, c], start=True, stop=False)
                    mm = nc.tensor.matmul(ps[:, 7, c], AT[:, 1, hd], vR[:, 1, c], start=False, stop=True)
                mm.then_inc(*rec_p.inc("out", 1))
                pe.wait_ge(*proj_a.at("g", 7))

                def turn(hd):
                    pe.wait_ge(*att_d.at("probs", hd))
                    if hd >= 2:
                        pe.wait_ge(*att_a.at("turned", hd - 2))
                    for n in range(3):
                        mm = nc.tensor.transpose(ps[:, 4 + hd % 2, n * P:(n + 1) * P], sc[:, hd, n * P:(n + 1) * P], ident)
                    mm.then_inc(*att_p.inc("turned", hd))

                turn(0)
                for hd in range(AH):
                    if hd + 1 < AH:
                        turn(hd + 1)
                    pe.wait_ge(*att_a.at("turned", hd))
                    r, kv = slice(64 * (hd % 2), 64 * (hd % 2) + 64), slice(64 * (hd // 4), 64 * (hd // 4) + 64)
                    q = pbT[:, hd % 3]
                    nc.tensor.matmul(ps[r, hd // 2, P:2 * P], av[:, 0, kv], q[:, 0:P], start=True, stop=False)
                    nc.tensor.matmul(ps[r, hd // 2, P:2 * P], av[:, 1, kv], q[:, P:2 * P], start=False, stop=True)
                    nc.tensor.matmul(ps[r, hd // 2, 0:P], av[:, 0, kv], q[:, 2 * P:3 * P], start=True, stop=True).then_inc(*att_p.inc("out", hd))
                for t in range(TT):
                    pe.wait_ge(*rec_d.at("normed", t))
                for k in range(4):
                    for t in range(TT):
                        mm = nc.tensor.transpose(ps[:, 6 + k // 2, k % 2 * SEQ + t * P:k % 2 * SEQ + (t + 1) * P], orec[:, t, k * P:(k + 1) * P], ident)
                    if k % 2:
                        mm.then_inc(*rec_p.inc("turned", k // 2))
                pe.wait_ge(*att_d.at("outT", 3))
                project_features("att_proj", attT, 0)
                pe.wait_ge(*rec_d.at("recT", 1))
                project_features("rec_proj", recT, 4)
                pe.wait_ge(*att_d.at("merged", 3))
                project_tokens("mix_out", mT, "mix1")

            def ple(stage, n):
                key = (f"{stage}_proj", 0)
                weights(key)
                w = bay_view(key, 0, [2, D])
                for t in range(TT):
                    pe.wait_ge(*h_ready.at(stage, t))
                    for half in range(2):
                        for k in range(2):
                            mm = nc.tensor.matmul(bank(2 * t + half), pT[:, n, k, t * P:(t + 1) * P], w[:, k, half * 512:(half + 1) * 512],
                                                  start=(k == 0), stop=(k == 1))
                through(mm, key)
                norm(stage)
                for n in range(4):
                    key = (f"{stage}_gate", n)
                    hi, lo = (t.rearrange("p (a b) -> p a b", a=2) for t in ple_views(key)[1:])
                    pe.wait_ge(*w_hi_ready.at(key))
                    pe.wait_ge(*(w_lo_d if n == 2 else w_lo_g).at(key))
                    for t in range(TT):
                        for half in range(2):
                            for m, (x, w) in enumerate(((x_hi, hi), (x_hi, lo), (x_lo, hi))):
                                if n + t + half == 0 and m == 2:
                                    pe.wait_ge(*x_lo_d.at(stage, 3))
                                for j in range(2):
                                    mm = nc.tensor.matmul(bank(4 + 2 * t + half), x[:, 2 * n + j, t * P:(t + 1) * P], w[:, j, half * 512:(half + 1) * 512],
                                                          start=(n + m + j == 0), stop=(n == 3 and m == 2 and j == 1))
                        if n == 3 and t == 0:
                            mm.then_inc(*acc_ready.inc(stage, 0))
                    through(mm, key)

            def hyb():
                norm("hyb")
                pair_of_features(("wk", 0), 0)
                pair_of_features(("wk", 1), 1)
                pair_of_features(("wr", 0), 2)
                pair_of_features(("wr", 1), 3)
                pe.wait_ge(*rw_in.at(("wk", 0)))
                pair_of_features("lora_in", 0)
                weights("lora_in_tail")
                pe.wait_ge(*rw_in.at(("wk", 1)))
                w = bay_view("lora_in_tail", 0, [KD, 32])
                through(features(ps[0:32, 1, 0:SEQ], lambda k: w[:, k, :]), "lora_in_tail")
                pe.wait_ge(*rw_in.at(("wr", 0)))
                pair_of_features(("wv", 0), 2)
                pe.wait_ge(*rw_in.at(("wr", 1)))
                pair_of_features(("wv", 1), 3)
                pe.wait_ge(*rw_in.at("lora_in"))
                pair_of_features(("sq", 0), 0)
                pe.wait_ge(*pre_a.at("tanh"))
                for key, r, b in (("w2", slice(0, 64), 4), ("a2", slice(64, P), 6)):
                    weights(key)
                    w = bay[r, chunks[key] % BAYS, 0:512]
                    for j in range(RWT):
                        mm = nc.tensor.matmul(ps[:, b + j // 2, j % 2 * SEQ:(j % 2 + 1) * SEQ], w[:, j * P:(j + 1) * P], xm[r, 12],
                                              start=True, stop=True)
                    through(mm, key)
                pe.wait_ge(*rw_in.at("lora_in_tail"))
                pair_of_features(("sq", 1), 1)
                pe.wait_ge(*rw_in.at(("wv", 0)))
                pair_of_features(("sk", 0), 2)
                pe.wait_ge(*pre_d.at("kk_squares"))
                pe.wait_ge(*pre_a.at("decay"))
                for j in range(RWT):
                    mm = nc.tensor.matmul(ps[:, 4 + j // 2, j % 2 * SEQ:(j % 2 + 1) * SEQ], mats[:, 1], dm0[:, j], start=True, stop=True)
                mm.then_inc(*pre_p.inc("kk_sums"))
                pe.wait_ge(*rw_in.at(("wv", 1)))
                pair_of_features(("sk", 1), 3)
                pe.wait_ge(*mix_d.at(("wv", 1)))
                pe.wait_ge(*pre_a.at("rate"))
                for t in range(TT):
                    for j in range(4):
                        mm = nc.tensor.transpose(ps[:, 6 + t, j * P:(j + 1) * P], xm[:, 8 + j, t * P:(t + 1) * P], ident)
                mm.then_inc(*pre_p.inc("v_turned"))
                pe.wait_ge(*stick_in.at("sq", 0))
                weights(("sv", 0))
                through(pair_of_tokens(("sv", 0), 0), ("sv", 0))
                pe.wait_ge(*stick_in.at("sq", 1))
                weights(("sv", 1))
                through(pair_of_tokens(("sv", 1), 1), ("sv", 1))
                pe.wait_ge(*pre_d.at("bonus_terms"))
                pe.wait_ge(*pre_d.at("kk_norm"))
                for j in range(RWT):
                    mm = nc.tensor.matmul(ps[:, 4 + j // 2, j % 2 * SEQ:(j % 2 + 1) * SEQ], mats[:, 1], xm[:, j], start=True, stop=True)
                mm.then_inc(*pre_p.inc("bonus"))
                pe.wait_ge(*pre_d.at("bk"))
                pe.wait_ge(*pre_a.at("vtok"))
                for n, t in enumerate((Bk, Kk)):
                    for j in range(4):
                        mm = nc.tensor.transpose(ps[:, 6 + n, j * P:(j + 1) * P], t[:, j, 0:P], ident)
                mm.then_inc(*pre_p.inc("bk_turned"))
                for n in range(16):
                    c, hd, b = n // 8, n % 8, n % 4
                    if n < 4:
                        pe.wait_ge(*(stick_in.at("sv", n) if n < 2 else stick_in.at("sk", n - 2)))
                    else:
                        pe.wait_ge(*inv_d.at("scores", n - 4))
                    ar = head(AR, hd)[:, c].rearrange("p a t -> p (a t)")
                    nc.tensor.matmul(ps[:, b, 0:256], head(Bk, hd)[:, c * P:(c + 1) * P], ar, start=True, stop=True)
                    nc.tensor.matmul(ps[:, b, 256:512], head(Kk, hd)[:, c * P:(c + 1) * P], ar, start=True, stop=True).then_inc(*inv_p.inc("scores", n))

                def stick_scores(g):
                    if g == 0:
                        pe.wait_ge(*pre_d.at("bonus"))
                    if g == 1:
                        pe.wait_ge(*pre_a.at("bk_turned"))
                    if g >= 2:
                        pe.wait_ge(*stick_a.at("out", g - 2))
                    for n in range(2):
                        b, q, k = 4 + 2 * (g % 2) + n, head(qaT, 2 * g + n), head(kaT, 2 * g + n)
                        nc.tensor.matmul(ps[:, b, 0:256], k[:, 0:P], q, start=True, stop=False, skip_group_check=True)
                        mm = nc.tensor.matmul(ps[:, b, 256:384], k[:, P:2 * P], q[:, P:2 * P], start=False, stop=False, skip_group_check=True)
                    mm.then_inc(*stick_p.inc("scores", g))

                def stick_sums(g):
                    pe.wait_ge(*stick_g.at("softplus", g))
                    for n in range(2):
                        b, s = 4 + 2 * (g % 2) + n, lsp[:, g % 2, n]
                        nc.tensor.matmul(ps[:, b, 0:384], mats[:, 3], s, start=False, stop=False, skip_group_check=True)
                        mm = nc.tensor.matmul(ps[:, b, P:2 * P], mats[:, 4], s[:, 256:384], start=False, stop=True, skip_group_check=True)
                    mm.then_inc(*stick_p.inc("sums", g))

                def stick_out(g):
                    pe.wait_ge(*stick_g.at("weights", g))
                    for n in range(2):
                        hd = 2 * g + n
                        o, w = ps[64 * n:64 * n + 64, 4 + 2 * (g % 2), 0:256], wst[:, g % 2, n]
                        nc.tensor.matmul(o, va[:, 0, hd * 64:(hd + 1) * 64], w[:, 0:256], start=True, stop=False, skip_group_check=True)
                        mm = nc.tensor.matmul(o[:, P:2 * P], va[:, 1, hd * 64:(hd + 1) * 64], w[:, 256:384], start=False, stop=True, skip_group_check=True)
                    mm.then_inc(*stick_p.inc("out", g))

                def level(n):
                    if n:
                        for g in range(4):
                            pe.wait_ge(*inv_d.at("X", n - 1, g))
                            for i in range(4):
                                mm = nc.tensor.matmul(ps[:, g, i * P:(i + 1) * P], G[:, g // 2, g % 2 * 4 + i, 0], X[:, g, i], start=True, stop=True)
                            mm.then_inc(*inv_p.inc("M1", n, g))
                        for g in range(4):
                            pe.wait_ge(*inv_a.at("M1", n, g))
                            for i in range(4):
                                mm = nc.tensor.matmul(ps[:, g, i * P:(i + 1) * P], M1[:, g, i], Y[:, g, i], start=True, stop=True)
                            mm.then_inc(*inv_p.inc("Y", n, g))
                    if n < LEVEL_N - 1:
                        for g in range(4):
                            pe.wait_ge(*inv_d.at("Y", n, g))
                            for i in range(4):
                                mm = nc.tensor.transpose(ps[:, g, i * P:(i + 1) * P], Y[:, g, i], ident)
                            mm.then_inc(*inv_p.inc("X", n, g))

                pe.wait_ge(*inv_d.at("scores", 15))
                stick_scores(0)
                level(0)
                stick_scores(1)
                level(1)
                stick_sums(0)
                level(2)
                stick_out(0)
                stick_sums(1)
                stick_scores(2)
                level(3)
                stick_out(1)
                stick_scores(3)
                stick_sums(2)
                level(4)
                stick_out(2)
                stick_sums(3)
                level(5)
                stick_out(3)
                level(6)

                def cols64(b, hd):
                    return ps[:, b, hd // 2 * 64:hd // 2 * 64 + 64]

                for c in range(2):
                    if c == 0:
                        pe.wait_ge(*stick_a.at("out", 2))
                        pe.wait_ge(*stick_a.at("out", 3))
                    else:
                        pe.wait_ge(*sol_d.at("state"))
                    for hd in range(8):
                        o, vv = cols64(4 + hd % 2, hd), vtok[:, c, hd * 64:(hd + 1) * 64]
                        if c:
                            nc.tensor.matmul(o, head(AR, hd)[:, c, 0], head(s0, hd), start=True, stop=False)
                        mm = nc.tensor.matmul(o, G[:, c, hd, 2], vv, start=(c == 0), stop=True)
                    mm.then_inc(*sol_p.inc("rhs", c))
                    pe.wait_ge(*sol_a.at("rhs", c))
                    if c == 0:
                        for g in range(4):
                            pe.wait_ge(*inv_d.at("Y", LEVEL_N - 1, g))
                    for hd in range(8):
                        mm = nc.tensor.matmul(ps[:, 6, (hd % 2 * 4 + hd // 2) * 64:(hd % 2 * 4 + hd // 2 + 1) * 64],
                                              Y[:, c * 2 + hd // 4, hd % 4], rs[:, hd % 2, hd // 2], start=True, stop=True)
                    mm.then_inc(*sol_p.inc("u", c))
                    pe.wait_ge(*sol_a.at("u", c))
                    if c == 0:
                        for hd in range(8):
                            o = ps[64 * (hd % 2):64 * (hd % 2) + 64, 7, hd // 2 * 64:hd // 2 * 64 + 64]
                            nc.tensor.matmul(o, btok[:, hd * 64:(hd + 1) * 64], us[:, hd % 2, hd // 2], start=True, stop=False)
                            mm = nc.tensor.matmul(o, ktok[:, hd * 64:(hd + 1) * 64], vtok[:, 0, hd * 64:(hd + 1) * 64], start=False, stop=True)
                        mm.then_inc(*sol_p.inc("state"))
                    for hd in range(8):
                        o = cols64(4 + hd % 2, hd)
                        if c:
                            nc.tensor.matmul(o, head(AR, hd)[:, c, 1], head(s0, hd), start=True, stop=False)
                        nc.tensor.matmul(o, G[:, c, hd, 1], us[:, hd % 2, hd // 2], start=(c == 0), stop=False)
                        mm = nc.tensor.matmul(o, G[:, c, hd, 3], vtok[:, c, hd * 64:(hd + 1) * 64], start=False, stop=True)
                    mm.then_inc(*sol_p.inc("y", c))
                    if c == 0:
                        pe.wait_ge(*sol_a.at("y", 0))
                pe.wait_ge(*sol_a.at("u", 1))
                weights("g2")
                weights("g2_tail")
                w, wt = bay[:, chunks["g2"] % BAYS, 0:512], bay[0:32, chunks["g2_tail"] % BAYS, 0:512]
                pe.wait_ge(*sol_d.at("state"))
                for j in range(RWT):
                    o = ps[:, 6 + j // 2, j % 2 * SEQ:(j % 2 + 1) * SEQ]
                    nc.tensor.matmul(o, w[:, j * P:(j + 1) * P], xm[:, 13], start=True, stop=False)
                    mm = nc.tensor.matmul(o, wt[:, j * P:(j + 1) * P], xm[0:32, 14], start=False, stop=True)
                mm.then_inc(*used.inc("g2", by=2))

                def turn_y():
                    pe.wait_ge(*sol_d.at("normed"))
                    for k in range(4):
                        for t in range(TT):
                            mm = nc.tensor.transpose(ps[:, 4 + k // 2, k % 2 * SEQ + t * P:k % 2 * SEQ + (t + 1) * P],
                                                     yv[:, t].rearrange("p a b -> p (a b)")[:, k * P:(k + 1) * P], ident)
                    mm.then_inc(*sol_p.inc("turned"))

                def rwkv_part():
                    turn_y()
                    pe.wait_ge(*sol_d.at("ob"))

                for g in range(4):
                    pe.wait_ge(*inv_d.at("Y", LEVEL_N - 1, g))
                project_tokens("hyb_out", lambda k: oaT[:, k] if k < 4 else obT[:, k - 4], "hyb", at_chunk={2: rwkv_part})

            def mla():
                norm("mla")
                for n in range(3):
                    key, width = ("down", n), min(256, 672 - 256 * n)
                    weights(key)
                    w = bay_view(key, 0, [KD, width])
                    for t in range(TT):
                        o = ps[:, t + n // 2 * 2, n % 2 * 256:n % 2 * 256 + width]
                        for k in range(KD):
                            mm = nc.tensor.matmul(o, xT[:, k, t * P:(t + 1) * P], w[:, k, :], start=(k == 0), stop=(k == KD - 1))
                    through(mm, key)
                pe.wait_ge(*lat_d.at("scaled"))
                for j in range(5):
                    for t in range(TT):
                        mm = nc.tensor.transpose(ps[:, 4 + j // 2, j % 2 * SEQ + t * P:j % 2 * SEQ + (t + 1) * P],
                                                 ctok[:, t, j * P:(j + 1) * P], ident)
                mm.then_inc(*lat_p.inc("turned"))
                pe.wait_ge(*lat_d.at("q"))
                pe.wait_ge(*lat_a.at("kv"))
                for n in range(3):
                    key = ("uq", n)
                    weights(key)
                    w = bay_view(key, 0, [3, 512])
                    for t in range(TT):
                        for k in range(3):
                            mm = nc.tensor.matmul(bank(UQ[n, t]), clT[:, k, t * P:(t + 1) * P], w[:, k, :], start=(k == 0), stop=(k == 2))
                    through(mm, key)
                for n in range(2):
                    key = ("ukv", n)
                    weights(key)
                    w = bay_view(key, 0, [2, 1024])
                    for t in range(TT):
                        for half in range(2):
                            b = UKV[n, t, half]
                            if b < 6:
                                wait_up(pe, b, ("q", b // 2, b % 2))
                            for k in range(2):
                                mm = nc.tensor.matmul(bank(b), clT[:, 3 + k, t * P:(t + 1) * P], w[:, k, half * 512:(half + 1) * 512],
                                                      start=(k == 0), stop=(k == 1))
                    through(mm, key)
                pe.wait_ge(*up_a.at("last"))
                pe.wait_ge(*up_d.at("last"))
                pe.wait_ge(*mla_d.at("rotated"))
                for i in range(MH + LAG_V):
                    if i < MH:
                        if i >= 2:
                            pe.wait_ge(*(mla_a if i % 2 == 0 else mla_d).at("turned", i - 2))
                        for n, s in enumerate((qtok, ktok2)):
                            for t in range(TT):
                                mm = nc.tensor.transpose(ps[0:QH, 4 + i % 2, n * SEQ + t * P:n * SEQ + (t + 1) * P], s[:, t, i], ident)
                        mm.then_inc(*mla_p.inc("turned", i))
                    hd = i - LAG_S
                    if 0 <= hd < MH:
                        pe.wait_ge(*(mla_a if hd % 2 == 0 else mla_d).at("turned", hd))
                        if hd >= 2:
                            pe.wait_ge(*mla_d.at("masked", hd - 2))
                        q, k, b = qkT[0:QH, hd % 3, 0], qkT[0:QH, hd % 3, 1], 6 + hd % 2
                        nc.tensor.matmul(ps[:, b, 0:256], q[:, P:2 * P], k, start=True, stop=True)
                        nc.tensor.matmul(ps[:, b, 256:384], q[:, 0:P], k[:, 0:P], start=True, stop=True).then_inc(*mla_p.inc("scores", hd))
                    hd = i - LAG_T
                    if 0 <= hd < MH:
                        pe.wait_ge(*mla_g.at("probs", hd))
                        if hd >= 2:
                            pe.wait_ge(*mla_a.at("probs", hd - 2))
                        for n in range(3):
                            mm = nc.tensor.transpose(ps[:, hd % 2, n * P:(n + 1) * P], msc[:, hd % 6, n * P:(n + 1) * P], ident)
                        mm.then_inc(*mla_p.inc("probs", hd))
                    hd = i - LAG_V
                    if 0 <= hd < MH:
                        pe.wait_ge(*mla_a.at("probs", hd))
                        if hd % 2 == 0 and hd >= 4:
                            pe.wait_ge(*mla_a.at("out", hd // 2 - 2))
                        r, b, q = slice(64 * (hd % 2), 64 * (hd % 2) + 64), 2 + hd // 2 % 2, mpb[:, hd % 2]
                        nc.tensor.matmul(ps[r, b, P:2 * P], vtk[:, 0, hd], q[:, 0:P], start=True, stop=False)
                        nc.tensor.matmul(ps[r, b, P:2 * P], vtk[:, 1, hd], q[:, P:2 * P], start=False, stop=True)
                        nc.tensor.matmul(ps[r, b, 0:P], vtk[:, 0, hd], q[:, 2 * P:3 * P], start=True, stop=True).then_inc(*mla_p.inc("out", hd))
                pe.wait_ge(*mla_a.at("out", MH // 2 - 1))
                project_tokens("mla_o", moT, "mla")

            norm("ffn1")
            ffn("ffn1")
            pe.wait_ge(tab_in.sem, 32)
            pe.wait_ge(*zeros.at("tab"))
            pe.wait_ge(*h_ready.at("mix1", 1))
            nc.tensor.matmul(ps[0:AH, 3, 0:384], tab[:], hot[:], start=True, stop=True).then_inc(*bias_p.inc("t"))
            norm("mix1")
            mix1()
            norm("ffn2")
            ffn("ffn2")
            ple("ple1", 0)
            hyb()
            norm("conv0")
            ffn("conv0")
            ple("ple20", 1)
            mla()
            norm("conv1")
            ffn("conv1")
            ple("ple21", 2)

        @block.scalar
        def _(act):
            def step(ins):
                ins.then_inc(*act_step.inc(act_step.count))
                act.wait_ge(*act_step.last())

            act.dma_start(first_rows, I["norm_ffn1"][0].rearrange("(r c) -> r c", c=P)).then_inc(first_in.sem, 16)

            def norm(n, gain):
                for t in range(TT):
                    if n == "ffn1":
                        act.wait_ge(*x_in.at("x"))
                    else:
                        act.wait_ge(*h_ready.at(n, t))
                    nc.scalar.activation(hn[:, t], h[:, t], ACT.Square, accum_out=ssq[:, t:t + 1]).then_inc(*squared.inc(n, t))
                act.wait_ge(*rstd_ready.at(n, 1))
                nc.scalar.activation(hn[:, 1, D // 2:], h[:, 1, D // 2:], ACT.Copy, scale=rstd[:, 1:2]).then_inc(*scaled_a.inc(n))
                for k in range(KD // 2, KD):
                    if k % 2 == 0:
                        act.wait_ge(*turned.at(n, k // 2))
                    ins = nc.scalar.activation((x_hi if n in SPLIT else xT)[:, k], ps[:, 4 + k // 2, k % 2 * SEQ:(k % 2 + 1) * SEQ], ACT.Copy,
                                               scale=col(gain, k))
                ins.then_inc(*(x_hi_a if n in SPLIT else x_a).inc(n))

            def split_hidden(f, g, i, *event):
                if f.startswith("conv"):
                    act.wait_ge(*conv_out.at_group(i, f, g))
                    nc.scalar.activation(gatev[:, g % 2], gluT[:, g % 2], ACT.Gelu).then_inc(*gate_act.inc(f, *event))
                act.wait_ge(*hid_ready.at_group(i, f, g))
                nc.scalar.activation(hid_hi[:, g % 2], hidT[:, g % 2], ACT.Copy).then_inc(*hid_hi_ready.inc(f, *event))

            def split_weights(f, g, i=None, which=slice(0, None)):
                for kind, of in split_steps(g)[which]:
                    raw, hi, _ = split_views(f, kind, of)
                    c = ffn_chunk(kind, of)
                    wait_weights(act, (f, c), i)
                    if c >= HI_BAYS:
                        act.wait_ge(*used_up_to((f, c - HI_BAYS), i))
                    nc.scalar.activation(hi, raw, ACT.Copy).then_inc(*w_hi_ready.inc(f, g, kind, of - g))
                    if g and kind == "up":
                        split_hidden(f, g - 1, i, g, "before")

            def ffn(f, conv, between=None):
                def group(g, i=None):
                    if g:
                        split_weights(f, g, i)
                    act.wait_ge(*used_up_to((f, ffn_chunk("up", g)), i))
                    gate = ps[:, 4 + 2 * (g % 2):6 + 2 * (g % 2), 0:SEQ]
                    if not conv:
                        if g >= 2:
                            act.wait_ge(*hid_ready.at_group(i, f, g - 2))
                        nc.scalar.activation(gatev[:, g % 2], gate, ACT.Sigmoid).then_inc(*gate_act.inc(f, g))
                    else:
                        gin = ps[:, 4 + 2 * (g % 2):6 + 2 * (g % 2), SEQ:2 * SEQ]
                        if g >= 2:
                            act.wait_ge(*hid_ready.at_group(i, f, g - 2))
                        nc.scalar.activation(gpad[:, g % 2, :, 2:2 + SEQ], gin, ACT.Copy).then_inc(*gate_act.inc(f, g))

                group(0)
                group(1)
                if between:
                    between()
                with act.Fori(0, ROUNDS) as i:
                    since = [(s, s.count) for s in (gate_act, w_hi_ready, hid_hi_ready)]
                    group(2, i)
                    group(3, i)
                    for s, c in since:
                        s.repeated(f, c, ROUNDS)
                group(GROUPS - 1)
                split_hidden(f, GROUPS - 1, None, "last")

            def keep(dst, b, key, *event, c=slice(0, 512), func=ACT.Copy):
                act.wait_ge(*used_up_to(key))
                src = ps[:, b, c]
                if len(dst.shape) == 3:
                    src = src.rearrange("p (a b) -> p a b", a=dst.shape[1])
                nc.scalar.activation(dst, src, func).then_inc(*proj_a.inc(*event))

            def bias_out():
                act.wait_ge(*lb_d.at("logit"))
                nc.scalar.activation(lbc[:], lbd[:], ACT.Sigmoid).then_inc(*lb_a.inc("lb"))
                act.wait_ge(*bias_d.at("t"))
                act.dma_start(scratch, tabd[:].unsqueeze(1).to_broadcast([AH, P, 384])).then_inc(tab_out.sem, 16)

            def mix1():
                for n in range(2):
                    keep(fT[:, 2 * n:2 * n + 2], n, ("rf", n), "rf", n, func=ACT.Sigmoid)
                act.wait_ge(tab_out.sem, 16)
                shifted = [bass.AP(tensor=scratch.tensor, offset=127 + o, ap=[[383, P], [384 * P, AH], [1, n]]) for o, n in ((0, 256), (P, P))]
                act.dma_start(bias[:, :, 0:256], shifted[0]).then_inc(bias_in.sem, 16)
                act.dma_start(bias[:, :, 256:384], shifted[1]).then_inc(bias_in.sem, 16)
                for n in range(2):
                    keep(vR[:, :, n * 256:(n + 1) * 256], n, ("ri", n), "ri", n)
                act.wait_ge(*rec_d.at("f"))
                nc.scalar.activation(bT[:], fT[:], ACT.Ln).then_inc(*rec_a.inc("log"))
                act.wait_ge(*proj_d.at("akT"))
                act.dma_start(akT[0:64, 1], akT[64:P, 0]).then_inc(ak_swapped.sem, 16)
                act.dma_start(akT[64:P, 1], akT[0:64, 0]).then_inc(ak_swapped.sem, 16)
                for n in range(2):
                    keep(sgT[:, 2 * n:2 * n + 2], 1 + n, ("rg", n), "rg", n)
                act.wait_ge(*att_d.at("minus_max"))
                nc.scalar.activation(esink[:], esink[:], ACT.Exp).then_inc(*att_a.inc("sink"))
                for hd in range(AH):
                    for n, c in enumerate((slice(0, 256), slice(256, 384))):
                        ins = nc.scalar.activation(sc[:, hd, c], sc[:, hd, c], ACT.Exp, bias=nmx[:, hd, n:n + 1], accum_out=den[:, hd, n:n + 1])
                    ins.then_inc(*att_a.inc("exp", hd))
                for n in range(len(LV)):
                    act.wait_ge(*rec_g.at("differences", n))
                    nc.scalar.activation(zT[:, n % 2], zT[:, n % 2], ACT.Exp).then_inc(*rec_a.inc("decay", n))
                    keep(gT[:, 2 * n:2 * n + 2], (3 + n) % 4, ("g", n), "g", n)
                act.wait_ge(*proj_a.last())
                nc.scalar.activation(sgT[:], sgT[:], ACT.Sigmoid).then_inc(*att_a.inc("gate_r"))
                nc.scalar.activation(gT[:], gT[:], ACT.Sigmoid).then_inc(*att_a.inc("gates"))
                for hd in range(2):
                    turned_probs(hd)
                for t in range(TT):
                    act.wait_ge(*rec_p.at("out", t))
                    if t == 0:
                        act.wait_ge(*rec_d.at("placed", len(LV)))
                    nc.scalar.activation(osq[:, t], ps[:, 6 + t], ACT.Square).then_inc(*rec_a.inc("squares", t))
                for hd in range(2, AH):
                    turned_probs(hd)

            def turned_probs(hd):
                act.wait_ge(*att_p.at("turned", hd))
                if hd >= 3:
                    act.wait_ge(*att_p.at("out", hd - 3))
                nc.scalar.activation(pbT[:, hd % 3], ps[:, 4 + hd % 2, 0:384], ACT.Copy).then_inc(*att_a.inc("turned", hd))

            def ple(stage, gain, normed):
                def split_gate(n):
                    key = (f"{stage}_gate", n)
                    raw, hi, _ = ple_views(key)
                    wait_weights(act, key)
                    act.wait_ge(*used_up_to((f"{stage}_gate", 0) if n == 3 else (FFN_BEFORE[stage], 3 * GROUPS - 3 + n)))
                    nc.scalar.activation(hi, raw, ACT.Copy).then_inc(*w_hi_ready.inc(key))

                split_gate(0)
                split_gate(1)
                norm(stage, gain)
                split_gate(2)
                split_gate(3)
                if normed:
                    act.wait_ge(*used_up_to((f"{stage}_proj", 0)))
                    for t in range(TT):
                        ins = nc.scalar.activation(pscr[:, t], ps[:, 2 * t:2 * t + 2].rearrange("p a b -> p (a b)"), ACT.Square,
                                                   accum_out=ssq[:, 2 + t:3 + t])
                    ins.then_inc(*ple_a.inc(stage, "squares"))
                for t in range(TT):
                    act.wait_ge(*(acc_ready.at(stage, 0) if t == 0 else used_up_to((f"{stage}_gate", 3))))
                    nc.scalar.activation(pgate[:, t], ps[:, 4 + 2 * t:6 + 2 * t].rearrange("p a b -> p (a b)"), ACT.Sigmoid).then_inc(*ple_a.inc(stage, t))

            def squares_of_h(n):
                for t in range(TT):
                    act.wait_ge(*h_ready.at(n, t))
                    nc.scalar.activation(hn[:, t], h[:, t], ACT.Square, accum_out=ssq[:, t:t + 1]).then_inc(*squared.inc(n, t))

            def hyb():
                norm("hyb", "attn_norm0")

                def keep_rw(key, tile, b, tiles=2, rows=P):
                    act.wait_ge(*used_up_to(key))
                    if key == ("wk", 0):
                        act.wait_ge(*mix_g.at("zero"))
                    nc.scalar.activation(pfT[0:rows, tile:tile + tiles, 1:], ps[0:rows, b, 0:tiles * SEQ].rearrange("p (a b) -> p a b", a=tiles),
                                         ACT.Copy).then_inc(*rw_in.inc(key))

                def keep_stick(name, n, b, dst, scale=1.0):
                    act.wait_ge(*used_up_to((name, n)))
                    src = ps[:, b].rearrange("p (a b) -> p a b", a=2)
                    nc.scalar.activation(dst, src, ACT.Copy, scale=scale).then_inc(*stick_in.inc(name, n))

                keep_rw(("wk", 0), 4, 0)
                keep_rw(("wk", 1), 6, 1)
                keep_rw(("wr", 0), 0, 2)
                keep_rw(("wr", 1), 2, 3)
                keep_rw("lora_in", 12, 0)
                keep_rw("lora_in_tail", 14, 1, 1, 32)
                act.wait_ge(*mix_d.at("lora_in"))
                nc.scalar.activation(xm[0:64, 12], xm[0:64, 12], ACT.Tanh).then_inc(*pre_a.inc("tanh"))
                nc.scalar.activation(xm[:, 13], xm[:, 13], ACT.Sigmoid)
                act.wait_ge(*mix_d.at("lora_in_tail"))
                nc.scalar.activation(xm[0:32, 14], xm[0:32, 14], ACT.Sigmoid)
                keep_rw(("wv", 0), 8, 2)
                keep_rw(("wv", 1), 10, 3)
                keep_stick("sq", 0, 0, qaT[:, 0:2], 0.125)
                act.wait_ge(*mix_d.at(("wv", 1)))
                for key, dst, b, bias_name, event in (("w2", lw, 4, "w0", "decay"), ("a2", aT, 6, "a0", "rate")):
                    act.wait_ge(*used_up_to(key))
                    for j in range(RWT):
                        ins = nc.scalar.activation(dst[:, j], ps[:, b + j // 2, j % 2 * SEQ:(j % 2 + 1) * SEQ], ACT.Sigmoid, bias=col(bias_name, j))
                    ins.then_inc(*pre_a.inc(event))
                keep_stick("sq", 1, 1, qaT[:, 2:4], 0.125)
                act.wait_ge(*pre_d.at("kk_sums"))
                nc.scalar.activation(ktmp[:], ktmp[:], ACT.Sqrt).then_inc(*pre_a.inc("kk_norm"))
                keep_stick("sk", 0, 2, kaT[:, 0:2])
                act.wait_ge(*pre_d.at("dm"))
                nc.scalar.activation(cc[:], dm[:], ACT.Exp, scale=KAPPA)
                nc.scalar.activation(dm[:], dm[:], ACT.Exp, scale=-KAPPA)
                nc.scalar.activation(dm0[:], dm0[:], ACT.Exp, scale=-KAPPA)
                nc.scalar.activation(sfac[:], sfac[:], ACT.Exp, scale=-KAPPA).then_inc(*pre_a.inc("exps"))
                keep_stick("sk", 1, 3, kaT[:, 2:4])
                act.wait_ge(*pre_p.at("v_turned"))
                nc.scalar.activation(vtok[:], ps[:, 6:8], ACT.Copy).then_inc(*pre_a.inc("vtok"))
                keep_stick("sv", 0, 0, va[:, :, 0:256])
                keep_stick("sv", 1, 1, va[:, :, 256:512])
                act.wait_ge(*pre_p.at("bk_turned"))
                nc.scalar.activation(hn[:, 1], ps[:, 6:8].rearrange("p a b -> p (a b)"), ACT.Copy).then_inc(*pre_a.inc("bk_turned"))

                def stick_softplus(g):
                    act.wait_ge(*stick_p.at("scores", g))
                    z = ps[:, 4 + 2 * (g % 2):6 + 2 * (g % 2), 0:384]
                    s = lsp[:, g % 2]
                    step(nc.scalar.activation(s, z, ACT.Abs))
                    step(nc.scalar.activation(s, s, ACT.Exp, scale=-1.0))
                    nc.scalar.activation(s, s, ACT.Ln, bias=1.0).then_inc(*stick_a.inc("log", g))

                def stick_weights(g):
                    act.wait_ge(*stick_p.at("sums", g))
                    nc.scalar.activation(wst[:, g % 2], ps[:, 4 + 2 * (g % 2):6 + 2 * (g % 2), 0:384], ACT.Exp).then_inc(*stick_a.inc("weights", g))

                def stick_keep(g):
                    act.wait_ge(*stick_p.at("out", g))
                    nc.scalar.activation(oaT[:, g], ps[:, 4 + 2 * (g % 2), 0:256], ACT.Copy).then_inc(*stick_a.inc("out", g))

                def level(n):
                    for g in range(4):
                        act.wait_ge(*inv_p.at("M1", n, g))
                        nc.scalar.activation(M1[:, g], ps[:, g].rearrange("p (a b) -> p a b", a=4), ACT.Copy).then_inc(*inv_a.inc("M1", n, g))

                stick_softplus(0)
                level(1)
                stick_softplus(1)
                level(2)
                stick_weights(0)
                stick_keep(0)
                stick_weights(1)
                stick_softplus(2)
                level(3)
                stick_keep(1)
                stick_softplus(3)
                stick_weights(2)
                level(4)
                stick_keep(2)
                stick_weights(3)
                level(5)
                stick_keep(3)
                level(6)
                for c in range(2):
                    act.wait_ge(*sol_p.at("rhs", c))
                    for n in range(2):
                        ins = nc.scalar.activation(rs[:, n], ps[:, 4 + n, 0:256].rearrange("p (a b) -> p a b", a=4), ACT.Copy)
                    ins.then_inc(*sol_a.inc("rhs", c))
                    act.wait_ge(*sol_p.at("u", c))
                    nc.scalar.activation(us[:].rearrange("p a b c -> p (a b c)"), ps[:, 6], ACT.Copy).then_inc(*sol_a.inc("u", c))
                    act.wait_ge(*sol_p.at("y", c))
                    for n in range(2):
                        dst = yv[:, c].rearrange("p (a b) e -> p b a e", b=2)[:, n]
                        ins = nc.scalar.activation(dst, ps[:, 4 + n, 0:256].rearrange("p (a b) -> p a b", a=4), ACT.Copy)
                    ins.then_inc(*sol_a.inc("y", c))
                act.wait_ge(*sol_d.at("centred"))
                nc.scalar.activation(ysq[:], yv[:], ACT.Square).then_inc(*sol_a.inc("squares"))

            def rotary_cos_sin():
                act.wait_ge(*rot_d.at("angles"))
                nc.scalar.activation(cosv[:], cosv[:], ACT.Sin)
                nc.scalar.activation(sinv[:], sinv[:], ACT.Sin).then_inc(*rot_a.inc("rot"))

            def mla():
                norm("mla", "attn_norm1")
                act.wait_ge(*used_up_to(("down", 1)))
                nc.scalar.activation(ctok[:, :, 0:512], ps[:, 0:2], ACT.Copy)
                act.wait_ge(*used_up_to(("down", 2)))
                step(nc.scalar.activation(ctok[:, :, 512:672], ps[:, 2:4, 0:160], ACT.Copy))
                for t in range(TT):
                    nc.scalar.activation(mlsq[:, t, 0:384], ctok[:, t, 0:384], ACT.Square, accum_out=ssq[:, t:t + 1])
                    ins = nc.scalar.activation(mlsq[:, t, 384:640], ctok[:, t, 384:640], ACT.Square, accum_out=ssq[:, 2 + t:3 + t])
                ins.then_inc(*lat_a.inc("squares"))
                act.wait_ge(*lat_p.at("turned"))
                nc.scalar.activation(clT[:, 4], ps[:, 6, 0:SEQ], ACT.Copy, scale=col("kv_norm", 1)).then_inc(*lat_a.inc("kv"))
                keep_up(act, 0)
                for i in range(MH + LAG_V):
                    if i < MH and i % 2 == 0:
                        act.wait_ge(*mla_p.at("turned", i))
                        if i >= 3:
                            act.wait_ge(*mla_p.at("scores", i - 3))
                        nc.scalar.activation(qkT[0:QH, i % 3].rearrange("p a b -> p (a b)"), ps[0:QH, 4 + i % 2], ACT.Copy).then_inc(*mla_a.inc("turned", i))
                    hd = i - LAG_T
                    if 0 <= hd < MH:
                        act.wait_ge(*mla_p.at("probs", hd))
                        if hd >= 2:
                            act.wait_ge(*mla_p.at("out", hd - 2))
                        nc.scalar.activation(mpb[:, hd % 2], ps[:, hd % 2, 0:384], ACT.Copy).then_inc(*mla_a.inc("probs", hd))
                    hd = i - LAG_S
                    if 0 <= hd < MH:
                        act.wait_ge(*mla_d.at("minus_max", hd))
                        for n, c in enumerate((slice(0, 256), slice(256, 384))):
                            s = msc[:, hd % 6, c]
                            ins = nc.scalar.activation(s, s, ACT.Exp, bias=mmax[:, hd % 6, n:n + 1], scale=MSCALE, accum_out=mden[:, hd % 6, n:n + 1])
                        ins.then_inc(*mla_a.inc("exp", hd))
                    hd = i - LAG_V
                    if hd >= 0 and hd % 2:
                        act.wait_ge(*mla_p.at("out", hd))
                        nc.scalar.activation(moT[:, hd // 2], ps[:, 2 + hd // 2 % 2, 0:256], ACT.Copy).then_inc(*mla_a.inc("out", hd // 2))

            act.wait_ge(*cols_ready.at("first"))
            split_weights("ffn1", 0, which=slice(0, 1))
            norm("ffn1", "norm_ffn1")
            split_weights("ffn1", 0, which=slice(1, None))
            ffn("ffn1", False)
            norm("mix1", "norm_mix")
            bias_out()
            mix1()
            act.wait_ge(*used_up_to(("mix_out", 0)))
            split_weights("ffn2", 0)
            norm("ffn2", "norm_ffn2")
            ffn("ffn2", False, between=rotary_cos_sin)
            ple("ple1", "norm_ple", False)
            squares_of_h("block1")
            hyb()
            act.wait_ge(*used_up_to(("hyb_out", 0)))
            split_weights("conv0", 0)
            norm("conv0", "conv_norm0")
            ffn("conv0", True)
            act.dma_start(row_gain[:, 0], I["ple_norm_2"][1].partition_broadcast(P)).then_inc(gains_in.sem, 16)
            ple("ple20", "ple_gate_norm0", True)
            act.wait_ge(*ple_d.at("ple20", "e"))
            act.wait_ge(gains_in.sem, 48)
            act.dma_start(row_gain[:, 1], I["final_norm_2"].partition_broadcast(P)).then_inc(gains_in.sem, 16)
            mla()
            act.wait_ge(*used_up_to(("mla_o", 0)))
            split_weights("conv1", 0)
            norm("conv1", "conv_norm1")
            ffn("conv1", True)
            ple("ple21", "ple_gate_norm1", True)
            squares_of_h("all")
            for t in range(TT):
                act.wait_ge(*h_ready.at("out", t))
                act.dma_start(out[0, t * P:(t + 1) * P, :], h[:, t]).then_inc(stored.sem, 16)
            act.wait_ge(stored.sem, 16 * TT)

        @block.gpsimd
        def _(pool):
            def step(ins):
                ins.then_inc(*pool_step.inc(pool_step.count))
                pool.wait_ge(*pool_step.last())

            nc.gpsimd.memset(stack[:], 0.0).then_inc(*zeros.inc("stack"))
            nc.gpsimd.memset(minus_half[:], -0.5).then_inc(*zeros.inc("half"))
            nc.gpsimd.memset(gpad[:, :, :, 0:2], 0.0).then_inc(*zeros.inc("gpad"))
            pool.wait_ge(*zeros.last())
            nc.gpsimd.memset(tab[N_BUCKETS:N_BUCKETS + 1, :], NEG).then_inc(*zeros.inc("tab"))
            pool.wait_ge(*zeros.last())
            nc.gpsimd.memset(ones[:], 1.0).then_inc(*zeros.inc("ones"))
            pool.wait_ge(*zeros.last())

            def power(n, width):
                if width == TT and n not in ("block1", "all"):
                    for t in range(TT):
                        pool.wait_ge(*mean_ready.at(n, t))
                        nc.gpsimd.tensor_tensor(rstd[:, t:t + 1], msq[:, t:t + 1], minus_half[:, t:t + 1], ALU.pow).then_inc(*rstd_ready.inc(n, t))
                    return
                pool.wait_ge(*mean_ready.at(n))
                nc.gpsimd.tensor_tensor(rstd[:, 0:width], msq[:, 0:width], minus_half[:, 0:width], ALU.pow).then_inc(*rstd_ready.inc(n))

            def split_ffn(f):
                def group(g, i=None, which=slice(0, None)):
                    for kind, of in split_steps(g)[which]:
                        if kind == "out":
                            continue
                        raw, hi, lo = split_views(f, kind, of)
                        pool.wait_ge(*w_hi_ready.at_group(i, f, g, kind, of - g))
                        nc.gpsimd.tensor_tensor(lo, raw, hi, ALU.subtract).then_inc(*w_lo_g.inc(f, g, kind, of - g))

                before_norm = 1 if f == "ffn1" else 3
                group(0, which=slice(0, before_norm))
                power(f, 2)
                group(0, which=slice(before_norm, None))
                group(1)
                with pool.Fori(0, ROUNDS) as i:
                    since = w_lo_g.count
                    group(2, i)
                    group(3, i)
                    w_lo_g.repeated(f, since, ROUNDS)
                group(GROUPS - 1)

            def mix1():
                pool.wait_ge(*mean_ready.at("mix1", 1))
                pool.wait_ge(*bias_p.at("t"))
                nc.gpsimd.memset(AT[:], 0.0).then_inc(*rec_g.inc("zero"))
                for n, m in enumerate(LV):
                    z = zT[:, n % 2].rearrange("p a s -> p (a s)").rearrange("p (b m) -> p b m", m=2 * m)
                    b = bT.rearrange("p a s -> p (a s)").rearrange("p (b m) -> p b m", m=2 * m)
                    mid = b[:, :, m - 1:m].to_broadcast([P, RH * SEQ // (2 * m), m])
                    if n == 0:
                        pool.wait_ge(*rec_d.at("sums"))
                    if n >= 2:
                        pool.wait_ge(*rec_p.at("scores", n - 1))
                    nc.gpsimd.tensor_tensor(z[:, :, 0:m], mid, b[:, :, 0:m], ALU.subtract)
                    nc.gpsimd.tensor_tensor(z[:, :, m:2 * m], b[:, :, m:2 * m], mid, ALU.subtract).then_inc(*rec_g.inc("differences", n))

            def power2(n):
                pool.wait_ge(*mean_ready.at(n, "e"))
                nc.gpsimd.tensor_tensor(rstd[:, 2:4], msq[:, 2:4], minus_half[:, 2:4], ALU.pow).then_inc(*rstd_ready.inc(n, "e"))

            def split_gate(stage, *which):
                for n in which:
                    key = (f"{stage}_gate", n)
                    raw, hi, lo = ple_views(key)
                    pool.wait_ge(*w_hi_ready.at(key))
                    nc.gpsimd.tensor_tensor(lo, raw, hi, ALU.subtract).then_inc(*w_lo_g.inc(key))

            def hyb():
                pool.wait_ge(*h_ready.at("hyb", 1))
                nc.gpsimd.memset(pfT[:, :, 0:1], 0.0).then_inc(*mix_g.inc("zero"))
                for key, tile, tiles, rows in MIXES:
                    pool.wait_ge(*rw_in.at(key))
                    t = slice(tile, tile + tiles)
                    nc.gpsimd.tensor_tensor(xm[0:rows, t], pfT[0:rows, t, 0:SEQ], pfT[0:rows, t, 1:], ALU.subtract).then_inc(*mix_g.inc(key))

                pool.wait_ge(*pre_d.at("bonus"))
                nc.gpsimd.memset(G[:].rearrange("p a b c d -> p (a b c d)"), 0.0).then_inc(*mix_g.inc("G"))

                def before(t, *event):
                    for n in range(2):
                        tiles = t[:, n].rearrange("p (b c) -> p b c", b=3)[:, 0::2, :]
                        ins = nc.gpsimd.affine_select(out=tiles, in_=tiles, compare_op=ALU.is_gt, fill=0.0, base=0,
                                                      pattern=[[0, 2], [1, P]], channel_multiplier=-1)
                    ins.then_inc(*stick_g.inc(*event))

                def softplus(g):
                    pool.wait_ge(*stick_d.at("softplus", g))
                    before(lsp[:, g % 2], "softplus", g)

                def weights(g):
                    pool.wait_ge(*stick_a.at("weights", g))
                    before(wst[:, g % 2], "weights", g)

                softplus(0)
                softplus(1)
                weights(0)
                weights(1)
                softplus(2)
                weights(2)
                softplus(3)
                weights(3)

            def mla():
                for hd in range(MH):
                    pool.wait_ge(*mla_d.at("inverse_sum", hd))
                    for n, c in enumerate((slice(0, 256), slice(256, 384))):
                        s = msc[:, hd % 6, c]
                        ins = nc.gpsimd.tensor_scalar(s, s, mden[:, hd % 6, n:n + 1], None, ALU.mult)
                    ins.then_inc(*mla_g.inc("probs", hd))

            split_ffn("ffn1")
            pool.wait_ge(consts_in.sem, 16 * N_CONSTS)
            nc.gpsimd.tensor_copy(masks[:], mask_rows).then_inc(*masks_ready.inc())
            pool.wait_ge(*masks_ready.at())
            power("mix1", 2)
            mix1()
            power("rec", 8)
            split_ffn("ffn2")
            split_gate("ple1", 0, 1)
            power("ple1", 2)
            split_gate("ple1", 3)
            power("block1", 2)
            power("hyb", 2)
            hyb()
            power("gn", 16)
            split_ffn("conv0")
            split_gate("ple20", 0, 1)
            power("ple20", 2)
            power2("ple20")
            split_gate("ple20", 3)
            power("mla", 2)
            power("latent", 4)
            mla()
            split_ffn("conv1")
            split_gate("ple21", 0, 1)
            power("ple21", 2)
            power2("ple21")
            split_gate("ple21", 3)
            power("all", 2)

        @block.vector
        def _(dve):
            v = nc.vector

            def step(ins):
                ins.then_inc(*dve_step.inc(dve_step.count))
                dve.wait_ge(*dve_step.last())

            dve.wait_ge(*cols_turned.at("first"))
            v.tensor_copy(first_gains[:], ps[:, 0, 0:KD]).then_inc(*cols_ready.inc("first"))
            dve.wait_ge(*cols_ready.at("first"))

            def keep_small_inputs():
                dve.wait_ge(*cols_turned.at("cols"))
                v.tensor_copy(cols[:], ps[:, 4, 0:3 * P]).then_inc(*cols_ready.inc("cols"))
                dve.wait_ge(*cols_turned.at("p"))
                v.tensor_copy(pT[:].rearrange("p n k s -> p n (k s)"), ps[:, 5:8]).then_inc(*cols_ready.inc("p"))
                dve.wait_ge(*cols_ready.at("p"))

            def norm(n, gain):
                for t in range(TT):
                    dve.wait_ge(*squared.at(n, t))
                    v.tensor_scalar(msq[:, t:t + 1], ssq[:, t:t + 1], 1.0 / D, EPS, ALU.mult, ALU.add).then_inc(*mean_ready.inc(n, t))
                    dve.wait_ge(*rstd_ready.at(n, t))
                    c = slice(0, D if t == 0 else D // 2)
                    v.tensor_scalar(hn[:, t, c], h[:, t, c], rstd[:, t:t + 1], None, ALU.mult).then_inc(*scaled_d.inc(n, t))
                for k in range(KD // 2):
                    if k % 2 == 0:
                        dve.wait_ge(*turned.at(n, k // 2))
                    ins = v.tensor_scalar((x_hi if n in SPLIT else xT)[:, k], ps[:, 4 + k // 2, k % 2 * SEQ:(k % 2 + 1) * SEQ], col(gain, k), None, ALU.mult)
                ins.then_inc(*(x_hi_d if n in SPLIT else x_d).inc(n))
                if n in SPLIT:
                    dve.wait_ge(*x_hi_d.at(n))
                    for k in range(KD):
                        if k == KD // 2:
                            dve.wait_ge(*x_hi_a.at(n))
                        ins = v.scalar_tensor_tensor(x_lo[:, k], ps[:, 4 + k // 2, k % 2 * SEQ:(k % 2 + 1) * SEQ], col(gain, k), x_hi[:, k],
                                                     ALU.mult, ALU.subtract)
                        if k % 2:
                            ins.then_inc(*x_lo_d.inc(n, k // 2))

            def residual(key, scale, after):
                for t in range(TT):
                    if t == 0:
                        dve.wait_ge(*acc_ready.at(key, 0))
                    else:
                        dve.wait_ge(*used_up_to(after))
                    for half in range(2):
                        part = h[:, t, half * 512:(half + 1) * 512]
                        ins = v.scalar_tensor_tensor(part, bank(2 * t + half), scale, part, ALU.mult, ALU.add)
                    ins.then_inc(*h_ready.inc(key_after(key), t))

            def rest_of_hidden(f, g, i, *event):
                wait_hidden(dve, hid_hi_ready, f, g, i)
                v.tensor_tensor(hid_lo[:, g % 2], hidT[:, g % 2], hid_hi[:, g % 2], ALU.subtract).then_inc(*hid_lo_ready.inc(f, *event))

            def ffn(f, conv, between=None):
                def group(g, i=None):
                    if g:
                        rest_of_hidden(f, g - 1, i, g, "before")
                    for kind, of in split_steps(g):
                        if kind == "out":
                            raw, hi, lo = split_views(f, kind, of)
                            dve.wait_ge(*w_hi_ready.at_group(i, f, g, kind, of - g))
                            v.tensor_tensor(lo, raw, hi, ALU.subtract).then_inc(*w_lo_d.inc(f, g, kind, of - g))
                    two = slice(4 + 2 * (g % 2), 6 + 2 * (g % 2))
                    s = g % 2
                    first, second = ps[:, two, 0:SEQ], ps[:, two, SEQ:2 * SEQ]
                    if g >= 2:
                        dve.wait_ge(*used_up_to((f, ffn_chunk("out", g - 2)), i))
                    dve.wait_ge(*gate_act.at_group(i, f, g))
                    if not conv:
                        v.tensor_tensor(gluT[:, s], first, gatev[:, s], ALU.mult).then_inc(*conv_out.inc(f, g))
                        dve.wait_ge(*conv_out.at_group(i, f, g))
                        v.tensor_tensor(hidT[:, s], gluT[:, s], second, ALU.mult).then_inc(*hid_ready.inc(f, g))
                        return
                    layer = f[-1]

                    def tap(name, j):
                        c = column[name] + 2 * g + j
                        return cols[:, c:c + 1] if i is None else cols[:, bass.ds(i * 4 + c, 1)]

                    for n, j in enumerate(range(2)):
                        v.tensor_scalar(glu2[:, s, j], gpad[:, s, j, 2:2 + SEQ], tap(f"conv_w{layer}2", j),
                                        tap(f"conv_b{layer}", j), ALU.mult, ALU.add).then_inc(*conv_out.inc(f, g, j, 0))
                    for j in range(2):
                        dve.wait_ge(*conv_out.at_group(i, f, g, j, 0))
                        v.scalar_tensor_tensor(gluT[:, s, j], gpad[:, s, j, 1:1 + SEQ], tap(f"conv_w{layer}1", j),
                                               glu2[:, s, j], ALU.mult, ALU.add).then_inc(*conv_out.inc(f, g, j, 1))
                    for j in range(2):
                        dve.wait_ge(*conv_out.at_group(i, f, g, j, 1))
                        ins = v.scalar_tensor_tensor(gluT[:, s, j], gpad[:, s, j, 0:SEQ], tap(f"conv_w{layer}0", j),
                                                     gluT[:, s, j], ALU.mult, ALU.add)
                    ins.then_inc(*conv_out.inc(f, g))
                    wait_hidden(dve, gate_act, f, g, i)
                    v.tensor_tensor(hidT[:, s], gatev[:, s], first, ALU.mult).then_inc(*hid_ready.inc(f, g))

                group(0)
                group(1)
                if between:
                    between()
                with dve.Fori(0, ROUNDS) as i:
                    since = [(s, s.count) for s in (conv_out, hid_ready, hid_lo_ready, w_lo_d)]
                    group(2, i)
                    group(3, i)
                    for s, c in since:
                        s.repeated(f, c, ROUNDS)
                group(GROUPS - 1)
                rest_of_hidden(f, GROUPS - 1, None, "last")
                if f == "ffn1":
                    keep_small_inputs()
                residual(f, 1.0 if conv else 0.5, (f, 3 * GROUPS - 1))

            def keep(dst, b, key, *event, c=slice(0, 512), scale=None):
                dve.wait_ge(*used_up_to(key))
                src = ps[:, b, c]
                if len(dst.shape) == 3:
                    src = src.rearrange("p (a b) -> p a b", a=dst.shape[1])
                if scale is None:
                    v.tensor_copy(dst, src).then_inc(*proj_d.inc(*event))
                else:
                    v.tensor_scalar(dst, src, scale, None, ALU.mult).then_inc(*proj_d.inc(*event))

            def mix1():
                dve.wait_ge(*masks_ready.at())
                for n in range(2):
                    dve.wait_ge(*proj_a.at("rf", n))
                    if n == 0:
                        dve.wait_ge(*lb_d.at("one_minus"))
                    for hd in (2 * n, 2 * n + 1):
                        ins = v.tensor_scalar(fT[:, hd], fT[:, hd], omlb[:, hd:hd + 1], lbc[:, hd:hd + 1], ALU.mult, ALU.add)
                ins.then_inc(*rec_d.inc("f"))
                for n in range(2):
                    keep(rqT[:, 2 * n:2 * n + 2], 2 + n, ("rq", n), "rq", n)
                dve.wait_ge(*rec_d.at("f"))
                v.tensor_scalar(kT[:], fT[:], -1.0, 1.0, ALU.mult, ALU.add).then_inc(*rec_d.inc("q_and_k"))
                dve.wait_ge(*rec_a.at("log"))
                dve.wait_ge(*zeros.at("ones"))
                dve.wait_ge(*rec_d.at("q_and_k"))
                for hd in range(RH):
                    ins = v.tensor_tensor_scan(fT[:, hd], ones[:], bT[:, hd], 0.0, ALU.mult, ALU.add)
                ins.then_inc(*rec_d.inc("scan"))
                for n in range(2):
                    keep(aqT[:, 2 * n:2 * n + 2], 2 + n, ("aq", n), "aq", n, scale=0.125)
                dve.wait_ge(*rec_d.at("scan"))
                v.tensor_copy(bT[:], fT[:]).then_inc(*rec_d.inc("sums"))
                dve.wait_ge(*used_up_to("akv"))
                v.tensor_copy(akT[:, 0], ps[:, 0, 0:SEQ]).then_inc(*proj_d.inc("akT"))
                keep(av[:], 0, "akv", "akv", c=slice(256, 512))
                dve.wait_ge(bias_in.sem, 32)
                for hd in range(AH):
                    dve.wait_ge(*att_p.at("scores", hd))
                    v.tensor_tensor(sc[:, hd], ps[:, 4 + hd % 4, 0:384], bias[:, hd], ALU.add).then_inc(*att_d.inc("biased", hd))
                    dve.wait_ge(*att_d.at("biased", hd))
                    v.tensor_reduce(mx[:, hd, 0:1], sc[:, hd, 0:256], AX.X, ALU.max)
                    ins = v.tensor_reduce(mx[:, hd, 1:2], sc[:, hd, 256:384], AX.X, ALU.max)
                step(ins)
                sink = sinkb[:].unsqueeze(2).to_broadcast([P, AH, 2])
                dve.wait_ge(consts_in.sem, 16 * N_CONSTS)
                step(v.tensor_tensor(mx[:], mx[:], sink, ALU.max))
                step(v.tensor_scalar(nmx[:], mx[:], -1.0, None, ALU.mult))
                v.tensor_tensor(esink[:], nmx[:], sink, ALU.add).then_inc(*att_d.inc("minus_max"))

                def place(n):
                    dve.wait_ge(*rec_p.at("scores", n))
                    b = 4 + n % 2 * 2
                    if n:
                        dve.wait_ge(*rec_d.at("placed", n - 1))
                    if n == len(LV):
                        v.tensor_copy(AT[:, 2], ps[:, b].rearrange("p (a b) -> p a b", a=RH)).then_inc(*rec_d.inc("placed", n))
                        return
                    if n == 0:
                        dve.wait_ge(*rec_g.at("zero"))
                    mask = masks[:, EYE if n == 0 else n - 1].unsqueeze(1).to_broadcast([P, RH, P])
                    for t in range(TT):
                        ins = v.copy_predicated(AT[:, t], mask, ps[:, b + t].rearrange("p (a b) -> p a b", a=RH))
                    ins.then_inc(*rec_d.inc("placed", n))

                for n, m in enumerate(LV):
                    dve.wait_ge(*rec_a.at("decay", n))
                    z, k, q = (t.rearrange("p a s -> p (a s)").rearrange("p (b m) -> p b m", m=2 * m) for t in (zT[:, n % 2], kT, rqT))
                    v.tensor_tensor(z[:, :, 0:m], z[:, :, 0:m], k[:, :, 0:m], ALU.mult)
                    v.tensor_tensor(z[:, :, m:2 * m], z[:, :, m:2 * m], q[:, :, m:2 * m], ALU.mult).then_inc(*rec_d.inc("decayed", n))
                    place(n)
                    if n == 3:
                        normalize_probs()
                place(len(LV))
                for t in range(TT):
                    dve.wait_ge(*rec_a.at("squares", t))
                    ins = v.tensor_reduce(ssq[:, 4 * t:4 * t + 4], osq[:, t].rearrange("p (a b) -> p a b", a=RH), AX.X, ALU.add)
                step(ins)
                v.tensor_scalar(msq[:, 0:8], ssq[:, 0:8], 1.0 / P, EPS, ALU.mult, ALU.add).then_inc(*mean_ready.inc("rec"))
                dve.wait_ge(*rstd_ready.at("rec"))
                for t in range(TT):
                    v.tensor_tensor(orec[:, t].rearrange("p (a b) -> p a b", a=RH), ps[:, 6 + t].rearrange("p (a b) -> p a b", a=RH),
                                    rstd[:, 4 * t:4 * t + 4].unsqueeze(2).to_broadcast([P, RH, P]), ALU.mult).then_inc(*rec_d.inc("normed", t))
                for j in range(4):
                    dve.wait_ge(*att_p.at("out", 2 * j + 1))
                    v.tensor_copy(attT[:, j], ps[:, j, 0:SEQ]).then_inc(*att_d.inc("outT", j))
                dve.wait_ge(*att_a.at("gate_r"))
                for n in range(2):
                    dve.wait_ge(*rec_p.at("turned", n))
                    v.scalar_tensor_tensor(recT[:, 2 * n:2 * n + 2], ps[:, 6 + n].rearrange("p (a b) -> p a b", a=2), col("rec_norm"),
                                           sgT[:, 2 * n:2 * n + 2], ALU.mult, ALU.mult).then_inc(*rec_d.inc("recT", n))
                dve.wait_ge(*att_a.at("gates"))
                for n in range(4):
                    dve.wait_ge(*(att_p.at("att_proj", n) if n < 3 else used_up_to(("att_proj", 1))))
                    ins = v.tensor_tensor(mT[:, 2 * n:2 * n + 2], ps[:, n].rearrange("p (a b) -> p a b", a=2), gT[:, 2 * n:2 * n + 2], ALU.mult)
                for n in range(4):
                    dve.wait_ge(*(att_p.at("rec_proj", n) if n < 3 else used_up_to(("rec_proj", 1))))
                    g = gT[:, 8 + 2 * n:10 + 2 * n]
                    step(v.tensor_tensor(g, ps[:, 4 + n].rearrange("p (a b) -> p a b", a=2), g, ALU.mult))
                    v.tensor_tensor(mT[:, 2 * n:2 * n + 2], mT[:, 2 * n:2 * n + 2], g, ALU.add).then_inc(*att_d.inc("merged", n))
                residual("mix1", 1.0, ("mix_out", 3))

            def normalize_probs():
                dve.wait_ge(*att_a.at("sink"))
                dve.wait_ge(*att_a.at("exp", AH - 1))
                step(v.tensor_tensor(den[:], den[:], esink[:], ALU.add))
                step(v.reciprocal(den[:], den[:]))
                for hd in range(AH):
                    for n, c in enumerate((slice(0, 256), slice(256, 384))):
                        ins = v.tensor_scalar(sc[:, hd, c], sc[:, hd, c], den[:, hd, n:n + 1], None, ALU.mult)
                    ins.then_inc(*att_d.inc("probs", hd))

            def ple(stage, gain, slot):
                norm(stage, gain)
                key = (f"{stage}_gate", 2)
                raw, hi, lo = ple_views(key)
                dve.wait_ge(*w_hi_ready.at(key))
                v.tensor_tensor(lo, raw, hi, ALU.subtract).then_inc(*w_lo_d.inc(key))
                if slot is None:
                    dve.wait_ge(*used_up_to((f"{stage}_proj", 0)))
                else:
                    dve.wait_ge(*ple_a.at(stage, "squares"))
                    v.tensor_scalar(msq[:, 2:4], ssq[:, 2:4], 1.0 / D, EPS, ALU.mult, ALU.add).then_inc(*mean_ready.inc(stage, "e"))
                    dve.wait_ge(*rstd_ready.at(stage, "e"))
                    dve.wait_ge(gains_in.sem, 48 if stage == "ple21" else 32)
                    for t in range(TT):
                        ins = v.scalar_tensor_tensor(pemb[:, t], ps[:, 2 * t:2 * t + 2].rearrange("p a b -> p (a b)"), rstd[:, 2 + t:3 + t],
                                                     row_gain[:, slot], ALU.mult, ALU.mult)
                    ins.then_inc(*ple_d.inc(stage, "e"))
                    dve.wait_ge(*ple_d.at(stage, "e"))
                for t in range(TT):
                    dve.wait_ge(*ple_a.at(stage, t))
                    e = ps[:, 2 * t:2 * t + 2].rearrange("p a b -> p (a b)") if slot is None else pemb[:, t]
                    step(v.tensor_tensor(pgate[:, t], pgate[:, t], e, ALU.mult))
                    v.tensor_tensor(h[:, t], h[:, t], pgate[:, t], ALU.add).then_inc(*h_ready.inc(key_after(stage), t))

            def final_norm(n, slot, gains):
                dve.wait_ge(*squared.at(n, 1))
                v.tensor_scalar(msq[:, 0:2], ssq[:, 0:2], 1.0 / D, EPS, ALU.mult, ALU.add).then_inc(*mean_ready.inc(n))
                dve.wait_ge(*rstd_ready.at(n))
                dve.wait_ge(gains_in.sem, gains)
                for t in range(TT):
                    v.scalar_tensor_tensor(h[:, t], h[:, t], rstd[:, t:t + 1], row_gain[:, slot], ALU.mult, ALU.mult).then_inc(*h_ready.inc(key_after(n), t))

            def hyb():
                norm("hyb", "attn_norm0")

                def mix(key, tile, tiles, rows):
                    dve.wait_ge(*mix_g.at(key))
                    for j in range(tile, tile + tiles):
                        mu = col("mu", j) if j < 14 else col("mu_tail")
                        ins = v.scalar_tensor_tensor(xm[0:rows, j], xm[0:rows, j], mu[0:rows], pfT[0:rows, j, 1:], ALU.mult, ALU.add)
                    ins.then_inc(*mix_d.inc(key))

                def flat(t):
                    return t.rearrange("p a s -> p (a s)")

                for m in MIXES[:2]:
                    mix(*m)
                dve.wait_ge(*mix_d.last())
                for j in range(RWT):
                    ins = v.tensor_scalar(kk[:, j], xm[:, 4 + j], col("k_k", j), None, ALU.mult)
                step(ins)
                v.tensor_tensor(dm0[:], kk[:], kk[:], ALU.mult).then_inc(*pre_d.inc("kk_squares"))
                for m in MIXES[2:]:
                    mix(*m)
                dve.wait_ge(*pre_a.at("decay"))
                for j in range(RWT):
                    for c in range(2):
                        s = slice(c * P, (c + 1) * P)
                        ins = v.tensor_tensor_scan(cc[:, j, s], ones[:, 0:P], lw[:, j, s], 0.0, ALU.mult, ALU.add)
                step(ins)
                c3, d3 = (t.rearrange("p a (c s) -> p (a c) s", c=2) for t in (cc, dm))
                step(v.tensor_tensor(d3, c3, c3[:, :, 63:64].to_broadcast([P, 8, P]), ALU.subtract))
                v.tensor_tensor(sfac[:], dm[:, :, P - 1:P].rearrange("p a b -> p (a b)"), cc[:, :, P + 63:P + 64].rearrange("p a b -> p (a b)"), ALU.add)
                dve.wait_ge(*pre_p.at("kk_sums"))
                v.tensor_scalar(ktmp[:], ps[:, 4:6].rearrange("p b (a s) -> p (b a) s", a=2), 1e-24, None, ALU.max).then_inc(*pre_d.inc("kk_sums"))
                v.tensor_tensor(dm0[:], dm[:], lw[:], ALU.subtract).then_inc(*pre_d.inc("dm"))
                dve.wait_ge(*pre_a.at("kk_norm"))
                step(v.reciprocal(ktmp[:], ktmp[:]))
                v.tensor_tensor(kk[:], kk[:], ktmp[:], ALU.mult).then_inc(*pre_d.inc("kk_norm"))
                dve.wait_ge(*pre_a.at("rate"))
                dve.wait_ge(*pre_d.at("kk_norm"))
                for j in range(RWT):
                    v.tensor_scalar(ktmp[:, j], aT[:, j], 1.0, col("k_a", j), ALU.subtract, ALU.mult)
                step(v.scalar_tensor_tensor(flat(Bk), flat(kk), -1.0, flat(aT), ALU.mult, ALU.mult))
                step(v.scalar_tensor_tensor(xm[:, 4:8], ktmp[:], 1.0, xm[:, 4:8], ALU.add, ALU.mult))
                dve.wait_ge(*pre_a.at("exps"))
                ar = AR.rearrange("p a c n s -> p (a c) n s")
                two = lambda t: t.rearrange("p a (c s) -> p (a c) s", c=2)
                v.tensor_tensor(ar[:, :, 0], two(kk), two(dm0), ALU.mult)
                step(v.tensor_tensor(ar[:, :, 1], two(xm[:, 0:4]), two(dm), ALU.mult))
                for j in range(RWT):
                    ins = v.scalar_tensor_tensor(xm[:, j], xm[:, j], col("r_k", j), xm[:, 4 + j], ALU.mult, ALU.mult)
                ins.then_inc(*pre_d.inc("bonus_terms"))
                v.tensor_tensor(Bk[:], Bk[:], cc[:], ALU.mult)
                v.tensor_tensor(Kk[:], xm[:, 4:8], cc[:], ALU.mult).then_inc(*pre_d.inc("bk"))
                dve.wait_ge(*pre_p.at("bonus"))
                dve.wait_ge(*pre_d.at("bk"))
                v.tensor_tensor(bonus[:], ps[:, 4:6].rearrange("p b (a s) -> p (b a) s", a=2), xm[:, 8:12], ALU.mult).then_inc(*pre_d.inc("bonus"))
                dve.wait_ge(*mix_g.at("G"))
                two_masks = masks[:, BEFORE:UPTO + 1].rearrange("p a b -> p (a b)").unsqueeze(1).to_broadcast([P, 2, 2 * P])
                for n in range(16):
                    dve.wait_ge(*inv_p.at("scores", n))
                    v.copy_predicated(G[:, n // 8, n % 8].rearrange("p (a b) c -> p a (b c)", a=2), two_masks,
                                      ps[:, n % 4].rearrange("p (a b) -> p a b", a=2)).then_inc(*inv_d.inc("scores", n))

                def stick_softplus(g):
                    dve.wait_ge(*stick_a.at("log", g))
                    s = lsp[:, g % 2]
                    v.scalar_tensor_tensor(s, ps[:, 4 + 2 * (g % 2):6 + 2 * (g % 2), 0:384], 0.0, s, ALU.max, ALU.add).then_inc(*stick_d.inc("softplus", g))

                def level(n):
                    mask = masks[:, n].unsqueeze(1).to_broadcast([P, 4, P])
                    if n == 0:
                        dve.wait_ge(*inv_d.at("scores", 15))
                        step(v.tensor_copy(Y[:].rearrange("p a b c -> p (a b) c"), ident.unsqueeze(1).to_broadcast([P, 16, P])))
                    for g in range(4):
                        if n == 0:
                            data = G[:, g // 2, g % 2 * 4:g % 2 * 4 + 4, 0]
                        else:
                            dve.wait_ge(*inv_p.at("Y", n, g))
                            data = ps[:, g].rearrange("p (a b) -> p a b", a=4)
                        v.copy_predicated(Y[:, g], mask, data).then_inc(*inv_d.inc("Y", n, g))
                    if n < LEVEL_N - 1:
                        for g in range(4):
                            dve.wait_ge(*inv_p.at("X", n, g))
                            v.tensor_copy(X[:, g], ps[:, g].rearrange("p (a b) -> p a b", a=4)).then_inc(*inv_d.inc("X", n, g))

                level(0)
                stick_softplus(0)
                level(1)
                stick_softplus(1)
                level(2)
                stick_softplus(2)
                level(3)
                stick_softplus(3)
                level(4)
                level(5)
                level(6)
                dve.wait_ge(*sol_p.at("state"))
                dve.wait_ge(*pre_a.at("exps"))
                v.tensor_tensor(s0[:], ps[:, 7, 0:256].rearrange("p (a b) -> p a b", a=4), sfac[:].unsqueeze(2).to_broadcast([P, 4, 64]),
                                ALU.mult).then_inc(*sol_d.inc("state"))
                y16, q16 = yv.rearrange("p c a b -> p (c a) b"), ysq.rearrange("p c a b -> p (c a) b")
                dve.wait_ge(*sol_a.at("y", 0))
                dve.wait_ge(*sol_a.at("y", 1))
                step(v.tensor_reduce(gmean[:], y16, AX.X, ALU.add))
                step(v.tensor_scalar(gmean[:], gmean[:], 1.0 / 64, None, ALU.mult))
                v.tensor_tensor(y16, y16, gmean[:].unsqueeze(2).to_broadcast([P, 16, 64]), ALU.subtract).then_inc(*sol_d.inc("centred"))
                dve.wait_ge(*sol_a.at("squares"))
                step(v.tensor_reduce(ssq[:], q16, AX.X, ALU.add))
                v.tensor_scalar(msq[:], ssq[:], 1.0 / 64, 64e-5, ALU.mult, ALU.add).then_inc(*mean_ready.inc("gn"))
                dve.wait_ge(*rstd_ready.at("gn"))
                v.tensor_tensor(y16, y16, rstd[:].unsqueeze(2).to_broadcast([P, 16, 64]), ALU.mult).then_inc(*sol_d.inc("normed"))
                dve.wait_ge(*sol_p.at("turned"))
                for j in range(RWT):
                    ins = v.tensor_scalar(obT[:, j], ps[:, 4 + j // 2, j % 2 * SEQ:(j % 2 + 1) * SEQ], col("ln_w", j), col("ln_b", j), ALU.mult, ALU.add)
                step(ins)
                step(v.tensor_tensor(obT[:], obT[:], bonus[:], ALU.add))
                dve.wait_ge(*used.at("g2"))
                v.tensor_tensor(obT[:], obT[:], ps[:, 6:8].rearrange("p b (a s) -> p (b a) s", a=2), ALU.mult).then_inc(*sol_d.inc("ob"))
                residual("hyb", 1.0, ("hyb_out", 3))

            def rotary_angles():
                two_pi = 2 * np.pi
                c1 = 6.28125
                c2 = float(np.float32(np.round((two_pi - c1) * 2.0 ** 20) / 2.0 ** 20))
                c3 = float(two_pi - c1 - c2)
                magic = 1.5 * 2.0 ** 23
                dve.wait_ge(rot_in.sem, 32)
                step(v.tensor_copy(posf[:], posi[:]))
                for t in range(TT):
                    ins = v.tensor_scalar(ang[:, t], freq[:], posf[:, t:t + 1], None, ALU.mult)
                step(ins)
                step(v.tensor_scalar(turns[:], ang[:], float(1 / two_pi), magic, ALU.mult, ALU.add))
                step(v.tensor_scalar(turns[:], turns[:], magic, None, ALU.subtract))
                for c in (c1, c2, c3):
                    step(v.scalar_tensor_tensor(ang[:], turns[:], -c, ang[:], ALU.mult, ALU.add))
                step(v.tensor_scalar(sinv[:], ang[:], 3.1415925, -3.1415925, ALU.min, ALU.max))
                step(v.tensor_scalar(turns[:], sinv[:], -1.0, None, ALU.mult))
                step(v.tensor_tensor(turns[:], turns[:], sinv[:], ALU.max))
                v.tensor_scalar(cosv[:], turns[:], -1.0, float(np.pi / 2), ALU.mult, ALU.add).then_inc(*rot_d.inc("angles"))

            def rotate(x, shape, c, s):
                n = int(np.prod(shape[1:]))
                view = lambda k: (rt[:, k, 0:n].rearrange("p (a b c) -> p a b c", a=shape[1], b=shape[2]) if len(shape) == 4
                                  else rt[:, k, 0:n].rearrange("p (a b) -> p a b", a=shape[1]))
                x1, x2 = x[..., 0:16], x[..., 16:32]
                v.tensor_tensor(view(0), x1, c, ALU.mult)
                v.tensor_tensor(view(1), x2, s, ALU.mult)
                v.tensor_tensor(view(2), x1, s, ALU.mult)
                step(v.tensor_tensor(view(3), x2, c, ALU.mult))
                v.tensor_tensor(x1, view(0), view(1), ALU.subtract)
                return v.tensor_tensor(x2, view(2), view(3), ALU.add)

            def mla():
                norm("mla", "attn_norm1")
                dve.wait_ge(*lat_a.at("squares"))
                v.tensor_scalar(msq[:, 0:2], ssq[:, 0:2], 1.0 / 384, EPS, ALU.mult, ALU.add)
                v.tensor_scalar(msq[:, 2:4], ssq[:, 2:4], 1.0 / 256, EPS, ALU.mult, ALU.add).then_inc(*mean_ready.inc("latent"))
                dve.wait_ge(*rstd_ready.at("latent"))
                for t in range(TT):
                    v.tensor_scalar(ctok[:, t, 0:384], ctok[:, t, 0:384], rstd[:, t:t + 1], None, ALU.mult)
                    ins = v.tensor_scalar(ctok[:, t, 384:640], ctok[:, t, 384:640], rstd[:, 2 + t:3 + t], None, ALU.mult)
                ins.then_inc(*lat_d.inc("scaled"))
                dve.wait_ge(*rot_a.at("rot"))
                step(rotate(ctok[:, :, 640:672], [P, TT, 16], cosv[:], sinv[:]))
                v.tensor_copy(ktok2[:, :, :, 64:96], ctok[:, :, 640:672].unsqueeze(2).to_broadcast([P, TT, MH, 32])).then_inc(*lat_d.inc("rotary_key"))
                dve.wait_ge(*lat_p.at("turned"))
                for j in range(4):
                    gain = col("q_norm", j) if j < 3 else col("kv_norm", 0)
                    ins = v.tensor_scalar(clT[:, j], ps[:, 4 + j // 2, j % 2 * SEQ:(j % 2 + 1) * SEQ], gain, None, ALU.mult)
                ins.then_inc(*lat_d.inc("q"))
                keep_up(dve, 1)
                dve.wait_ge(*up_a.at("q", 2, 0))
                dve.wait_ge(*up_d.at("q", 2, 1))
                cs, sn = (t.unsqueeze(2).to_broadcast([P, TT, MH, 16]) for t in (cosv[:], sinv[:]))
                rotate(qtok[:, :, :, 64:96], [P, TT, MH, 16], cs, sn).then_inc(*mla_d.inc("rotated"))
                mask = mats[:, 2].unsqueeze(1).to_broadcast([P, 2, P])
                for i in range(MH + 2):
                    if i < MH and i % 2:
                        dve.wait_ge(*mla_p.at("turned", i))
                        if i >= 3:
                            dve.wait_ge(*mla_p.at("scores", i - 3))
                        v.tensor_copy(qkT[0:QH, i % 3].rearrange("p a b -> p (a b)"), ps[0:QH, 4 + i % 2]).then_inc(*mla_d.inc("turned", i))
                    hd = i - LAG_S
                    if 0 <= hd < MH:
                        s, b = msc[:, hd % 6], 6 + hd % 2
                        dve.wait_ge(*mla_p.at("scores", hd))
                        if hd >= 6:
                            dve.wait_ge(*mla_p.at("probs", hd - 6))
                        v.tensor_copy(s[:, 0:P], ps[:, b, 0:P])
                        v.tensor_tensor(s[:, P:3 * P].rearrange("p (a b) -> p a b", a=2), ps[:, b, P:3 * P].rearrange("p (a b) -> p a b", a=2), mask,
                                        ALU.add).then_inc(*mla_d.inc("masked", hd))
                        dve.wait_ge(*mla_d.at("masked", hd))
                        v.tensor_reduce(mmax[:, hd % 6, 0:1], s[:, 0:256], AX.X, ALU.max)
                        step(v.tensor_reduce(mmax[:, hd % 6, 1:2], s[:, 256:384], AX.X, ALU.max))
                        v.tensor_scalar(mmax[:, hd % 6], mmax[:, hd % 6], -MSCALE, None, ALU.mult).then_inc(*mla_d.inc("minus_max", hd))
                    hd = i - 2
                    if 0 <= hd < MH:
                        dve.wait_ge(*mla_a.at("exp", hd))
                        v.reciprocal(mden[:, hd % 6], mden[:, hd % 6]).then_inc(*mla_d.inc("inverse_sum", hd))
                residual("mla", 1.0, ("mla_o", 3))

            norm("ffn1", "norm_ffn1")
            ffn("ffn1", False)
            norm("mix1", "norm_mix")
            v.tensor_tensor(lbd[:], cols[:, column["lb0"]:column["lb0"] + RH], cols[:, column["lb1"]:column["lb1"] + RH],
                            ALU.subtract).then_inc(*lb_d.inc("logit"))
            dve.wait_ge(*bias_p.at("t"))
            v.tensor_copy(tabd[:], ps[0:AH, 3, 0:384]).then_inc(*bias_d.inc("t"))
            dve.wait_ge(*lb_a.at("lb"))
            v.tensor_scalar(omlb[:], lbc[:], -1.0, 1.0, ALU.mult, ALU.add).then_inc(*lb_d.inc("one_minus"))
            mix1()
            norm("ffn2", "norm_ffn2")
            ffn("ffn2", False, between=rotary_angles)
            ple("ple1", "norm_ple", None)
            final_norm("block1", 0, 32)
            hyb()
            norm("conv0", "conv_norm0")
            ffn("conv0", True)
            ple("ple20", "ple_gate_norm0", 1)
            mla()
            norm("conv1", "conv_norm1")
            ffn("conv1", True)
            ple("ple21", "ple_gate_norm1", 0)
            final_norm("all", 1, 64)

    return new


def key_after(key):
    return "out" if key == "all" else STAGES[STAGES.index(key) + 1]


def kernel(**inputs):
    import concourse.bacc as bacc
    from concourse.bass_utils import run_bass_kernel_spmd

    arrays = {name: np.ascontiguousarray(a) for name, a in inputs.items()}
    arrays.update(host_constants())

    def program(book):
        nc = bacc.Bacc("TRN2", target_bir_lowering=False, num_devices=1)
        aps = {name: nc.dram_tensor(f"in_{name}", a.shape, mybir.dt.from_np(a.dtype), kind="ExternalInput").ap()
               for name, a in arrays.items()}
        scratch = nc.dram_tensor("bias_by_distance", (8, P, 384), F32, kind="Internal").ap()
        out = nc.dram_tensor("out", (1, SEQ, D), F32, kind="ExternalOutput").ap()
        return nc, build(nc, aps, scratch, out, book)

    _, book = program({})
    nc, _ = program(book)
    r = run_bass_kernel_spmd(nc, [{f"in_{n}": a for n, a in arrays.items()}], core_ids=[0])
    return r.results[0]["out"]
```
